# Optimizing a Trainium2 kernel written in Bass

```python
import math
import jax
import jax.numpy as jnp
from jax import lax
import numpy as np
import jax, jax.numpy as jnp

D_MODEL = 1024
BATCH = 1
SEQ = 256
DEPTH = 1

D_MIX = D_MODEL
D_CONV = D_MIX // 2
CONV_GROUPS = 8
D_GLA = D_MIX - D_CONV
GLA_HEADS = 4
HEAD_V = D_GLA // GLA_HEADS
HEAD_K = HEAD_V // 2
D_GLA_K = GLA_HEADS * HEAD_K
GATE_RANK = 16
GATE_NORMALIZER = 16.0
CHUNK = 64
D_FF = 2816
CONV_WIDTH = 3
EPS = 1e-6
SPLIT_SIZES = (D_CONV, D_CONV, D_CONV,
               D_GLA_K, D_GLA_K, D_GLA, D_GLA,
               GATE_RANK, GATE_RANK)
D_IN = sum(SPLIT_SIZES)


def rmsnorm(x, g):
    xf = x.astype(jnp.float32)
    y = xf * lax.rsqrt(jnp.mean(xf * xf, axis=-1, keepdims=True) + EPS)
    return (y * g.astype(jnp.float32)).astype(x.dtype)

def dwconv3(x, w):
    xp = jnp.pad(x, ((0, 0), (1, 1), (0, 0)))
    return w[0] * xp[:, :-2] + w[1] * xp[:, 1:-1] + w[2] * xp[:, 2:]

def split_cols(p):
    idx, acc = [], 0
    for s in SPLIT_SIZES[:-1]:
        acc += s
        idx.append(acc)
    return jnp.split(p, idx, axis=-1)

def gla_chunked(q, k, v, log_a):
    b_, h_, L, dk = q.shape
    dv = v.shape[-1]
    n = L // CHUNK
    q = q.reshape(b_, h_, n, CHUNK, dk)
    k = k.reshape(b_, h_, n, CHUNK, dk)
    v = v.reshape(b_, h_, n, CHUNK, dv)
    cum = jnp.cumsum(log_a.reshape(b_, h_, n, CHUNK, dk), axis=3)
    cum_last = cum[:, :, :, -1:, :]
    q_in = q * jnp.exp(cum)
    k_in = k * jnp.exp(-cum)
    k_out = k * jnp.exp(cum_last - cum)
    mask = jnp.tril(jnp.ones((CHUNK, CHUNK), dtype=bool))
    scores = jnp.einsum('bhnid,bhnjd->bhnij', q_in, k_in)
    scores = jnp.where(mask, scores, 0.0)
    o_intra = jnp.einsum('bhnij,bhnje->bhnie', scores, v)
    kv = jnp.einsum('bhnjd,bhnje->bhnde', k_out, v)
    decay = jnp.exp(cum_last[:, :, :, 0, :])

    def step(state, inp):
        d_n, kv_n = inp
        return d_n[..., None] * state + kv_n, state

    _, s_prev = lax.scan(step, jnp.zeros((b_, h_, dk, dv), jnp.float32),
                         (jnp.moveaxis(decay, 2, 0), jnp.moveaxis(kv, 2, 0)))
    s_prev = jnp.moveaxis(s_prev, 0, 2)
    o_inter = jnp.einsum('bhnid,bhnde->bhnie', q_in, s_prev)
    return (o_intra + o_inter).reshape(b_, h_, L, dv)

def to_heads(t, d_head):
    b_, L, _ = t.shape
    return t.reshape(b_, L, -1, d_head).transpose(0, 2, 1, 3)

def gate_log_decay(lr, w_up, bias):
    pre = (lr @ w_up + bias).astype(jnp.float32)
    return jax.nn.log_sigmoid(pre) / GATE_NORMALIZER

def mixer(h, w_in, conv_a, gate_up_fwd, gate_bias_fwd, gate_up_bwd, gate_bias_bwd,
          gla_head_norm, w_out):
    p = h @ w_in
    gb, gc, gv, q, k, v, go, lr_f, lr_b = split_cols(p)
    y_a = gb * dwconv3(gc * gv, conv_a)
    la_f = gate_log_decay(lr_f, gate_up_fwd, gate_bias_fwd)
    la_b = gate_log_decay(lr_b, gate_up_bwd, gate_bias_bwd)
    qh = to_heads(q, HEAD_K).astype(jnp.float32) * (HEAD_K ** -0.5)
    kh = to_heads(k, HEAD_K).astype(jnp.float32)
    vh = to_heads(v, HEAD_V).astype(jnp.float32)
    af = to_heads(la_f, HEAD_K)
    ab = to_heads(la_b, HEAD_K)
    flip = lambda t: jnp.flip(t, axis=2)
    o_f = gla_chunked(qh, kh, vh, af)
    o_b = flip(gla_chunked(flip(qh), flip(kh), flip(vh), flip(ab)))
    o = o_f + o_b
    o = o * lax.rsqrt(jnp.mean(o * o, axis=-1, keepdims=True) + EPS) * gla_head_norm.astype(jnp.float32)
    b_, _, L, _ = o.shape
    o = o.transpose(0, 2, 1, 3).reshape(b_, L, D_GLA).astype(h.dtype)
    y_b = jax.nn.silu(go) * o
    y = jnp.concatenate([y_a, y_b], axis=-1)
    return y @ w_out

def conv_mlp(h, w_up, conv_w, w_down):
    u = dwconv3(h @ w_up, conv_w)
    gate, val = jnp.split(u, 2, axis=-1)
    return (jax.nn.silu(gate) * val) @ w_down

def first_inputs(seed: int = 0) -> dict:
    key = jax.random.key(seed)
    ks = jax.random.split(key, 20)
    f32 = jnp.float32
    nrm = lambda k, shape, scale: jax.random.normal(k, shape, f32) * scale
    gain = lambda k, shape: 1.0 + 0.05 * jax.random.normal(k, shape, f32)
    return {
        "x": jax.random.normal(ks[0], (BATCH, SEQ, D_MODEL), f32),
        "norm_mix_pre": gain(ks[1], (DEPTH, D_MODEL)),
        "norm_mix_post": gain(ks[2], (DEPTH, D_MODEL)),
        "norm_ffn_pre": gain(ks[3], (DEPTH, D_MODEL)),
        "norm_ffn_post": gain(ks[4], (DEPTH, D_MODEL)),
        "w_in": nrm(ks[5], (DEPTH, D_MODEL, D_IN), D_MODEL ** -0.5),
        "conv_a": nrm(ks[6], (DEPTH, CONV_WIDTH, D_CONV), CONV_WIDTH ** -0.5),
        "gate_up_fwd": nrm(ks[7], (DEPTH, GATE_RANK, D_GLA_K), GATE_RANK ** -0.5),
        "gate_bias_fwd": nrm(ks[8], (DEPTH, D_GLA_K), 0.1),
        "gate_up_bwd": nrm(ks[9], (DEPTH, GATE_RANK, D_GLA_K), GATE_RANK ** -0.5),
        "gate_bias_bwd": nrm(ks[10], (DEPTH, D_GLA_K), 0.1),
        "gla_head_norm": gain(ks[11], (DEPTH, HEAD_V)),
        "w_out": nrm(ks[12], (DEPTH, D_MIX, D_MODEL), D_MIX ** -0.5),
        "w_up": nrm(ks[13], (DEPTH, D_MODEL, 2 * D_FF), D_MODEL ** -0.5),
        "conv_ffn": nrm(ks[14], (DEPTH, CONV_WIDTH, 2 * D_FF), CONV_WIDTH ** -0.5),
        "w_down": nrm(ks[15], (DEPTH, D_FF, D_MODEL), D_FF ** -0.5),
    }

def first_block(x, norm_mix_pre, norm_mix_post, norm_ffn_pre, norm_ffn_post, w_in, conv_a,
              gate_up_fwd, gate_bias_fwd, gate_up_bwd, gate_bias_bwd, gla_head_norm,
              w_out, w_up, conv_ffn, w_down):
    for l in range(DEPTH):
        h = rmsnorm(x, norm_mix_pre[l])
        y = mixer(h, w_in[l], conv_a[l], gate_up_fwd[l], gate_bias_fwd[l], gate_up_bwd[l],
                  gate_bias_bwd[l], gla_head_norm[l], w_out[l])
        x = x + rmsnorm(y, norm_mix_post[l])
        h = rmsnorm(x, norm_ffn_pre[l])
        y = conv_mlp(h, w_up[l], conv_ffn[l], w_down[l])
        x = x + rmsnorm(y, norm_ffn_post[l])
    return x


DEPTH_2 = 2

HEAD_DIM = 64
N_HEADS_TOTAL = D_MODEL // HEAD_DIM
N_HEADS_FOX = N_HEADS_TOTAL // 2
N_HEADS_SB = N_HEADS_TOTAL - N_HEADS_FOX
N_HEADS_SWA = N_HEADS_TOTAL
N_KV_SWA = max(1, N_HEADS_SWA // 8)
WINDOW = 128
Q_BLOCK = 128
ROPE_THETA = 500000.0
ROPE_DIM = HEAD_DIM // 4
D_FF_2 = ((8 * D_MODEL // 3 + 127) // 128) * 128
N_EXPERTS = 8
TOP_K = 2
D_FF_EXPERT = 7 * D_MODEL // 2
D_PLE = 256
LN_EPS = 1e-5
N_EVEN = (DEPTH_2 + 1) // 2
N_ODD = DEPTH_2 // 2
DEEPNORM_ALPHA = (2.0 * DEPTH_2) ** 0.25
DEEPNORM_BETA = (8.0 * DEPTH_2) ** -0.25
FOX_W = N_HEADS_FOX * HEAD_DIM
SB_W = N_HEADS_SB * HEAD_DIM
AB_IN = 3 * FOX_W + N_HEADS_FOX + 3 * SB_W
AB_SPLITS = [FOX_W, 2 * FOX_W, 3 * FOX_W, 3 * FOX_W + N_HEADS_FOX,
             3 * FOX_W + N_HEADS_FOX + SB_W, 3 * FOX_W + N_HEADS_FOX + 2 * SB_W]
SWA_IN = (N_HEADS_SWA + 2 * N_KV_SWA) * HEAD_DIM
SWA_SPLITS = [N_HEADS_SWA * HEAD_DIM, (N_HEADS_SWA + N_KV_SWA) * HEAD_DIM]


F32 = jnp.float32

def layer_norm(x, g, b):
    xf = x.astype(F32)
    mu = jnp.mean(xf, axis=-1, keepdims=True)
    xc = xf - mu
    var = jnp.mean(xc * xc, axis=-1, keepdims=True)
    return (xc * lax.rsqrt(var + LN_EPS) * g.astype(F32) + b.astype(F32)).astype(x.dtype)

def swiglu(x, w_gate_up, w_down):
    g, u = jnp.split(x @ w_gate_up, 2, axis=-1)
    return (jax.nn.silu(g) * u) @ w_down

def partial_rope(x, pos):
    half = ROPE_DIM // 2
    inv = ROPE_THETA ** (-jnp.arange(half, dtype=F32) * 2.0 / ROPE_DIM)
    ang = pos.astype(F32)[:, None] * inv[None, :]
    cos = jnp.cos(ang)[None, :, None, :]
    sin = jnp.sin(ang)[None, :, None, :]
    xr = x[..., :ROPE_DIM].astype(F32)
    x1, x2 = xr[..., :half], xr[..., half:]
    rot = jnp.concatenate([x1 * cos - x2 * sin, x2 * cos + x1 * sin], axis=-1).astype(x.dtype)
    return jnp.concatenate([rot, x[..., ROPE_DIM:]], axis=-1)

def fox_attention(q, k, v, log_f):
    B, S, H, dh = q.shape
    scale = dh ** -0.5
    c = jnp.cumsum(log_f, axis=1).transpose(0, 2, 1)
    k_pos = jnp.arange(S)

    def block(i):
        start = i * Q_BLOCK
        qb = lax.dynamic_slice_in_dim(q, start, Q_BLOCK, axis=1)
        cb = lax.dynamic_slice_in_dim(c, start, Q_BLOCK, axis=2)
        s = jnp.einsum('bqhd,bkhd->bhqk', qb, k, preferred_element_type=F32) * scale
        s = s + cb[..., :, None] - c[..., None, :]
        q_pos = start + jnp.arange(Q_BLOCK)
        mask = k_pos[None, :] <= q_pos[:, None]
        w = jax.nn.softmax(jnp.where(mask, s, -jnp.inf), axis=-1)
        return jnp.einsum('bhqk,bkhd->bqhd', w.astype(v.dtype), v)

    out = lax.map(block, jnp.arange(S // Q_BLOCK))
    return out.transpose(1, 0, 2, 3, 4).reshape(B, S, H, dh)

def stick_breaking_attention(q, k, v):
    B, S, H, dh = q.shape
    scale = dh ** -0.5
    k_pos = jnp.arange(S)

    def block(i):
        start = i * Q_BLOCK
        qb = lax.dynamic_slice_in_dim(q, start, Q_BLOCK, axis=1)
        z = jnp.einsum('bqhd,bkhd->bhqk', qb, k, preferred_element_type=F32) * scale
        q_pos = start + jnp.arange(Q_BLOCK)
        mask = k_pos[None, :] < q_pos[:, None]
        log_1mb = jnp.where(mask, jax.nn.log_sigmoid(-z), 0.0)
        later = lax.cumsum(log_1mb, axis=3, reverse=True) - log_1mb
        a = jnp.where(mask, jnp.exp(jax.nn.log_sigmoid(z) + later), 0.0)
        return jnp.einsum('bhqk,bkhd->bqhd', a.astype(v.dtype), v)

    out = lax.map(block, jnp.arange(S // Q_BLOCK))
    return out.transpose(1, 0, 2, 3, 4).reshape(B, S, H, dh)

def sliding_window_gqa_sinks(q, k, v, sinks):
    B, S, HQ, dh = q.shape
    HKV = k.shape[2]
    G = HQ // HKV
    W = WINDOW
    n = S // W
    scale = dh ** -0.5
    qb = q.reshape(B, n, W, HKV, G, dh)

    def with_prev(t):
        t = t.reshape(B, n, W, HKV, dh)
        prev = jnp.concatenate([jnp.zeros_like(t[:, :1]), t[:, :-1]], axis=1)
        return jnp.concatenate([prev, t], axis=2)

    kk, vv = with_prev(k), with_prev(v)
    s = jnp.einsum('bnqhgd,bnkhd->bnhgqk', qb, kk, preferred_element_type=F32) * scale
    diff = jnp.arange(W)[:, None] + W - jnp.arange(2 * W)[None, :]
    band = (diff >= 0) & (diff < W)
    key_abs = jnp.arange(n)[:, None] * W + jnp.arange(2 * W)[None, :] - W
    mask = band[None] & (key_abs >= 0)[:, None, :]
    s = jnp.where(mask[None, :, None, None], s, -jnp.inf)
    sink = sinks.astype(F32).reshape(HKV, G)[None, None, :, :, None]
    mx = jnp.maximum(jnp.max(s, axis=-1), sink)
    e = jnp.exp(s - mx[..., None])
    w = e / (jnp.sum(e, axis=-1) + jnp.exp(sink - mx))[..., None]
    out = jnp.einsum('bnhgqk,bnkhd->bnqhgd', w.astype(v.dtype), vv)
    return out.reshape(B, S, HQ, dh)

def fox_sb_mixer(x, w_in, b_f, w_out):
    B, S, _ = x.shape
    h = x @ w_in
    qa, ka, va, fa, qs, ks, vs = jnp.split(h, AB_SPLITS, axis=-1)
    hd = lambda t, H: t.reshape(B, S, H, HEAD_DIM)
    log_f = jax.nn.log_sigmoid((fa + b_f).astype(F32))
    oa = fox_attention(hd(qa, N_HEADS_FOX), hd(ka, N_HEADS_FOX), hd(va, N_HEADS_FOX), log_f)
    ob = stick_breaking_attention(hd(qs, N_HEADS_SB), hd(ks, N_HEADS_SB), hd(vs, N_HEADS_SB))
    o = jnp.concatenate([oa.reshape(B, S, FOX_W), ob.reshape(B, S, SB_W)], axis=-1)
    return o @ w_out

def swa_mixer(x, w_qkv, sinks, w_out, pos):
    B, S, _ = x.shape
    q, k, v = jnp.split(x @ w_qkv, SWA_SPLITS, axis=-1)
    q = partial_rope(q.reshape(B, S, N_HEADS_SWA, HEAD_DIM), pos)
    k = partial_rope(k.reshape(B, S, N_KV_SWA, HEAD_DIM), pos)
    v = v.reshape(B, S, N_KV_SWA, HEAD_DIM)
    o = sliding_window_gqa_sinks(q, k, v, sinks)
    return o.reshape(B, S, N_HEADS_SWA * HEAD_DIM) @ w_out

def moe_swiglu(x, router_w, router_b, w_gate_up, w_down):
    B, S, D = x.shape
    xf = x.reshape(-1, D)
    logits = jnp.einsum('td,de->te', xf, router_w, preferred_element_type=F32) + router_b.astype(F32)
    top_v, top_i = lax.top_k(logits, TOP_K)
    gates = jax.nn.softmax(top_v, axis=-1)
    combine = jnp.sum(gates[..., None] * jax.nn.one_hot(top_i, N_EXPERTS, dtype=F32), axis=1)
    y = jnp.zeros(xf.shape, F32)
    for e in range(N_EXPERTS):
        y = y + combine[:, e:e + 1] * swiglu(xf, w_gate_up[e], w_down[e]).astype(F32)
    return y.astype(x.dtype).reshape(B, S, D)

def second_inputs(seed: int = 0) -> dict:
    key = jax.random.key(seed)
    ks = jax.random.split(key, 20)
    nrm = lambda k, shape, s: jax.random.normal(k, shape, F32) * s
    return {
        'x': nrm(ks[0], (BATCH, SEQ, D_MODEL), 1.0),
        'p': nrm(ks[1], (DEPTH_2, BATCH, SEQ, D_PLE), 1.0),
        'ln_mix_g': 1.0 + nrm(ks[2], (DEPTH_2, D_MODEL), 0.02),
        'ln_mix_b': nrm(ks[3], (DEPTH_2, D_MODEL), 0.02),
        'ln_ffn_g': 1.0 + nrm(ks[4], (DEPTH_2, D_MODEL), 0.02),
        'ln_ffn_b': nrm(ks[5], (DEPTH_2, D_MODEL), 0.02),
        'ab_w_in': nrm(ks[6], (N_EVEN, D_MODEL, AB_IN), D_MODEL ** -0.5),
        'ab_b_f': jax.random.uniform(ks[7], (N_EVEN, N_HEADS_FOX), F32, 1.0, 5.0),
        'ab_w_out': nrm(ks[8], (N_EVEN, FOX_W + SB_W, D_MODEL), (FOX_W + SB_W) ** -0.5 * DEEPNORM_BETA),
        'c_w_qkv': nrm(ks[9], (N_ODD, D_MODEL, SWA_IN), D_MODEL ** -0.5),
        'c_sinks': nrm(ks[10], (N_ODD, N_HEADS_SWA), 1.0),
        'c_w_out': nrm(ks[11], (N_ODD, N_HEADS_SWA * HEAD_DIM, D_MODEL), (N_HEADS_SWA * HEAD_DIM) ** -0.5 * DEEPNORM_BETA),
        'ffn_w_gate_up': nrm(ks[12], (N_EVEN, D_MODEL, 2 * D_FF_2), D_MODEL ** -0.5),
        'ffn_w_down': nrm(ks[13], (N_EVEN, D_FF_2, D_MODEL), D_FF_2 ** -0.5 * DEEPNORM_BETA),
        'router_w': nrm(ks[14], (N_ODD, D_MODEL, N_EXPERTS), D_MODEL ** -0.5),
        'router_b': nrm(ks[15], (N_ODD, N_EXPERTS), 0.01),
        'moe_w_gate_up': nrm(ks[16], (N_ODD, N_EXPERTS, D_MODEL, 2 * D_FF_EXPERT), D_MODEL ** -0.5),
        'moe_w_down': nrm(ks[17], (N_ODD, N_EXPERTS, D_FF_EXPERT, D_MODEL), D_FF_EXPERT ** -0.5 * DEEPNORM_BETA),
        'ple_w_gate': nrm(ks[18], (DEPTH_2, D_MODEL, D_MODEL), D_MODEL ** -0.5),
        'ple_w_proj': nrm(ks[19], (DEPTH_2, D_PLE, D_MODEL), D_PLE ** -0.5 * 0.5),
    }

def second_block(x, p, ln_mix_g, ln_mix_b, ln_ffn_g, ln_ffn_b, ab_w_in, ab_b_f, ab_w_out,
              c_w_qkv, c_sinks, c_w_out, ffn_w_gate_up, ffn_w_down, router_w, router_b,
              moe_w_gate_up, moe_w_down, ple_w_gate, ple_w_proj):
    pos = jnp.arange(x.shape[1])
    for i in range(DEPTH_2):
        j = i // 2
        if i % 2 == 0:
            h = fox_sb_mixer(x, ab_w_in[j], ab_b_f[j], ab_w_out[j])
        else:
            h = swa_mixer(x, c_w_qkv[j], c_sinks[j], c_w_out[j], pos)
        x = layer_norm(DEEPNORM_ALPHA * x + h, ln_mix_g[i], ln_mix_b[i])
        if i % 2 == 0:
            h = swiglu(x, ffn_w_gate_up[j], ffn_w_down[j])
        else:
            h = moe_swiglu(x, router_w[j], router_b[j], moe_w_gate_up[j], moe_w_down[j])
        x = layer_norm(DEEPNORM_ALPHA * x + h, ln_ffn_g[i], ln_ffn_b[i])
        x = x + jax.nn.sigmoid(x @ ple_w_gate[i]) * (p[i] @ ple_w_proj[i])
    return x


def setup_inputs(seed=0):
    out = dict(first_inputs(seed))
    for name, value in second_inputs(seed + 1).items():
        if name != "x":
            out[name + "_2"] = value
    return out


def reference(
    x, norm_mix_pre, norm_mix_post, norm_ffn_pre, norm_ffn_post, w_in, conv_a, gate_up_fwd,
    gate_bias_fwd, gate_up_bwd, gate_bias_bwd, gla_head_norm, w_out, w_up, conv_ffn, w_down,
    p_2, ln_mix_g_2, ln_mix_b_2, ln_ffn_g_2, ln_ffn_b_2, ab_w_in_2, ab_b_f_2, ab_w_out_2,
    c_w_qkv_2, c_sinks_2, c_w_out_2, ffn_w_gate_up_2, ffn_w_down_2, router_w_2, router_b_2,
    moe_w_gate_up_2, moe_w_down_2, ple_w_gate_2, ple_w_proj_2,
):
    x = first_block(
        x, norm_mix_pre, norm_mix_post, norm_ffn_pre, norm_ffn_post, w_in, conv_a, gate_up_fwd,
        gate_bias_fwd, gate_up_bwd, gate_bias_bwd, gla_head_norm, w_out, w_up, conv_ffn, w_down,
    )
    return second_block(
        x, p_2, ln_mix_g_2, ln_mix_b_2, ln_ffn_g_2, ln_ffn_b_2, ab_w_in_2, ab_b_f_2, ab_w_out_2,
        c_w_qkv_2, c_sinks_2, c_w_out_2, ffn_w_gate_up_2, ffn_w_down_2, router_w_2, router_b_2,
        moe_w_gate_up_2, moe_w_down_2, ple_w_gate_2, ple_w_proj_2,
    )


_drawn_inputs = setup_inputs


def setup_inputs(seed=0):
    import zlib

    import numpy as np

    out = dict(_drawn_inputs(seed))
    spreads = {}
    factors = {'gate_bias_fwd': 3.655, 'gate_bias_bwd': 3.135, 'c_sinks_2': 7.821, 'router_b_2': 6.476}
    for name, (base, spread) in spreads.items():
        noise = np.random.default_rng([zlib.crc32(name.encode()), seed]).standard_normal(out[name].shape)
        drawn = base * np.exp(spread * noise) if base else spread * noise
        out[name] = jnp.asarray(drawn.astype(out[name].dtype))
    for name, factor in factors.items():
        out[name] = (out[name] * factor).astype(out[name].dtype)
    return out
```

```python
from contextlib import ExitStack

import concourse.bass as bass
from concourse import mybir

ALU = mybir.AluOpType
ACT = mybir.ActivationFunctionType
F32 = mybir.dt.float32
F32R = mybir.dt.float32r
I32 = mybir.dt.int32
U32 = mybir.dt.uint32
AX_X = mybir.AxisListType.X

P = 128
SEQ, D = 256, 1024
NT = SEQ // P
KD = D // P
NB = 512
RING = 4
CHUNK = 2048

D_HALF = 512
GLA_HEADS, HEAD_K, HEAD_V, GLA_CHUNK, RANK = 4, 64, 128, 64, 16
N_GK = GLA_HEADS * HEAD_K
C_GB, C_GC, C_GV, C_Q, C_K, C_V, C_GO, C_LR = 0, 512, 1024, 1536, 1792, 2048, 2560, 3072
D_IN = 3104
D_FF = 2816
KF = D_FF // P
RMS_EPS, LN_EPS = 1e-6, 1e-5
DH = 64
N_AB = 8
FOX_W = N_AB * DH
AB_IN = 6 * FOX_W + N_AB
AB_QA, AB_KA, AB_VA, AB_FA = 0, FOX_W, 2 * FOX_W, 3 * FOX_W
AB_QS, AB_KS, AB_VS = 3 * FOX_W + N_AB, 4 * FOX_W + N_AB, 5 * FOX_W + N_AB
N_SWA, N_KV = 16, 2
SWA_IN = (N_SWA + 2 * N_KV) * DH
SWA_K, SWA_V = N_SWA * DH, (N_SWA + N_KV) * DH
ROPE_HALF = 8
N_EXP, D_EXP, D_PLE = 8, 3584, 256
KE = D_EXP // P
ITEMS = N_EXP + 3
ALPHA = 4.0 ** 0.25
SCW = 3 * P
NEG = -1.0e30
DECAY = 1.0 / 16.0


N_STREAM = ["w_in", "w_out", "w_up", "w_down", "ab_in", "ab_out", "ffn_up", "ffn_down", "ple0", "qkv", "c_out",
            "moe", "ple1"]


def weight_plan(w):

    def wide(m, k, n0, n):
        step = min(k, CHUNK // n) if n < NB else CHUNK // NB
        return (n0, n, [(k0, min(step, k - k0), m) for k0 in range(0, k, step)])

    def project(m, k, n):
        return [wide(m, k, n0, min(NB, n - n0)) for n0 in range(0, n, NB)]

    def gated(m):
        out = []
        for n0 in range(0, D_FF, NB):
            n = min(NB, D_FF - n0)
            out += [wide(m, KD, n0, n), wide(m, KD, D_FF + n0, n)]
        return out

    def ple(i):
        out = []
        for n0 in range(0, D, NB):
            out += [wide(w["ple_gate"][i], KD, n0, NB), wide(w["ple_proj"][i], D_PLE // P, n0, NB)]
        return out

    return [
        ("w_in", project(w["w_in"], KD, D_IN)), ("w_out", project(w["w_out"], KD, D)),
        ("w_up", gated(w["w_up"])), ("w_down", project(w["w_down"], KF, D)),
        ("ab_in", project(w["ab_in"], KD, AB_IN)), ("ab_out", project(w["ab_out"], KD, D)),
        ("ffn_up", gated(w["ffn_up"])), ("ffn_down", project(w["ffn_down"], KF, D)),
        ("ple0", ple(0)),
        ("qkv", project(w["qkv"], KD, SWA_IN)), ("c_out", project(w["c_out"], KD, D)),
        ("moe", []), ("ple1", ple(1)),
    ]


MOE_PAIRS = D_EXP // NB
MOE_DOWN = [4] * 6 + [2, 2]
MOE_UP_CHUNKS = MOE_PAIRS * 4
MOE_CHUNKS = MOE_UP_CHUNKS + 2 * len(MOE_DOWN)


def build(nc, a, out, upto="end"):
    weights = dict(
        w_in=a["w_in"][0], w_out=a["w_out"][0], w_up=a["w_up"][0], w_down=a["w_down"][0],
        ab_in=a["ab_w_in_2"][0], ab_out=a["ab_w_out_2"][0], ffn_up=a["ffn_w_gate_up_2"][0],
        ffn_down=a["ffn_w_down_2"][0], qkv=a["c_w_qkv_2"][0], c_out=a["c_w_out_2"][0],
        ple_gate=[a["ple_w_gate_2"][0], a["ple_w_gate_2"][1]],
        ple_proj=[a["ple_w_proj_2"][0], a["ple_w_proj_2"][1]],
    )
    moe_up, moe_down = a["moe_w_gate_up_2"][0], a["moe_w_down_2"][0]
    stop = len(N_STREAM) if upto == "end" else N_STREAM.index(upto) + 1
    plan = weight_plan(weights)[:stop]
    live = set(N_STREAM[:stop])

    phase, chunk0 = {}, {}
    c = b = 0
    for name, blocks in plan:
        phase[name], chunk0[name] = [], c
        for n0, n, pieces in blocks:
            phase[name].append((b, c, n0, n, pieces))
            b, c = b + 1, c + len(pieces)
    N_STATIC = c
    width = {cc + i: n * nk for bl in phase.values() for _, cc, _, n, ps in bl for i, (_, nk, _) in enumerate(ps)}
    LOOPS = {"w_in": (3, 2 * NB), "ab_in": (3, 2 * NB), "w_up": (5, NB), "ffn_up": (5, NB)}

    with ExitStack() as ctx:
        free = [-(-nc.sbuf_base // 64) * 64]
        TOP = 229344

        def nbytes(shape):
            n = 4
            for s in shape[1:]:
                n *= s
            return -(-n // 32) * 32

        def at(name, shape, dt, offset):
            assert offset + nbytes(shape) <= TOP, (name, offset + nbytes(shape), TOP)
            return nc.alloc_sbuf_tensor_at(name, shape, dt, offset=offset)

        def sb(name, shape, dt=F32):
            t = at(name, shape, dt, free[0])
            free[0] += nbytes(shape)
            return t

        def layout(first, *specs):
            made = []
            for name, shape, dt in specs:
                made.append(at(name, shape, dt, first))
                first += nbytes(shape)
            return made

        sems = {}

        def S(name):
            if name not in sems:
                sems[name] = ctx.enter_context(nc.semaphore(name))
            return sems[name]

        w_raw = sb("w_raw", [P, RING, CHUNK])
        w_hi = sb("w_hi", [P, RING, CHUNK], F32R)
        w_lo = sb("w_lo", [P, RING, CHUNK], F32R)
        x = sb("x", [P, NT, D])
        y = sb("y", [P, NT, D])
        gain = sb("gain", [P, 2, D])
        ident = sb("ident", [P, P])
        ones = sb("ones", [P, P])
        tri_incl = sb("tri_incl", [P, P])
        tri_excl = sb("tri_excl", [P, P])
        neg_from = sb("neg_from", [P, P])
        neg_ones = sb("neg_ones", [P, P])
        tri_fwd = sb("tri_fwd", [P, P])
        tri_bwd = sb("tri_bwd", [P, P])
        slot_row = sb("slot_row", [P, P])
        head_gain = sb("head_gain", [P, HEAD_V])
        rb_row = sb("rb_row", [P, N_EXP])
        stat = sb("stat", [P, 16])
        bn = sb("bn", [P, NT, 2, 6])
        route = sb("route", [P, 256])
        route_u = sb("route_u", [P, NT, 8], U32)
        route_i = sb("route_i", [P, 4], I32)
        at_xt = free[0]
        at_phase = at_xt + 2 * nbytes([P, KD, SEQ])

        xt_hi, xt_lo = layout(at_xt, ("xt_hi", [P, KD, SEQ], F32R), ("xt_lo", [P, KD, SEQ], F32R))
        (junk,) = layout(at_xt, ("junk", [P, NT, D], F32))

        (p0, logd, tmp0, cum, e1, e2, e3, qk0, conv_w, gate_w, dec, ss8) = layout(
            at_phase, ("p0", [P, NT, D_IN], F32), ("logd", [P, NT, NB], F32), ("tmp0", [P, NT, NB], F32),
            ("cum", [P, 4, SEQ], F32), ("e1", [P, 4, SEQ], F32), ("e2", [P, 4, SEQ], F32),
            ("e3", [P, 4, SEQ], F32), ("qk0", [P, 4, SEQ], F32), ("conv_w", [P, 3, D_HALF], F32),
            ("gate_w", [2 * RANK + 1, 2 * N_GK], F32), ("dec", [P, 4, 4], F32), ("ss8", [P, 3, 8], F32))
        o_logd = at_phase + nbytes([P, NT, D_IN])
        (kout, st, lrt) = layout(
            o_logd, ("kout", [P, NT, NB], F32),
            ("st", [P, 2, 2, 2 * NT, P], F32),
            ("lrt", [2 * RANK + 1, SEQ], F32))
        (state, q_half) = layout(
            at_xt, ("state", [P, 4, 4, HEAD_V], F32), ("q_half", [P, 2, 4, SEQ], F32))
        (ht_hi, ht_lo, pg, pv, ug, uv, cw) = layout(
            at_phase, ("ht_hi", [P, KF, SEQ], F32R), ("ht_lo", [P, KF, SEQ], F32R), ("pg", [P, NT, NB], F32),
            ("pv", [P, NT, NB], F32), ("ug", [P, 4, SEQ], F32), ("uv", [P, 4, SEQ], F32),
            ("cw", [P, 2 * KF, 3], F32))
        (p1, qk1, pt, sba, mask_fox, neg_head, ct, fbias, lf, cq, smx, mask_sb, keep_sb) = layout(
            at_phase, ("p1", [P, NT, AB_IN], F32), ("qk1", [P, 8, SEQ], F32), ("pt", [P, 2, SCW], F32),
            ("sba", [P, 4, SCW], F32), ("mask_fox", [P, SCW], F32), ("neg_head", [P, N_AB, P], F32),
            ("ct", [P, SEQ], F32), ("fbias", [P, N_AB], F32), ("lf", [P, 3, NT, N_AB], F32),
            ("cq", [P, NT, N_AB], F32), ("smx", [P, 6, NT, N_AB], F32), ("mask_sb", [P, SCW], F32),
            ("keep_sb", [P, SCW], F32))
        (s_all,) = layout(at_xt, ("s_all", [P, N_AB, SCW], F32))
        (sbb,) = layout(at_xt, ("sbb", [P, 4, SCW], F32))
        (p2, qk2, pt2, mask_swa, kdup, rope, rtmp, smx2, sink) = layout(
            at_phase, ("p2", [P, NT, SWA_IN], F32), ("qk2", [P, 10, SEQ], F32), ("pt2", [P, 2, SCW], F32),
            ("mask_swa", [P, SCW], F32), ("kdup", [P, NT, N_KV, 2, DH], F32),
            ("rope", [P, 2, NT, ROPE_HALF], F32), ("rtmp", [P, 4, NT, 18 * ROPE_HALF], F32),
            ("smx2", [P, 6, NT, 8], F32), ("sink", [P, N_SWA], F32))
        (pn, ppt_hi, ppt_lo, sig) = layout(
            at_phase, ("pn", [P, NT, D_PLE], F32), ("ppt_hi", [P, 2, SEQ], F32R), ("ppt_lo", [P, 2, SEQ], F32R),
            ("sig", [P, NT, NB], F32))
        (xn_hi, xn_lo, xg_hi, xg_lo, mh_hi, mh_lo, mg, mh, rw) = layout(
            at_phase, ("xn_hi", [P, NT, D], F32R), ("xn_lo", [P, NT, D], F32R), ("xg_hi", [P, KD, P], F32R),
            ("xg_lo", [P, KD, P], F32R), ("mh_hi", [P, KE, P], F32R), ("mh_lo", [P, KE, P], F32R),
            ("mg", [P, NB], F32), ("mh", [P, 2, NB], F32), ("rw", [P, KD, N_EXP], F32))
        (ys_hi, ys_lo, sel, selt, gslot) = layout(
            at_xt, ("ys_hi", [P, D], F32R), ("ys_lo", [P, D], F32R), ("sel", [P, NT, P], F32R),
            ("selt", [P, SEQ], F32R), ("gslot", [P, 1], F32))

        psum = ctx.enter_context(nc.psum_tensor("psum", [P, 8, NB], F32))
        acc = [[psum[:, 2 * s + t, :] for t in range(NT)] for s in range(2)]
        scr = psum[:, 4:8, :]

        N_BEFORE_MOE = chunk0.get("moe", N_STATIC)
        R_ITEM = MOE_CHUNKS // RING

        block = ctx.enter_context(nc.Block())

        class Place:
            chunk, cap, looping = 0, N_BEFORE_MOE, False

        def split_loop(eng, name, body, me=None, unroll=False):
            bl = phase[name]
            if name in LOOPS and not unroll:
                trips, _ = LOOPS[name]
                with eng.Fori(0, trips) as i:
                    if me:
                        me.looping, before = True, me.chunk
                    body(bl[0:2], i)
                if me:
                    assert me.chunk == before + RING
                    me.looping, me.chunk = False, before + RING * trips
                bl = bl[2 * trips:]
            for i in range(0, len(bl), 2):
                body(bl[i:i + 2], 0)

        def ncol(name, n0, r):
            return n0 if isinstance(r, int) else r * LOOPS[name][1] + n0

        def sl(n0, n):
            return slice(n0, n0 + n) if isinstance(n0, int) else bass.ds(n0, n)

        def wait_used(eng, c, r=0):
            eng.wait_ge(S("w_used"), RING + c + RING * r)

        def wait_evacuated(eng, bb, r=0):
            eng.wait_ge(S(f"acc_free{bb % 2}"), bb // 2 + 2 + r)

        def last_block(name):
            return phase[name][-1][0]

        def wait_phase_evacuated(eng, name):
            wait_evacuated(eng, last_block(name))
            wait_evacuated(eng, last_block(name) - 1)

        def end_chunk(name):
            _, cc, _, _, ps = phase[name][-1]
            return cc + len(ps)

        @block.sync
        def _(sp):
            sp.dma_start(x[:], a["x"][0].rearrange("(t p) n -> p t n", p=P)).then_inc(S("x_landed"), 16)

            def load(k, r, src, nk, n):
                sp.wait_ge(S("lo_ready"), k + 1 + RING * r)
                sp.dma_start(w_raw[:, k % RING, 0:nk * n].rearrange("p (k n) -> p k n", n=n), src)\
                  .then_inc(S(f"w_landed{k % RING}"), 16)

            def loads(name, r0=0):
                def body(blocks, r):
                    for _, cc, n0, n, ps in blocks:
                        for i, (k0, nk, m) in enumerate(ps):
                            load(cc + i, r + r0, m[k0 * P:(k0 + nk) * P, sl(ncol(name, n0, r), n)]
                                 .rearrange("(k p) n -> p k n", p=P), nk, n)
                split_loop(sp, name, body)

            for name in N_STREAM[:min(stop, 11)]:
                loads(name)
            if "moe" in live:
                def expert(e, r):
                    k = N_BEFORE_MOE
                    for j in range(MOE_PAIRS):
                        for n0 in (j * NB, D_EXP + j * NB):
                            for k0 in (0, 4):
                                load(k, r, moe_up[bass.ds(e, 1), k0 * P:(k0 + 4) * P, n0:n0 + NB]
                                     .rearrange("e (k p) n -> p (e k) n", p=P), 4, NB)
                                k += 1
                    for n0 in (0, NB):
                        k0 = 0
                        for nk in MOE_DOWN:
                            load(k, r, moe_down[bass.ds(e, 1), k0 * P:(k0 + nk) * P, n0:n0 + NB]
                                 .rearrange("e (k p) n -> p (e k) n", p=P), nk, NB)
                            k, k0 = k + 1, k0 + nk

                with sp.Fori(0, N_EXP) as i:
                    expert(i, i * R_ITEM)
                sp.wait_ge(S("routed"), 1)
                n_items = sp.value_load(route_i[0:1, 3:4], min_val=N_EXP, max_val=ITEMS)
                for j in range(ITEMS - N_EXP):
                    with sp.If(n_items > N_EXP + j):
                        e = sp.value_load(route_i[0:1, j:j + 1], min_val=0, max_val=N_EXP - 1)
                        expert(e, (N_EXP + j) * R_ITEM)
                    sp.end_ifs()
                if "ple1" in live:
                    loads("ple1", n_items * R_ITEM)
            sp.wait_ge(S("x_done"), 1)
            sp.dma_start(out[0].rearrange("(t p) n -> p t n", p=P), x[:]).then_inc(S("out_landed"), 16)
            sp.wait_ge(S("out_landed"), 16)

        def kv_place(g, c_):
            order = [[(0, 0), (1, 0), (0, 2), (1, 2), (2, 2), (3, 2)], [(0, 1), (1, 1), (2, 3), (3, 3), (2, 1), (3, 1)]]
            i = order[c_ % 2].index((g, c_))
            return scr[:, 2 * (c_ % 2) + i // 4, (i % 4) * P:(i % 4 + 1) * P]

        gains = [("norm_mix_pre", 0), ("norm_mix_post", 0), ("norm_ffn_pre", 0), ("norm_ffn_post", 0),
                 ("ln_mix_g_2", 0), ("ln_mix_b_2", 0), ("ln_ffn_g_2", 0), ("ln_ffn_b_2", 0),
                 ("ln_mix_g_2", 1), ("ln_mix_b_2", 1), ("ln_ffn_g_2", 1), ("ln_ffn_b_2", 1)]

        @block.gpsimd
        def _(pool):
            def one(ins):
                pool.drain()

            def gain_row(i):
                if i >= 2:
                    pool.wait_ge(S("gain_used"), i - 1)
                g, l = gains[i]
                pool.dma_start(gain[:, i % 2, :], a[g][l:l + 1, :].broadcast_to([P, D]))\
                    .then_inc(S(f"gain_landed{i % 2}"), 16)

            def keep(t, pattern, first, per_row, fill=0.0, op=ALU.is_ge):
                one(pool.affine_select(out=t, in_=t, pattern=pattern, compare_op=op, fill=fill, base=first,
                                       channel_multiplier=per_row))

            gain_row(0)
            gain_row(1)
            pool.memset(ident[:], 0.0)
            one(None)
            pool.affine_select(out=ident[:], in_=ident[:], pattern=[[-1, P]], compare_op=ALU.not_equal, fill=1.0,
                               base=0, channel_multiplier=1).then_inc(S("ident_ready"), 1)
            pool.dma_start(conv_w[:], a["conv_a"].broadcast_to([P, 3, D_HALF])).then_inc(S("conv_w_landed"), 16)
            pool.dma_start(head_gain[:], a["gla_head_norm"].broadcast_to([P, HEAD_V])).then_inc(S("head_gain_landed"), 16)
            pool.dma_start(rb_row[:], a["router_b_2"].broadcast_to([P, N_EXP])).then_inc(S("rb_landed"), 16)
            pool.memset(gate_w[:], 0.0)
            for t, v in ((ones, 1.0), (tri_incl, 1.0), (tri_excl, 1.0), (neg_from, -1.0), (neg_ones, -1.0),
                         (tri_fwd, DECAY), (tri_bwd, DECAY)):
                pool.memset(t[:], v)
            pool.iota(slot_row[:], pattern=[[1, P]], base=0, channel_multiplier=0,
                      allow_small_or_imprecise_dtypes=True)
            one(None)
            for src, r, cc in (("gate_up_fwd", 0, 0), ("gate_up_bwd", RANK, N_GK)):
                pool.dma_start(gate_w[r:r + RANK, cc:cc + N_GK], a[src][0]).then_inc(S("gate_w_landed"), 16)
            for src, cc in (("gate_bias_fwd", 0), ("gate_bias_bwd", N_GK)):
                pool.dma_start(gate_w[2 * RANK:2 * RANK + 1, cc:cc + N_GK], a[src]).then_inc(S("gate_w_landed"), 16)
            keep(tri_incl[:], [[1, P]], 0, -1)
            keep(tri_excl[:], [[1, P]], -1, -1)
            keep(neg_from[:], [[-1, P]], 0, 1)
            keep(tri_fwd[:], [[1, P]], 0, -1)
            keep(tri_bwd[:], [[-1, P]], 0, 1)
            keep(tri_fwd[:, GLA_CHUNK:P], [[0, P - GLA_CHUNK]], -GLA_CHUNK, 1)
            keep(tri_bwd[:, 0:GLA_CHUNK], [[0, GLA_CHUNK]], GLA_CHUNK - 1, -1)
            pool.drain().then_inc(S("tri_ready"), 1)

            for bb in (0, 1, 2):
                wait_evacuated(pool, bb)
            pool.wait_ge(S("conv_w_landed"), 16)
            gc, gv = p0[:, :, C_GC:C_GC + D_HALF], p0[:, :, C_GV:C_GV + D_HALF]
            ya = y[:, :, 0:D_HALF]
            one(pool.tensor_tensor(gc, gc, gv, ALU.mult))
            pool.memset(gv, 0.0)
            one(pool.memset(ya, 0.0))
            for dst, src in ((gv[1:P, :, :], gc[0:P - 1, :, :]), (gv[0:1, 1:2, :], gc[P - 1:P, 0:1, :]),
                             (ya[0:P - 1, :, :], gc[1:P, :, :]), (ya[P - 1:P, 0:1, :], gc[0:1, 1:2, :])):
                pool.dma_start(dst, src).then_inc(S("shift_landed"), 16)
            pool.wait_ge(S("shift_landed"), 64)
            for dst, tap in ((ya, 2), (gv, 0), (gc, 1)):
                for t in range(NT):
                    pool.tensor_tensor(dst[:, t, :], dst[:, t, :], conv_w[:, tap, :], ALU.mult)
            one(None)
            one(pool.tensor_tensor(gv, gv, gc, ALU.add))
            one(pool.tensor_tensor(ya, ya, gv, ALU.add))
            pool.tensor_tensor(ya, ya, p0[:, :, C_GB:C_GB + D_HALF], ALU.mult).then_inc(S("ya_ready"), 1)

            gain_row(2)
            if "w_up" in live:
                gain_row(3)
                wait_phase_evacuated(pool, "w_out")
                for k in range(2 * KF):
                    pool.dma_start(cw[:, k, :], a["conv_ffn"][0, :, k * P:(k + 1) * P].rearrange("j p -> p j"),
                                   allow_slow_non_contiguous=True).then_inc(S("cw_landed"), 16)
            if "ab_in" in live:
                for i in (4, 5):
                    gain_row(i)
                wait_phase_evacuated(pool, "w_down")
                pool.dma_start(fbias[:], a["ab_b_f_2"].broadcast_to([P, N_AB])).then_inc(S("fbias_landed"), 16)
                for t, v in ((mask_fox[:], 0.0), (mask_sb[:], 0.0), (keep_sb[:], 1.0), (neg_head[:], -1.0), (ct[:], 0.0)):
                    pool.memset(t, v)
                one(None)
                keep(mask_fox[:, 0:P], [[-1, P]], 0, 1, NEG)
                keep(mask_fox[:, P:SCW], [[-1, SEQ]], P, 1, NEG)
                for t, fill in ((mask_sb, NEG), (keep_sb, 0.0)):
                    keep(t[:, 0:SEQ], [[1, SEQ]], -1, -1, fill)
                    keep(t[:, SEQ:SCW], [[1, P]], -1, -1, fill)
                keep(neg_head[:], [[1, N_AB], [0, P]], 0, -1, 0.0)
                keep(neg_head[:], [[-1, N_AB], [0, P]], 0, 1, 0.0)
                pool.drain().then_inc(S("ab_masks_ready"), 1)
            if "ffn_up" in live:
                for i in (6, 7):
                    gain_row(i)
            if "ple0" in live:
                wait_phase_evacuated(pool, "ffn_down")
                pool.dma_start(pn[:], a["p_2"][0, 0].rearrange("(t p) n -> p t n", p=P)).then_inc(S("p_landed"), 16)
            if "qkv" in live:
                for i in (8, 9):
                    gain_row(i)
                pool.wait_ge(S("ple_x"), 1)
                pool.dma_start(rope[:], a["rope"].rearrange("c (t p) n -> p c t n", p=P)).then_inc(S("rope_landed"), 16)
                pool.dma_start(sink[:], a["c_sinks_2"].broadcast_to([P, N_SWA])).then_inc(S("sink_landed"), 16)
                one(pool.memset(mask_swa[:], 0.0))
                keep(mask_swa[:, 0:P], [[-1, P]], 0, 1, NEG)
                keep(mask_swa[:, P:SCW], [[-1, SEQ]], P, 1, NEG)
                keep(mask_swa[:, P:SCW], [[1, SEQ]], -1, -1, NEG)
                pool.drain().then_inc(S("swa_mask_ready"), 1)
            if "moe" in live:
                for i in (10, 11):
                    gain_row(i)
                wait_phase_evacuated(pool, "c_out")
                pool.dma_start(rw[:], a["router_w_2"][0].rearrange("(k p) e -> p k e", p=P)).then_inc(S("rw_landed"), 16)
            if "ple1" in live:
                pool.wait_ge(S("moe_x"), 1)
                pool.dma_start(pn[:], a["p_2"][1, 0].rearrange("(t p) n -> p t n", p=P)).then_inc(S("p_landed"), 16)

        @block.scalar
        def _(act):
            me = Place()
            for s in range(2):
                act.sem_inc(S(f"acc_free{s}"), 1)

            def copy(o, i, func=ACT.Copy, **kw):
                return act.activation(o, i, func, **kw)

            def round_chunk(k, r, n):
                act.wait_ge(S(f"w_landed{k % RING}"), 16 * (k // RING + 1) + 16 * r)
                wait_used(act, k - RING + 1, r)
                copy(w_hi[:, k % RING, 0:n], w_raw[:, k % RING, 0:n]).then_inc(S("hi_ready"), 1)

            def round_to(c, r=0):
                while me.chunk < (c if me.looping else min(c, me.cap)):
                    round_chunk(me.chunk, r, CHUNK if me.looping else width[me.chunk])
                    me.chunk += 1

            def root(n):
                act.wait_ge(S("ms_ready"), n + 1)
                copy(stat[:, 2:4], stat[:, 0:2], ACT.Sqrt).then_inc(S("root_ready"), 1)

            def operand(m):
                for j in range(4):
                    act.wait_ge(S("t_ready"), 4 * m + j + 1)
                    copy(xt_hi[:, 4 * (j % 2):4 * (j % 2) + 4, (j // 2) * P:(j // 2 + 1) * P],
                         scr[:, j, :].rearrange("p (k n) -> p k n", n=P)).then_inc(S("xt_hi_ready"), 1)

            def evacuate(name, dst):
                def body(blocks, r):
                    for bb, cc, n0, n, ps in blocks:
                        round_to(cc + len(ps) + 2, r)
                        wait_used(act, cc + len(ps), r)
                        for t in range(NT):
                            i = copy(dst[:, t, sl(ncol(name, n0, r), n)], acc[bb % 2][t][:, 0:n])
                        i.then_inc(S(f"acc_free{bb % 2}"), 1)
                split_loop(act, name, body, me)

            def log_sigmoid_tail(o, z):
                copy(o, z, ACT.Abs)
                act.drain()
                copy(o, o, ACT.Exp, scale=-1.0)
                act.drain()
                return copy(o, o, ACT.Ln, bias=1.0)

            root(0)
            operand(0)
            round_to(2)
            evacuate("w_in", p0)
            act.wait_ge(S("lr_t"), 1)
            copy(lrt[0:2 * RANK, :], scr[0:2 * RANK, 0, 0:SEQ]).then_inc(S("lrt_ready"), 1)
            act.wait_ge(S("qk_t"), 1)
            copy(qk0[:, 0:2, :], scr[:, 1, :].rearrange("p (f n) -> p f n", n=SEQ), scale=HEAD_K ** -0.5)
            copy(qk0[:, 2:4, :], scr[:, 2, :].rearrange("p (f n) -> p f n", n=SEQ)).then_inc(S("qk0_ready"), 1)
            act.wait_ge(S("gate_pre"), 1)
            log_sigmoid_tail(tmp0[:], psum[:, 0:2, :]).then_inc(S("gate_ln"), 1)
            act.wait_ge(S("cum_ready"), 1)
            copy(e1[:], cum[:], ACT.Exp).then_inc(S("gla_exp"), 1)
            copy(e2[:], cum[:], ACT.Exp, scale=-1.0).then_inc(S("gla_exp"), 1)
            act.wait_ge(S("cum_rest"), 1)
            copy(e3[:], e3[:], ACT.Exp).then_inc(S("gla_exp"), 1)
            act.wait_ge(S("q_in"), 1)
            act.wait_ge(S("q_half_zero"), 1)
            for par in range(2):
                v = lambda t: t.rearrange("p g (c q n) -> p (g c) q n", q=2, n=GLA_CHUNK)[:, :, par, :]
                i = copy(v(q_half[:, par]), v(e1[:]))
            i.then_inc(S("q_half_ready"), 1)
            for t in range(NT):
                act.wait_ge(S("kout_t"), t + 1)
                copy(kout[:, t, :], scr[:, 3 * t, :]).then_inc(S("kout_ready"), 1)
            go = p0[:, :, C_GO:C_GO + D_HALF]
            wait_evacuated(act, 5)
            copy(go, go, ACT.Silu).then_inc(S("go_ready"), 1)
            act.wait_ge(S("gla_o"), NT)
            act.wait_ge(S("e2_free"), 1)
            copy(e2[:], psum[:, 0:4, 0:SEQ], ACT.Square).then_inc(S("o_sq"), 1)
            act.wait_ge(S("o_ms"), 1)
            copy(ss8[:, 1, :], ss8[:, 0, :], ACT.Sqrt).then_inc(S("o_root"), 1)
            operand(1)
            evacuate("w_out", y)
            root(1)

            def up_conv(blocks, r):
                (bg, cg, n0, n, _), (bv, cv, _, _, psv) = blocks
                j, nc_ = n0 // NB, n // P
                for bb, cc, dst in ((bg, cg, pg), (bv, cv, pv)):
                    end = cc + (cv - cg)
                    round_to(end + 2)
                    wait_used(act, end)
                    for t in range(NT):
                        i = copy(dst[:, t, 0:n], acc[bb % 2][t][:, 0:n])
                    i.then_inc(S(f"acc_free{bb % 2}"), 1)
                if j:
                    act.wait_ge(S("ht_ready"), j)
                for h, u in ((0, ug), (1, uv)):
                    act.wait_ge(S("conv_t"), 2 * j + h + 1)
                    if j == 0 and h == 0:
                        act.wait_ge(S("cw_landed"), 16 * 2 * KF)
                    for k in range(nc_):
                        ch = h * KF + 4 * j + k
                        i = copy(u[:, k, :], scr[:, 2 * h + k // 2, (k % 2) * SEQ:(k % 2 + 1) * SEQ],
                                 scale=cw[:, ch, 1:2])
                    i.then_inc(S("tap_mid"), 1)
                act.wait_ge(S("gate_conv"), j + 1)
                copy(ug[:, 0:nc_, :], ug[:, 0:nc_, :], ACT.Silu).then_inc(S("silu_ready"), 1)
                act.wait_ge(S("h_ready"), j + 1)
                copy(ht_hi[:, 4 * j:4 * j + nc_, :], uv[:, 0:nc_, :]).then_inc(S("ht_hi_ready"), 1)

            if "w_up" in live:
                root(2)
                operand(2)
                split_loop(act, "w_up", up_conv, me, unroll=True)
            if "w_down" in live:
                evacuate("w_down", y)
                root(3)

            def softmax(q, smx_, sink_=False):
                act.wait_ge(S("at_negm"), q + 1)
                for h in range(8):
                    for t, (c0, c1) in enumerate(((0, P), (P, SCW))):
                        i = copy(s_all[:, h, c0:c1], s_all[:, h, c0:c1], ACT.Exp, bias=smx_[:, 1, t, h:h + 1],
                                 accum_out=smx_[:, 2, t, h:h + 1])
                    act.drain().then_inc(S("at_p"), 1)
                if sink_:
                    copy(smx_[:, 4, :, :], smx_[:, 3, :, :], ACT.Exp)
                act.drain().then_inc(S("at_sum"), 1)

            if "ab_in" in live:
                operand(3)
                evacuate("ab_in", p1)
                act.wait_ge(S("lf_pre"), 1)
                log_sigmoid_tail(lf[:, 1, :, :], lf[:, 0, :, :]).then_inc(S("lf_ln"), 1)
                for g in range(2):
                    for tile in range(4):
                        act.wait_ge(S("ab_t"), 4 * g + tile + 1)
                        copy(qk1[:, 2 * tile:2 * tile + 2, :], scr[:, tile, :].rearrange("p (f n) -> p f n", n=SEQ),
                             scale=DH ** -0.5 if tile < 2 else 1.0).then_inc(S("qk1_ready"), 1)
                    if g == 0:
                        softmax(0, smx)
                for g in range(2):
                    act.wait_ge(S("sb_z"), g + 1)
                    log_sigmoid_tail(sba[:], scr[:, :, 0:SCW]).then_inc(S("sb_ln"), 1)
                    act.wait_ge(S("sb_masked"), g + 1)
                    copy(sba[:], sba[:], ACT.Exp).then_inc(S("sb_a"), 1)
            if "ab_out" in live:
                operand(4)
                evacuate("ab_out", y)
                root(4)

            def up_gated(blocks, r):
                (bg, cg, n0, n, _), (bv, cv, _, _, _) = blocks
                j, nc_ = n0 // NB, n // P
                round_to(cv + 2)
                wait_used(act, cv)
                if j:
                    act.wait_ge(S("hn_ready"), j)
                for t in range(NT):
                    i = copy(pv[:, t, 0:n], acc[bg % 2][t][:, 0:n], ACT.Silu)
                i.then_inc(S(f"acc_free{bg % 2}"), 1)
                round_to(cv + (cv - cg) + 2)
                act.wait_ge(S("hn_t"), j + 1)
                copy(ht_hi[:, 4 * j:4 * j + nc_, :], scr[:, 0:-(-nc_ // 2), :].rearrange("p b (f n) -> p (b f) n", n=SEQ))\
                    .then_inc(S("ht_hi_ready"), 1)

            if "ffn_up" in live:
                operand(5)
                split_loop(act, "ffn_up", up_gated, me, unroll=True)
            if "ffn_down" in live:
                evacuate("ffn_down", y)
                root(5)

            def ple(i, m, r=0):
                operand(m)
                act.wait_ge(S("p_t"), i + 1)
                copy(ppt_hi[:], scr[:, 0, :].rearrange("p (k n) -> p k n", n=SEQ)).then_inc(S("ppt_hi_ready"), 1)
                name = f"ple{i}"
                for q in range(2):
                    (bg, cg, _, _, _), (bp, cp, _, _, psp) = phase[name][2 * q:2 * q + 2]
                    round_to(cp + 1, r)
                    wait_used(act, cp, r)
                    if q or i:
                        act.wait_ge(S("ple_added"), 2 * i + q)
                    for t in range(NT):
                        j = copy(sig[:, t, :], acc[bg % 2][t], ACT.Sigmoid)
                    j.then_inc(S(f"acc_free{bg % 2}"), 1)
                    round_to(cp + 3, r)

            if "ple0" in live:
                ple(0, 6)
            if "qkv" in live:
                operand(7)
                evacuate("qkv", p2)
                for j in range(3):
                    act.wait_ge(S("swa_t"), j + 1)
                    nb = 4 if j < 2 else 2
                    if j < 2:
                        copy(qk2[:, 4 * j:4 * j + 4, :], scr[:, 2 * (j % 2):2 * (j % 2) + 2, :]
                             .rearrange("p b (f n) -> p (b f) n", n=SEQ), scale=DH ** -0.5)\
                            .then_inc(S("qk2_ready"), 1)
                    else:
                        copy(qk2[:, 8:10, :], scr[:, 0, :].rearrange("p (f n) -> p f n", n=SEQ))\
                            .then_inc(S("qk2_ready"), 1)
                for g in range(2):
                    softmax(1 + g, smx2, True)
            if "c_out" in live:
                operand(8)
                evacuate("c_out", y)
                root(6)

            def item(i):
                c0, r = N_BEFORE_MOE, i * R_ITEM

                def rounds(k0, k1):
                    for k in range(k0, k1):
                        n = NB * MOE_DOWN[(k - MOE_UP_CHUNKS) % len(MOE_DOWN)] if k >= MOE_UP_CHUNKS else CHUNK
                        round_chunk(c0 + k, r, n)

                rounds(0, 2)
                act.wait_ge(S("gathered"), 3 * i + 1)
                copy(xg_hi[:], scr[:, 0:2, :].rearrange("p b (k n) -> p (b k) n", n=P)).then_inc(S("xg_hi_ready"), 1)
                act.wait_ge(S("gathered"), 3 * i + 3)
                copy(selt[:], psum[:, 2, 0:SEQ])
                copy(gslot[:], psum[:, 2, SEQ:SEQ + 1]).then_inc(S("selt_ready"), 1)
                rounds(2, 4)
                for j in range(MOE_PAIRS):
                    wait_used(act, c0 + 4 * j + 2, r)
                    if j:
                        act.wait_ge(S("mh_ready"), MOE_PAIRS * i + j)
                    copy(mg[:], psum[:, 2 * (j % 2), :], ACT.Silu).then_inc(S("mg_ready"), 1)
                    rounds(4 * j + 4, 4 * j + 6)
                    if j:
                        act.wait_ge(S("mh_t"), MOE_PAIRS * i + j)
                        copy(mh_hi[:, 4 * j - 4:4 * j, :], psum[:, 6 + (j - 1) % 2, :].rearrange("p (k n) -> p k n", n=P))\
                            .then_inc(S("mh_hi_ready"), 1)
                    rounds(4 * j + 6, 4 * j + 8)
                j = MOE_PAIRS
                act.wait_ge(S("mh_t"), MOE_PAIRS * i + j)
                copy(mh_hi[:, 4 * j - 4:4 * j, :], psum[:, 6 + (j - 1) % 2, :].rearrange("p (k n) -> p k n", n=P))\
                    .then_inc(S("mh_hi_ready"), 1)
                k = 4 * j + 4
                for n in range(2):
                    end = MOE_UP_CHUNKS + len(MOE_DOWN) * (n + 1)
                    rounds(k, min(end + 2, MOE_CHUNKS))
                    k = min(end + 2, MOE_CHUNKS)
                    wait_used(act, c0 + end, r)
                    copy(ys_hi[:, n * NB:(n + 1) * NB], psum[:, 4 + n, :], scale=gslot[:, 0:1])\
                        .then_inc(S("ys_hi_ready"), 1)

            if "moe" in live:
                operand(9)
                copy(xn_hi[:], x[:]).then_inc(S("xn_hi_ready"), 1)
                act.wait_ge(S("top_gap"), 1)
                copy(route[:, 142:144], route[:, 140:142], ACT.Exp).then_inc(S("top_exp"), 1)
                act.wait_ge(S("routed"), 1)
                n_items = act.value_load(route_i[0:1, 3:4], min_val=N_EXP, max_val=ITEMS)
                with act.Fori(0, ITEMS) as i:
                    with act.If(i < n_items):
                        item(i)
                    act.end_ifs()
                me.cap = N_STATIC
                root(7)
            if "ple1" in live:
                round_to(me.chunk + 2, n_items * R_ITEM)
                ple(1, 10, n_items * R_ITEM)

        @block.vector
        def _(dve):
            me = Place()
            dve.sem_inc(S("lo_ready"), RING)
            TT, STT, TS = dve.tensor_tensor, dve.scalar_tensor_tensor, dve.tensor_scalar
            used_rows = [0]

            def split_chunk(k, r, n):
                dve.wait_ge(S("hi_ready"), k + 1 + RING * r)
                TT(w_lo[:, k % RING, 0:n], w_raw[:, k % RING, 0:n], w_hi[:, k % RING, 0:n].bitcast(F32), ALU.subtract)\
                    .then_inc(S("lo_ready"), 1)

            def round_to(c, r=0):
                while me.chunk < (c if me.looping else min(c, me.cap)):
                    split_chunk(me.chunk, r, CHUNK if me.looping else width[me.chunk])
                    me.chunk += 1

            def operand(m):
                for j in range(4):
                    dve.wait_ge(S("xt_hi_ready"), 4 * m + j + 1)
                    o = (slice(None), slice(4 * (j % 2), 4 * (j % 2) + 4), slice((j // 2) * P, (j // 2 + 1) * P))
                    TT(xt_lo[o], scr[:, j, :].rearrange("p (k n) -> p k n", n=P), xt_hi[o].bitcast(F32), ALU.subtract)\
                        .then_inc(S("xt_ready"), 1)

            def row(i):
                dve.wait_ge(S(f"gain_landed{i % 2}"), 16 * (i // 2 + 1))
                return gain[:, i % 2, :]

            def inverse_root(n):
                dve.drain().then_inc(S("ms_ready"), 1)
                dve.wait_ge(S("root_ready"), n + 1)
                dve.reciprocal(stat[:, 4:6], stat[:, 2:4])
                dve.drain()

            def rms(n, src):
                for t in range(NT):
                    dve.tensor_tensor_reduce(junk[:, t, :], src[:, t, :], src[:, t, :], 1.0, 0.0, ALU.mult, ALU.add,
                                             stat[:, 6 + t:7 + t])
                dve.drain()
                TS(stat[:, 0:2], stat[:, 6:8], 1.0 / D, RMS_EPS, ALU.mult, ALU.add)
                inverse_root(n)

            def rms_before(n, i):
                rms(n, x)
                g = row(i)
                for t in range(NT):
                    STT(y[:, t, :], x[:, t, :], stat[:, 4 + t:5 + t], g, ALU.mult, ALU.mult)
                dve.drain().then_inc(S("t_source"), 1)
                dve.sem_inc(S("gain_used"), 1)

            def rms_after(n, i):
                rms(n, y)
                g = row(i)
                for t in range(NT):
                    STT(y[:, t, :], y[:, t, :], stat[:, 4 + t:5 + t], g, ALU.mult, ALU.mult)
                dve.drain().then_inc(S("gain_used"), 1)
                TT(x[:], x[:], y[:], ALU.add)
                dve.drain()

            def layer_norm(n, i):
                for t in range(NT):
                    STT(x[:, t, :], x[:, t, :], ALPHA, y[:, t, :], ALU.mult, ALU.add)
                dve.drain()
                for t in range(NT):
                    for h in range(2):
                        dve.bn_stats(bn[:, t, h, :], x[:, t, h * NB:(h + 1) * NB])
                dve.drain()
                for t in range(NT):
                    dve.bn_aggr(stat[:, 8 + 2 * t:10 + 2 * t], bn[:, t, :, :])
                dve.drain()
                TS(stat[:, 0:2], stat[:, 9:12:2], LN_EPS, None, ALU.add)
                inverse_root(n)
                g, b_ = row(i), row(i + 1)
                for t in range(NT):
                    TS(x[:, t, :], x[:, t, :], stat[:, 8 + 2 * t:9 + 2 * t], stat[:, 4 + t:5 + t], ALU.subtract, ALU.mult)
                for v, op in ((g, ALU.mult), (b_, ALU.add)):
                    dve.drain()
                    for t in range(NT):
                        TT(x[:, t, :], x[:, t, :], v, op)
                dve.drain().then_inc(S("gain_used"), 2)
                dve.sem_inc(S("t_source"), 1)

            def follow(name):
                def body(blocks, r):
                    for bb, cc, n0, n, ps in blocks:
                        round_to(cc + len(ps) + 2, r)
                split_loop(dve, name, body, me)
                wait_phase_evacuated(dve, name)

            dve.wait_ge(S("x_landed"), 16)
            rms_before(0, 0)
            operand(0)
            round_to(2)
            follow("w_in")
            dve.memset(q_half[:], 0.0).then_inc(S("q_half_zero"), 1)
            dve.memset(lrt[2 * RANK:2 * RANK + 1, :], 1.0).then_inc(S("lrt_ones"), 1)
            dve.wait_ge(S("gate_ln"), 1)
            STT(logd[:], psum[:, 0:2, :], 0.0, tmp0[:], ALU.min, ALU.subtract).then_inc(S("logd_ready"), 1)
            dve.wait_ge(S("cum_t"), 1)
            cum_ps = psum[:, 2:4, :].rearrange("p b (f n) -> p (b f) n", n=SEQ)
            dve.tensor_copy(cum[:], cum_ps)
            dve.drain().then_inc(S("cum_ready"), 1)
            chunks = lambda t: t.rearrange("p f (c n) -> p f c n", n=GLA_CHUNK)
            for d, last in ((0, GLA_CHUNK - 1), (1, 0)):
                for f in (2 * d, 2 * d + 1):
                    v = chunks(cum[:])[:, f, :, :]
                    i = TT(chunks(e3[:])[:, f, :, :], v[:, :, last:last + 1].broadcast_to([P, 4, GLA_CHUNK]), v, ALU.subtract)
            i.then_inc(S("cum_rest"), 1)
            dve.wait_ge(S("gla_exp"), 1)
            for d, last in ((0, GLA_CHUNK - 1), (1, 0)):
                dve.tensor_copy(dec[:, 2 * d:2 * d + 2, :], chunks(e1[:])[:, 2 * d:2 * d + 2, :, last])
            dve.drain()
            dve.wait_ge(S("qk0_ready"), 1)
            for n, (e, q) in enumerate(((e1, 0), (e2, 2), (e3, 2))):
                dve.wait_ge(S("gla_exp"), n + 1)
                for d in range(2):
                    i = TT(e[:, 2 * d:2 * d + 2, :], e[:, 2 * d:2 * d + 2, :], qk0[:, q:q + 2, :], ALU.mult)
                i.then_inc(S(("q_in", "k_in", "k_out")[n]), 1)
            dve.memset(st[:], 0.0)
            dve.drain()
            for d, tri in ((0, tri_fwd), (1, tri_bwd)):
                dve.wait_ge(S("gla_scores"), d + 1)
                dve.copy_predicated(st[:, d].rearrange("p a b n -> p (a b) n"),
                                    tri[:].bitcast(I32).unsqueeze(1).broadcast_to([P, 8, P]),
                                    psum[:, 2 * d:2 * d + 2, :].rearrange("p b (k n) -> p (b k) n", n=P))\
                    .then_inc(S("st_ready"), 1)
            dve.wait_ge(S("gla_kv"), 1)
            for step in range(3):
                for g in range(4):
                    src, dst = (step, step + 1) if g < 2 else (3 - step, 2 - step)
                    kv = kv_place(g, src)
                    if step == 0:
                        dve.tensor_copy(state[:, g, dst, :], kv)
                    else:
                        STT(state[:, g, dst, :], state[:, g, src, :], dec[:, g, src:src + 1], kv, ALU.mult, ALU.add)
                dve.drain()
            dve.sem_inc(S("state_ready"), 1)
            dve.sem_inc(S("e2_free"), 1)
            dve.wait_ge(S("o_sq"), 1)
            dve.reduce_sum(ss8[:, 2, :], e2[:].rearrange("p a (b n) -> p (a b) n", n=HEAD_V), AX_X)
            dve.drain()
            TS(ss8[:, 0, :], ss8[:, 2, :], 1.0 / HEAD_V, RMS_EPS, ALU.mult, ALU.add).then_inc(S("o_ms"), 1)
            dve.wait_ge(S("o_root"), 1)
            dve.reciprocal(ss8[:, 2, :], ss8[:, 1, :])
            dve.drain()
            o8 = e3[:].rearrange("p a (b n) -> p (a b) n", n=HEAD_V)
            for t in range(NT):
                TT(o8[:, 4 * t:4 * t + 4, :].rearrange("p (a b) n -> p a b n", b=2),
                   psum[:, 2 * t:2 * t + 2, 0:SEQ].rearrange("p a (b n) -> p a b n", n=HEAD_V),
                   ss8[:, 2, 4 * t:4 * t + 4].rearrange("p (a b) -> p a b", b=2).unsqueeze(3).broadcast_to([P, 2, 2, HEAD_V]),
                   ALU.mult)
            dve.drain()
            dve.wait_ge(S("head_gain_landed"), 16)
            TT(o8, o8, head_gain[:].unsqueeze(1).broadcast_to([P, 8, HEAD_V]), ALU.mult)
            dve.drain()
            dve.wait_ge(S("go_ready"), 1)
            dve.wait_ge(S("ya_ready"), 1)
            for t in range(NT):
                heads = lambda v: v.rearrange("p (b a n) -> p a b n", a=2, n=HEAD_V)
                TT(heads(y[:, t, D_HALF:D]), o8[:, 4 * t:4 * t + 4, :].rearrange("p (a b) n -> p a b n", b=2),
                   heads(p0[:, t, C_GO:C_GO + D_HALF]), ALU.mult)
            dve.drain().then_inc(S("t_source"), 1)
            operand(1)
            follow("w_out")
            rms_after(1, 1)

            def up_conv(blocks, r):
                (bg, cg, n0, n, _), (bv, cv, _, _, _) = blocks
                j, nc_ = n0 // NB, n // P
                round_to(cv + 2)
                round_to(cv + (cv - cg) + 2)
                for h, u in ((0, ug), (1, uv)):
                    dve.wait_ge(S("tap_mid"), 2 * j + h + 1)
                    for tap in (0, 2):
                        o, s = (slice(1, SEQ), slice(0, SEQ - 1)) if tap == 0 else (slice(0, SEQ - 1), slice(1, SEQ))
                        for k in range(nc_):
                            ps_ = scr[:, 2 * h + k // 2, (k % 2) * SEQ:(k % 2 + 1) * SEQ]
                            ch = h * KF + 4 * j + k
                            STT(u[:, k, o], ps_[:, s], cw[:, ch, tap:tap + 1], u[:, k, o], ALU.mult, ALU.add)
                        if (h, tap) == (0, 2):
                            dve.drain().then_inc(S("gate_conv"), 1)
                        elif (h, tap) == (1, 2):
                            dve.drain().then_inc(S("scr_free"), 1)
                        else:
                            dve.drain()
                dve.wait_ge(S("silu_ready"), j + 1)
                TT(uv[:, 0:nc_, :], ug[:, 0:nc_, :], uv[:, 0:nc_, :], ALU.mult)
                dve.drain().then_inc(S("h_ready"), 1)
                dve.wait_ge(S("ht_hi_ready"), j + 1)
                o = (slice(None), slice(4 * j, 4 * j + nc_))
                TT(ht_lo[o], uv[:, 0:nc_, :], ht_hi[o].bitcast(F32), ALU.subtract).then_inc(S("ht_ready"), 1)

            if "w_up" in live:
                rms_before(2, 2)
                operand(2)
                split_loop(dve, "w_up", up_conv, me, unroll=True)
            if "w_down" in live:
                follow("w_down")
                rms_after(3, 3)

            def softmax(q, smx_, mask, column):
                for h in range(8):
                    dve.wait_ge(S("at_qk"), 8 * q + h + 1)
                    if q == 0:
                        for t, (c0, c1) in enumerate(((0, P), (P, SCW))):
                            i = STT(s_all[:, h, c0:c1], scr[:, h % 4, c0:c1], cq[:, t, h:h + 1], mask[:, c0:c1],
                                    ALU.add, ALU.add)
                    else:
                        i = TT(s_all[:, h, :], scr[:, h % 4, 0:SCW], mask[:], ALU.add)
                    i.then_inc(S("at_s"), 1)
                dve.drain()
                dve.reduce_max(smx_[:, 0, 0, :], s_all[:, :, 0:P], AX_X)
                dve.reduce_max(smx_[:, 0, 1, :], s_all[:, :, P:SCW], AX_X)
                dve.drain()
                if q:
                    s8 = sink[:, 8 * (q - 1):8 * q].unsqueeze(1).broadcast_to([P, NT, 8])
                    TT(smx_[:, 0], smx_[:, 0], s8, ALU.max)
                    dve.drain()
                    TT(smx_[:, 3], s8, smx_[:, 0], ALU.subtract)
                TS(smx_[:, 1], smx_[:, 0], -1.0, None, ALU.mult)
                dve.drain().then_inc(S("at_negm"), 1)
                for h in range(8):
                    dve.wait_ge(S("at_t"), 8 * q + h + 1)
                    dve.tensor_copy((pt if q == 0 else pt2)[:, h % 2, :], psum[:, h % 2, 0:SCW]).then_inc(S("at_pt"), 1)
                dve.wait_ge(S("at_sum"), q + 1)
                if q:
                    TT(smx_[:, 2], smx_[:, 2], smx_[:, 4], ALU.add)
                    dve.drain()
                dve.reciprocal(smx_[:, 5], smx_[:, 2])
                dve.drain()
                dve.wait_ge(S("at_o"), q + 1)
                for t in range(NT):
                    i = TT(y[:, t, column:column + 8 * DH].rearrange("p (h n) -> p h n", n=DH),
                           psum[:, 2 + t, :].rearrange("p (h n) -> p h n", n=DH),
                           smx_[:, 5, t, :].unsqueeze(2).broadcast_to([P, 8, DH]), ALU.mult)
                dve.drain().then_inc(S("at_y"), 1)

            if "ab_in" in live:
                dve.sem_inc(S("t_source"), 1)
                operand(3)
                follow("ab_in")
                dve.wait_ge(S("fbias_landed"), 16)
                TT(lf[:, 0, :, :], p1[:, :, AB_FA:AB_FA + N_AB], fbias[:].unsqueeze(1).broadcast_to([P, NT, N_AB]), ALU.add)
                dve.drain().then_inc(S("lf_pre"), 1)
                dve.wait_ge(S("lf_ln"), 1)
                STT(lf[:, 2, :, :], lf[:, 0, :, :], 0.0, lf[:, 1, :, :], ALU.min, ALU.subtract)
                dve.drain().then_inc(S("lf_ready"), 1)
                dve.wait_ge(S("ab_masks_ready"), 1)
                dve.wait_ge(S("lf_cum"), 1)
                dve.tensor_copy(cq[:], psum[:, 0, 0:NT * N_AB].rearrange("p (t h) -> p t h", h=N_AB))
                dve.tensor_copy(ct[0:N_AB, :], psum[0:N_AB, 1, 0:SEQ])
                dve.drain().then_inc(S("fox_cum_ready"), 1)
                softmax(0, smx, mask_fox, 0)
                for g in range(2):
                    dve.wait_ge(S("sb_ln"), g + 1)
                    z = scr[:, :, 0:SCW]
                    wide = lambda m: m[:].unsqueeze(1).broadcast_to([P, 4, SCW])
                    STT(sbb[:], z, 0.0, sba[:], ALU.max, ALU.add)
                    dve.drain()
                    TT(sbb[:], sbb[:], wide(keep_sb), ALU.mult)
                    dve.drain().then_inc(S("sb_sp"), 1)
                    dve.wait_ge(S("sb_exponent"), g + 1)
                    TT(sba[:], z, wide(mask_sb), ALU.add)
                    dve.drain().then_inc(S("sb_masked"), 1)
                dve.wait_ge(S("sb_o"), 1)
                for t in range(NT):
                    dve.tensor_copy(y[:, t, FOX_W:2 * FOX_W], psum[:, 2 + t, :])
                dve.drain()
                dve.sem_inc(S("t_source"), 1)
            if "ab_out" in live:
                operand(4)
                follow("ab_out")
                layer_norm(4, 4)

            def up_gated(blocks, r):
                (bg, cg, n0, n, _), (bv, cv, _, _, _) = blocks
                j, nc_ = n0 // NB, n // P
                round_to(cv + 2)
                round_to(cv + (cv - cg) + 2)
                wait_evacuated(dve, bg)
                wait_used(dve, cv + (cv - cg))
                if j:
                    dve.wait_ge(S("hn_t"), j)
                for t in range(NT):
                    i = TT(pg[:, t, 0:n], pv[:, t, 0:n], acc[bv % 2][t][:, 0:n], ALU.mult)
                i.then_inc(S(f"acc_free{bv % 2}"), 1)
                dve.drain().then_inc(S("hn_ready"), 1)
                q = 6 + j
                dve.wait_ge(S("ht_hi_ready"), q + 1)
                o = (slice(None), slice(4 * j, 4 * j + nc_))
                TT(ht_lo[o], scr[:, 0:-(-nc_ // 2), :].rearrange("p b (f n) -> p (b f) n", n=SEQ), ht_hi[o].bitcast(F32),
                   ALU.subtract).then_inc(S("ht_ready"), 1)

            if "ffn_up" in live:
                operand(5)
                split_loop(dve, "ffn_up", up_gated, me, unroll=True)
            if "ffn_down" in live:
                follow("ffn_down")
                layer_norm(5, 6)

            def ple(i, m, r=0):
                operand(m)
                dve.wait_ge(S("ppt_hi_ready"), i + 1)
                TT(ppt_lo[:], scr[:, 0, :].rearrange("p (k n) -> p k n", n=SEQ), ppt_hi[:].bitcast(F32), ALU.subtract)\
                    .then_inc(S("ppt_ready"), 1)
                for q in range(2):
                    (bg, cg, n0, _, _), (bp, cp, _, _, psp) = phase[f"ple{i}"][2 * q:2 * q + 2]
                    round_to(cp + 3, r)
                    wait_evacuated(dve, bg)
                    wait_used(dve, cp + 1, r)
                    for t in range(NT):
                        j = TT(sig[:, t, :], sig[:, t, :], acc[bp % 2][t], ALU.mult)
                    j.then_inc(S(f"acc_free{bp % 2}"), 1)
                    dve.drain()
                    TT(x[:, :, n0:n0 + NB], x[:, :, n0:n0 + NB], sig[:], ALU.add)
                    dve.drain().then_inc(S("ple_added"), 1)

            if "ple0" in live:
                ple(0, 6)
                dve.sem_inc(S("ple_x"), 1)
            if "qkv" in live:
                dve.sem_inc(S("t_source"), 1)
                operand(7)
                follow("qkv")
                dve.wait_ge(S("rope_landed"), 16)
                hd = p2[:, :, 0:SWA_V].rearrange("p t (h n) -> p t h n", n=DH)
                x1, x2 = hd[:, :, :, 0:ROPE_HALF], hd[:, :, :, ROPE_HALF:2 * ROPE_HALF]
                rt = [rtmp[:, k].rearrange("p t (h n) -> p t h n", n=ROPE_HALF) for k in range(4)]
                for t in range(NT):
                    cs = [rope[:, k, t, :].unsqueeze(1).broadcast_to([P, 18, ROPE_HALF]) for k in range(2)]
                    for k, (v, f) in enumerate(((x1, 0), (x2, 1), (x2, 0), (x1, 1))):
                        TT(rt[k][:, t], v[:, t], cs[f], ALU.mult)
                dve.drain()
                TT(x1, rt[0], rt[1], ALU.subtract)
                TT(x2, rt[2], rt[3], ALU.add)
                dve.drain()
                for u in range(2):
                    dve.tensor_copy(kdup[:, :, :, u, :], p2[:, :, SWA_K:SWA_V].rearrange("p t (g n) -> p t g n", n=DH))
                dve.drain().then_inc(S("rotated"), 1)
                dve.wait_ge(S("swa_mask_ready"), 1)
                dve.wait_ge(S("sink_landed"), 16)
                for g in range(2):
                    softmax(1 + g, smx2, mask_swa, g * 8 * DH)
                dve.sem_inc(S("t_source"), 1)
            if "c_out" in live:
                operand(8)
                follow("c_out")
                layer_norm(6, 8)

            def item(i):
                c0, r = N_BEFORE_MOE, i * R_ITEM

                def splits(k0, k1):
                    for k in range(k0, k1):
                        n = NB * MOE_DOWN[(k - MOE_UP_CHUNKS) % len(MOE_DOWN)] if k >= MOE_UP_CHUNKS else CHUNK
                        split_chunk(c0 + k, r, n)

                for t in range(NT):
                    dve.tensor_copy(cur[:, t:t + 1], slotc[:, bass.ds(i + t * ITEMS, 1)])
                    dve.tensor_copy(cur[:, 2 + t:3 + t], combc[:, bass.ds(i + t * ITEMS, 1)])
                dve.drain()
                for t in range(NT):
                    TS(sel[:, t, :], slot_row[:], cur[:, t:t + 1], None, ALU.is_equal)
                dve.drain().then_inc(S("sel_ready"), 1)
                splits(0, 2)
                dve.wait_ge(S("gathered"), 3 * i + 2)
                dve.tensor_copy(xg_lo[:], scr[:, 2:4, :].rearrange("p b (k n) -> p (b k) n", n=P)).then_inc(S("xg_ready"), 1)
                splits(2, 4)
                for j in range(MOE_PAIRS):
                    splits(4 * j + 4, 4 * j + 6)
                    if j:
                        lo_h(i, j - 1)
                    dve.wait_ge(S("mg_ready"), MOE_PAIRS * i + j + 1)
                    wait_used(dve, c0 + 4 * j + 4, r)
                    if j >= 2:
                        dve.wait_ge(S("mh_t"), MOE_PAIRS * i + j - 1)
                    TT(mh[:, j % 2, :], mg[:], psum[:, 2 * (j % 2) + 1, :], ALU.mult).then_inc(S("mh_ready"), 1)
                    splits(4 * j + 6, 4 * j + 8)
                lo_h(i, MOE_PAIRS - 1)
                k = 4 * MOE_PAIRS + 4
                for n in range(2):
                    end = MOE_UP_CHUNKS + len(MOE_DOWN) * (n + 1)
                    splits(k, min(end + 2, MOE_CHUNKS))
                    k = min(end + 2, MOE_CHUNKS)
                    dve.wait_ge(S("ys_hi_ready"), 2 * i + n + 1)
                    o = slice(n * NB, (n + 1) * NB)
                    STT(ys_lo[:, o], psum[:, 4 + n, :], gslot[:, 0:1], ys_hi[:, o].bitcast(F32), ALU.mult, ALU.subtract)\
                        .then_inc(S("ys_ready"), 1)
                for t in range(NT):
                    dve.wait_ge(S("scattered"), 2 * i + t + 1)
                    TT(y[:, t, :], y[:, t, :], psum[:, 2 * t:2 * t + 2, :].rearrange("p b n -> p (b n)"), ALU.add)
                dve.drain()

            def lo_h(i, j):
                dve.wait_ge(S("mh_hi_ready"), MOE_PAIRS * i + j + 1)
                TT(mh_lo[:, 4 * j:4 * j + 4, :], psum[:, 6 + j % 2, :].rearrange("p (k n) -> p k n", n=P),
                   mh_hi[:, 4 * j:4 * j + 4, :].bitcast(F32), ALU.subtract).then_inc(S("mh_split"), 1)

            tok = lambda c, w=N_EXP: route[:, c:c + NT * w].rearrange("p (t e) -> p t e", e=w)
            logits, top8, hot1, hot2, comb, selm, rank1 = (tok(16 * k) for k in range(7))
            top8 = tok(16)
            slotc, combc = route[:, 112:134], route[:, 148:170]
            gap, gap_e, g1, g2 = (route[:, c:c + 2] for c in (140, 142, 144, 146))
            row8 = lambda k: route[:, 170 + 8 * k:178 + 8 * k]
            cnt, over, over_before, pick, tmp8, eid8, one8 = (row8(k) for k in range(7))
            eidf = route[:, 226:230]
            cur = route[:, 230:234]
            idxf = route[:, 234:250].rearrange("p (t e) -> p t e", e=8)

            if "moe" in live:
                operand(9)
                dve.wait_ge(S("xn_hi_ready"), 1)
                TT(xn_lo[:], x[:], xn_hi[:].bitcast(F32), ALU.subtract)
                dve.memset(y[:], 0.0)
                dve.memset(one8, 1.0)
                dve.tensor_copy(eid8, slot_row[:, 0:N_EXP])
                dve.wait_ge(S("logits"), 1)
                dve.wait_ge(S("rb_landed"), 16)
                TT(logits, scr[:, 0, 0:NT * N_EXP].rearrange("p (t e) -> p t e", e=N_EXP),
                   rb_row[:].unsqueeze(1).broadcast_to([P, NT, N_EXP]), ALU.add)
                dve.drain()
                for t in range(NT):
                    dve.max(top8[:, t, :], logits[:, t, :])
                dve.drain()
                TT(gap.unsqueeze(2), top8[:, :, 1:2], top8[:, :, 0:1], ALU.subtract)
                for t in range(NT):
                    dve.max_index(route_u[:, t, :], top8[:, t, :], logits[:, t, :])
                dve.drain().then_inc(S("top_gap"), 1)
                dve.tensor_copy(idxf, route_u[:])
                dve.drain()
                for k, hot in ((0, hot1), (1, hot2)):
                    TT(hot, eid8.unsqueeze(1).broadcast_to([P, NT, N_EXP]), idxf[:, :, k:k + 1].broadcast_to([P, NT, N_EXP]),
                       ALU.is_equal)
                dve.drain()
                TT(selm, hot1, hot2, ALU.add)
                dve.drain().then_inc(S("chosen"), 1)
                dve.wait_ge(S("top_exp"), 1)
                TS(g2, gap_e, 1.0, None, ALU.add)
                dve.drain()
                dve.reciprocal(g1, g2)
                dve.drain()
                TT(g2, g1, gap_e, ALU.mult)
                dve.drain()
                for hot, g in ((hot1, g1), (hot2, g2)):
                    TT(hot, hot, g.unsqueeze(2).broadcast_to([P, NT, N_EXP]), ALU.mult)
                dve.drain()
                TT(comb, hot1, hot2, ALU.add)
                dve.wait_ge(S("ranks"), 1)
                TS(rank1, scr[:, 1, 0:NT * N_EXP].rearrange("p (t e) -> p t e", e=N_EXP), 1.0, None, ALU.add)
                dve.tensor_copy(cnt, scr[:, 1, 16:24])
                dve.drain()
                TT(rank1, rank1, selm, ALU.mult)
                TS(over, cnt, float(P), None, ALU.is_gt)
                dve.drain()
                dve.tensor_tensor_scan(over_before, one8, over, 0.0, ALU.mult, ALU.add)
                sc, cc_ = (v.rearrange("p (t i) -> p t i", i=ITEMS) for v in (slotc, combc))
                TS(sc[:, :, 0:N_EXP], rank1, -1.0, None, ALU.add)
                dve.tensor_copy(cc_[:, :, 0:N_EXP], comb)
                dve.drain()
                TT(over_before, over_before, over, ALU.subtract)
                dve.reduce_sum(eidf[:, 3:4], over, AX_X)
                dve.drain()
                TS(eidf[:, 3:4], eidf[:, 3:4], float(N_EXP), None, ALU.add)
                for k in range(ITEMS - N_EXP):
                    TS(pick, over_before, float(k), None, ALU.is_equal)
                    dve.drain()
                    TT(pick, pick, over, ALU.mult)
                    dve.drain()
                    TT(tmp8, pick, eid8, ALU.mult)
                    dve.drain()
                    dve.reduce_sum(eidf[:, k:k + 1], tmp8, AX_X)
                    for src, dst in ((rank1, sc), (comb, cc_)):
                        TT(hot1, src, pick.unsqueeze(1).broadcast_to([P, NT, N_EXP]), ALU.mult)
                        dve.drain()
                        dve.reduce_sum(dst[:, :, N_EXP + k], hot1, AX_X)
                        dve.drain()
                    TS(sc[:, :, N_EXP + k], sc[:, :, N_EXP + k], -1.0 - P, None, ALU.add)
                    dve.drain()
                dve.tensor_copy(route_i[:], eidf)
                dve.drain().then_inc(S("routed"), 1)
                n_items = dve.value_load(route_i[0:1, 3:4], min_val=N_EXP, max_val=ITEMS)
                with dve.Fori(0, ITEMS) as i:
                    with dve.If(i < n_items):
                        item(i)
                    dve.end_ifs()
                me.cap = N_STATIC
                dve.sem_inc(S("moe_x"), 1)
                layer_norm(7, 10)
            if "ple1" in live:
                r = n_items * R_ITEM
                round_to(me.chunk + 2, r)
                ple(1, 10, r)
            dve.drain()
            dve.sem_inc(S("x_done"), 1)

        @block.tensor
        def _(pe):
            pe.sem_inc(S("w_used"), RING)
            mm = pe.matmul

            def products(bl, r, hi, lo, r4=None, used=None):
                bb, cc, n0, n, ps = bl
                ra = 0 if r4 is not None else r
                rc = r if r4 is None else r4
                pe.wait_ge(S(f"acc_free{bb % 2}"), bb // 2 + 1 + ra)
                kmax = ps[-1][0] + ps[-1][1] - 1
                for i, (k0, nk, _) in enumerate(ps):
                    slot = (cc + i) % RING
                    pe.wait_ge(S("lo_ready"), RING + cc + i + 1 + RING * rc)
                    if used:
                        used(k0)
                    for kk in range(nk):
                        k = k0 + kk
                        wh = w_hi[:, slot, kk * n:(kk + 1) * n]
                        wl = w_lo[:, slot, kk * n:(kk + 1) * n]
                        for t in range(NT):
                            o = acc[bb % 2][t][:, 0:n]
                            mm(o, hi(k, t), wh, start=(k == 0), stop=False)
                            mm(o, hi(k, t), wl, start=False, stop=False)
                            m = mm(o, lo(k, t), wh, start=False, stop=(k == kmax))
                    m.then_inc(S("w_used"), 1)

            xh = lambda k, t: xt_hi[:, k, t * P:(t + 1) * P]
            xl = lambda k, t: xt_lo[:, k, t * P:(t + 1) * P]
            hh = lambda k, t: ht_hi[:, k, t * P:(t + 1) * P]
            hl = lambda k, t: ht_lo[:, k, t * P:(t + 1) * P]

            def turn(o, i):
                return pe.transpose(o, i, ident[:])

            def operand(m, src):
                pe.wait_ge(S("t_source"), m + 1)
                if m == 0:
                    pe.wait_ge(S("ident_ready"), 1)
                for t in range(NT):
                    for g in range(2):
                        for k in range(4):
                            i = turn(scr[:, 2 * t + g, k * P:(k + 1) * P], src[:, t, (4 * g + k) * P:(4 * g + k + 1) * P])
                        i.then_inc(S("t_ready"), 1)
                pe.wait_ge(S("xt_ready"), 4 * (m + 1))

            def project(name, hi, lo, used=None):
                split_loop(pe, name, lambda blocks, r: [products(b_, r, hi, lo, used=used) for b_ in blocks])

            operand(0, y)
            project("w_in", xh, xl)
            wait_evacuated(pe, 6)
            wait_evacuated(pe, 5)
            for t in range(NT):
                i = turn(scr[0:2 * RANK, 0, t * P:(t + 1) * P], p0[:, t, C_LR:C_LR + 2 * RANK])
            i.then_inc(S("lr_t"), 1)
            for f in range(4):
                for t in range(NT):
                    i = turn(scr[:, 1 + f // 2, (f % 2) * SEQ + t * P:(f % 2) * SEQ + (t + 1) * P],
                             p0[:, t, C_Q + f * P:C_Q + (f + 1) * P])
            i.then_inc(S("qk_t"), 1)
            pe.wait_ge(S("lrt_ready"), 1)
            pe.wait_ge(S("lrt_ones"), 1)
            pe.wait_ge(S("gate_w_landed"), 64)
            for t in range(NT):
                i = mm(psum[:, t, :], lrt[:, t * P:(t + 1) * P], gate_w[:], start=True, stop=True)
            i.then_inc(S("gate_pre"), 1)
            pe.wait_ge(S("logd_ready"), 1)
            pe.wait_ge(S("tri_ready"), 1)
            for g in range(4):
                for t in range(NT):
                    o = (g % 2) * SEQ + t * P
                    i = mm(psum[:, 2 + g // 2, o:o + P], logd[:, t, g * P:(g + 1) * P], (tri_fwd if g < 2 else tri_bwd)[:],
                           start=True, stop=True)
            i.then_inc(S("cum_t"), 1)
            pe.wait_ge(S("q_in"), 1)
            pe.wait_ge(S("k_in"), 1)
            for d in range(2):
                for h in range(GLA_HEADS):
                    lane = slice(HEAD_K * (h % 2), HEAD_K * (h % 2 + 1))
                    for t in range(NT):
                        o = ((h // 2) * NT + t) * P
                        i = mm(psum[:, 2 * d + h % 2, o:o + P], e2[lane, 2 * d + h // 2, t * P:(t + 1) * P],
                               e1[lane, 2 * d + h // 2, t * P:(t + 1) * P], start=True, stop=True)
                i.then_inc(S("gla_scores"), 1)
            pe.wait_ge(S("k_out"), 1)
            for t in range(NT):
                for g in range(4):
                    i = turn(scr[:, 3 * t, g * P:(g + 1) * P], e3[:, g, t * P:(t + 1) * P])
                i.then_inc(S("kout_t"), 1)
            pe.wait_ge(S("kout_ready"), 2)
            for g in range(4):
                for c_ in ((0, 1, 2) if g < 2 else (3, 2, 1)):
                    lane = slice(GLA_CHUNK * (c_ % 2), GLA_CHUNK * (c_ % 2 + 1))
                    for hp in range(2):
                        h = 2 * (g % 2) + hp
                        i = mm(kv_place(g, c_)[HEAD_K * hp:HEAD_K * (hp + 1), :],
                               kout[lane, c_ // 2, g * P + hp * HEAD_K:g * P + (hp + 1) * HEAD_K],
                               p0[lane, c_ // 2, C_V + h * HEAD_V:C_V + (h + 1) * HEAD_V], start=True, stop=True)
            i.then_inc(S("gla_kv"), 1)
            pe.wait_ge(S("st_ready"), 2)
            pe.wait_ge(S("q_half_ready"), 1)
            pe.wait_ge(S("state_ready"), 1)
            for t in range(NT):
                for h in range(GLA_HEADS):
                    o = psum[:, 2 * t + h % 2, (h // 2) * HEAD_V:(h // 2 + 1) * HEAD_V]
                    v = p0[:, t, C_V + h * HEAD_V:C_V + (h + 1) * HEAD_V]
                    lane = slice(HEAD_K * (h % 2), HEAD_K * (h % 2 + 1))
                    parts = [(st[:, d, h % 2, (h // 2) * NT + t, :], v) for d in range(2)]
                    for c_ in (2 * t, 2 * t + 1):
                        for d in range(2):
                            if c_ != (0 if d == 0 else 3):
                                g = 2 * d + h // 2
                                parts.append((q_half[lane, c_ % 2, g, t * P:(t + 1) * P], state[lane, g, c_, :]))
                    for k, (l, r_) in enumerate(parts):
                        i = mm(o, l, r_, start=(k == 0), stop=(k == len(parts) - 1))
                i.then_inc(S("gla_o"), 1)
            operand(1, y)
            project("w_out", xh, xl)

            def up_conv(blocks, r):
                b0 = phase["w_up"][0][0]
                for b_ in blocks:
                    products(b_, r, xh, xl)
                j = (blocks[0][0] - b0) // 2
                n = blocks[0][3]
                pe.wait_ge(S("scr_free"), j + 1 + r)
                for h, src in ((0, pg), (1, pv)):
                    wait_evacuated(pe, blocks[h][0], r)
                    for k in range(n // P):
                        for t in range(NT):
                            o = (k % 2) * SEQ + t * P
                            i = turn(scr[:, 2 * h + k // 2, o:o + P], src[:, t, k * P:(k + 1) * P])
                    i.then_inc(S("conv_t"), 1)

            if "w_up" in live:
                pe.sem_inc(S("scr_free"), 1)
                operand(2, y)
                split_loop(pe, "w_up", up_conv)
            if "w_down" in live:
                project("w_down", hh, hl, lambda k0: pe.wait_ge(S("ht_ready"), k0 // 4 + 1))

            def attend(q, queries, keys, values, pt_):
                def pv(h):
                    pe.wait_ge(S("at_pt"), 8 * q + h + 1)
                    o = slice(h * DH, (h + 1) * DH)
                    mm(psum[:, 2, o], pt_[:, h % 2, 0:P], values(h, 0), start=True, stop=True)
                    mm(psum[:, 3, o], pt_[:, h % 2, P:SEQ], values(h, 0), start=True, stop=False)
                    return mm(psum[:, 3, o], pt_[:, h % 2, SEQ:SCW], values(h, 1), start=False, stop=True)

                for h in range(8):
                    if q or h >= 4:
                        pe.wait_ge(S("at_s"), 8 * q + h - 3 if h >= 4 else 8 * q)
                    b_ = scr[:, h % 4, :]
                    for t, (c0, c1) in enumerate(((0, P), (P, SCW))):
                        i = mm(b_[:, c0:c1], queries(h)[:, t * P:(t + 1) * P], keys(h)[:, 0:c1 - c0], start=True, stop=(q > 0))
                        if q == 0:
                            i = mm(b_[:, c0:c1], neg_head[:, h, :], ct[:, 0:c1 - c0], start=False, stop=True)
                    i.then_inc(S("at_qk"), 1)
                if q:
                    pe.wait_ge(S("at_y"), q)
                for h in range(8):
                    pe.wait_ge(S("at_p"), 8 * q + h + 1)
                    if h >= 2:
                        pe.wait_ge(S("at_pt"), 8 * q + h - 1)
                    for k in range(3):
                        i = turn(psum[:, h % 2, k * P:(k + 1) * P], s_all[:, h, k * P:(k + 1) * P])
                    i.then_inc(S("at_t"), 1)
                    if h:
                        pv(h - 1)
                pv(7).then_inc(S("at_o"), 1)

            if "ab_in" in live:
                operand(3, x)
                project("ab_in", xh, xl)
                wait_phase_evacuated(pe, "ab_in")
                pe.wait_ge(S("lf_ready"), 1)
                l0, l1 = lf[:, 2, 0, :], lf[:, 2, 1, :]
                mm(psum[:, 0, 0:N_AB], tri_incl[:], l0, start=True, stop=True)
                mm(psum[:, 0, N_AB:2 * N_AB], ones[:], l0, start=True, stop=False)
                mm(psum[:, 0, N_AB:2 * N_AB], tri_incl[:], l1, start=False, stop=True)
                mm(psum[0:N_AB, 1, 0:P], l0, tri_incl[:], start=True, stop=True)
                mm(psum[0:N_AB, 1, P:SEQ], l0, ones[:], start=True, stop=False)
                mm(psum[0:N_AB, 1, P:SEQ], l1, tri_incl[:], start=False, stop=True).then_inc(S("lf_cum"), 1)

                def turn_qk(g, cq_, ck_):
                    for tile in range(4):
                        for f in range(2):
                            for t in range(NT):
                                c_ = (cq_ if tile < 2 else ck_) + (2 * (tile % 2) + f) * P
                                i = turn(scr[:, tile, f * SEQ + t * P:f * SEQ + (t + 1) * P], p1[:, t, c_:c_ + P])
                        i.then_inc(S("ab_t"), 1)
                    pe.wait_ge(S("qk1_ready"), 4 * (g + 1))

                def qh(h):
                    return qk1[DH * (h % 2):DH * (h % 2 + 1), h // 2, :]

                def kh(h):
                    return qk1[DH * (h % 2):DH * (h % 2 + 1), 4 + h // 2, :]

                turn_qk(0, AB_QA, AB_KA)
                pe.wait_ge(S("fox_cum_ready"), 1)
                attend(0, qh, kh, lambda h, t: p1[:, t, AB_VA + h * DH:AB_VA + (h + 1) * DH], pt)
                pe.wait_ge(S("at_s"), 8)
                turn_qk(1, AB_QS, AB_KS)
                pe.wait_ge(S("at_y"), 1)
                for g in range(2):
                    if g:
                        pe.wait_ge(S("sb_masked"), g)
                    for u in range(4):
                        h = 4 * g + u
                        mm(scr[:, u, 0:SEQ], kh(h)[:, 0:P], qh(h), start=True, stop=True)
                        i = mm(scr[:, u, SEQ:SCW], kh(h)[:, P:SEQ], qh(h)[:, P:SEQ], start=True, stop=True)
                    i.then_inc(S("sb_z"), 1)
                    pe.wait_ge(S("sb_sp"), g + 1)
                    for u in range(4):
                        s0, s1 = sbb[:, u, 0:SEQ], sbb[:, u, SEQ:SCW]
                        h = 4 * g + u
                        mm(scr[:, u, 0:SEQ], kh(h)[:, 0:P], qh(h), start=True, stop=False)
                        mm(scr[:, u, P:SEQ], neg_ones[:], s1, start=False, stop=False, skip_group_check=True)
                        mm(scr[:, u, 0:SEQ], neg_from[:], s0, start=False, stop=True)
                        mm(scr[:, u, SEQ:SCW], kh(h)[:, P:SEQ], qh(h)[:, P:SEQ], start=True, stop=False)
                        i = mm(scr[:, u, SEQ:SCW], neg_from[:], s1, start=False, stop=True)
                    i.then_inc(S("sb_exponent"), 1)
                    pe.wait_ge(S("sb_a"), g + 1)
                    for u in range(4):
                        h = 4 * g + u
                        o = slice(h * DH, (h + 1) * DH)
                        v = lambda t: p1[:, t, AB_VS + h * DH:AB_VS + (h + 1) * DH]
                        mm(psum[:, 2, o], sba[:, u, 0:P], v(0), start=True, stop=True)
                        mm(psum[:, 3, o], sba[:, u, P:SEQ], v(0), start=True, stop=False)
                        i = mm(psum[:, 3, o], sba[:, u, SEQ:SCW], v(1), start=False, stop=True)
                i.then_inc(S("sb_o"), 1)
            if "ab_out" in live:
                operand(4, y)
                project("ab_out", xh, xl)

            def up_gated(blocks, r):
                b0 = phase["ffn_up"][0][0]
                for b_ in blocks:
                    products(b_, r, xh, xl)
                j = (blocks[0][0] - b0) // 2
                n = blocks[0][3]
                pe.wait_ge(S("ht_ready"), 6 + j + r)
                pe.wait_ge(S("hn_ready"), j + 1 + r)
                for k in range(n // P):
                    for t in range(NT):
                        o = (k % 2) * SEQ + t * P
                        i = turn(scr[:, k // 2, o:o + P], pg[:, t, k * P:(k + 1) * P])
                i.then_inc(S("hn_t"), 1)

            if "ffn_up" in live:
                operand(5, x)
                split_loop(pe, "ffn_up", up_gated)
            if "ffn_down" in live:
                project("ffn_down", hh, hl, lambda k0: pe.wait_ge(S("ht_ready"), 6 + k0 // 4 + 1))

            def ple(i, m, r=0):
                operand(m, x)
                pe.wait_ge(S("p_landed"), 16 * (i + 1))
                for k in range(2):
                    for t in range(NT):
                        j = turn(scr[:, 0, k * SEQ + t * P:k * SEQ + (t + 1) * P], pn[:, t, k * P:(k + 1) * P])
                j.then_inc(S("p_t"), 1)
                for q in range(4):
                    if q == 1:
                        pe.wait_ge(S("ppt_ready"), i + 1)
                    hi, lo = (xh, xl) if q % 2 == 0 else (lambda k, t: ppt_hi[:, k, t * P:(t + 1) * P],
                                                         lambda k, t: ppt_lo[:, k, t * P:(t + 1) * P])
                    products(phase[f"ple{i}"][q], 0, hi, lo, r4=r)

            if "ple0" in live:
                ple(0, 6)
            if "qkv" in live:
                operand(7, x)
                project("qkv", xh, xl)
                pe.wait_ge(S("rotated"), 1)
                for j in range(3):
                    if j == 2:
                        pe.wait_ge(S("qk2_ready"), 1)
                    for f in range(4 if j < 2 else 2):
                        for t in range(NT):
                            src = p2[:, t, (4 * j + f) * P:(4 * j + f + 1) * P] if j < 2 else \
                                kdup[:, t, f, :, :].rearrange("p u n -> p (u n)")
                            o = (f % 2) * SEQ + t * P
                            i = turn(scr[:, (2 * j if j < 2 else 0) + f // 2, o:o + P], src)
                    i.then_inc(S("swa_t"), 1)
                pe.wait_ge(S("qk2_ready"), 3)
                for g in range(2):
                    lane = lambda h: slice(DH * (h % 2), DH * (h % 2 + 1))
                    attend(1 + g, lambda h: qk2[lane(h), 4 * g + h // 2, :], lambda h: qk2[lane(h), 8 + g, :],
                           lambda h, t: p2[:, t, SWA_V + g * DH:SWA_V + (g + 1) * DH], pt2)
            if "c_out" in live:
                operand(8, y)
                project("c_out", xh, xl)

            def item(i):
                c0, r = N_BEFORE_MOE, i * R_ITEM
                pe.wait_ge(S("sel_ready"), i + 1)
                for part, b0 in ((xn_hi, 4), (xn_lo, 6)):
                    for k in range(KD):
                        for t in range(NT):
                            m = mm(psum[:, b0 + k // 4, (k % 4) * P:(k % 4 + 1) * P], part[:, t, k * P:(k + 1) * P],
                                   sel[:, t, :], start=(t == 0), stop=(t == NT - 1))
                    m.then_inc(S("gathered"), 1)
                for t in range(NT):
                    turn(psum[:, 2, t * P:(t + 1) * P], sel[:, t, :].bitcast(F32))
                for t in range(NT):
                    m = mm(psum[:, 2, SEQ:SEQ + 1], sel[:, t, :].bitcast(F32), cur_pe[:, t:t + 1], start=(t == 0), stop=(t == NT - 1))
                m.then_inc(S("gathered"), 1)
                pe.wait_ge(S("xg_ready"), i + 1)
                pe.wait_ge(S("xg_hi_ready"), i + 1)
                pe.wait_ge(S("selt_ready"), i + 1)

                def chunk(k, o, hi, lo, k0, nk, first, last):
                    pe.wait_ge(S("lo_ready"), RING + c0 + k + 1 + RING * r)
                    slot = (c0 + k) % RING
                    for kk in range(nk):
                        wh, wl = (w[:, slot, kk * NB:(kk + 1) * NB] for w in (w_hi, w_lo))
                        q = k0 + kk
                        mm(o, hi[:, q, :], wh, start=(q == first), stop=False)
                        mm(o, hi[:, q, :], wl, start=False, stop=False)
                        m = mm(o, lo[:, q, :], wh, start=False, stop=(q == last))
                    m.then_inc(S("w_used"), 1)

                def turn_h(j):
                    pe.wait_ge(S("mh_ready"), MOE_PAIRS * i + j + 1)
                    if j >= 2:
                        pe.wait_ge(S("mh_split"), MOE_PAIRS * i + j - 1)
                    for k in range(4):
                        m = turn(psum[:, 6 + j % 2, k * P:(k + 1) * P], mh[:, j % 2, k * P:(k + 1) * P])
                    m.then_inc(S("mh_t"), 1)

                for j in range(MOE_PAIRS):
                    if j >= 2:
                        pe.wait_ge(S("mh_ready"), MOE_PAIRS * i + j - 1)
                    for h in range(2):
                        for u in range(2):
                            chunk(4 * j + 2 * h + u, psum[:, 2 * (j % 2) + h, :], xg_hi, xg_lo, 4 * u, 4, 0, KD - 1)
                        if h == 0 and j:
                            turn_h(j - 1)
                turn_h(MOE_PAIRS - 1)
                k = MOE_UP_CHUNKS
                for n in range(2):
                    k0 = 0
                    for nk in MOE_DOWN:
                        pe.wait_ge(S("mh_split"), MOE_PAIRS * i + k0 // 4 + 1)
                        chunk(k, psum[:, 4 + n, :], mh_hi, mh_lo, k0, nk, 0, KE - 1)
                        k, k0 = k + 1, k0 + nk
                pe.wait_ge(S("ys_ready"), 2 * i + 2)
                for t in range(NT):
                    for n in range(2):
                        for q, part in enumerate((ys_hi, ys_lo)):
                            m = mm(psum[:, 2 * t + n, :], selt[:, t * P:(t + 1) * P], part[:, n * NB:(n + 1) * NB],
                                   start=(q == 0), stop=(q == 1))
                    m.then_inc(S("scattered"), 1)

            cur_pe = route[:, 232:234]
            if "moe" in live:
                operand(9, x)
                pe.wait_ge(S("rw_landed"), 16)
                for t in range(NT):
                    for k in range(KD):
                        for q, part in enumerate((xt_hi, xt_lo)):
                            m = mm(scr[:, 0, t * N_EXP:(t + 1) * N_EXP], part[:, k, t * P:(t + 1) * P].bitcast(F32), rw[:, k, :],
                                   start=(k == 0 and q == 0), stop=(k == KD - 1 and q == 1))
                m.then_inc(S("logits"), 1)
                pe.wait_ge(S("chosen"), 1)
                sm = lambda t: route[:, 80 + 8 * t:88 + 8 * t]
                mm(scr[:, 1, 0:8], tri_excl[:], sm(0), start=True, stop=True)
                mm(scr[:, 1, 8:16], ones[:], sm(0), start=True, stop=False)
                mm(scr[:, 1, 8:16], tri_excl[:], sm(1), start=False, stop=True)
                mm(scr[:, 1, 16:24], ones[:], sm(0), start=True, stop=False)
                mm(scr[:, 1, 16:24], ones[:], sm(1), start=False, stop=True).then_inc(S("ranks"), 1)
                pe.wait_ge(S("routed"), 1)
                n_items = pe.value_load(route_i[0:1, 3:4], min_val=N_EXP, max_val=ITEMS)
                with pe.Fori(0, ITEMS) as i:
                    with pe.If(i < n_items):
                        item(i)
                    pe.end_ifs()
            if "ple1" in live:
                ple(1, 10, n_items * R_ITEM)


_INS = ["x", "norm_mix_pre", "norm_mix_post", "norm_ffn_pre", "norm_ffn_post", "w_in", "conv_a", "gate_up_fwd",
        "gate_bias_fwd", "gate_up_bwd", "gate_bias_bwd", "gla_head_norm", "w_out", "w_up", "conv_ffn", "w_down",
        "p_2", "ln_mix_g_2", "ln_mix_b_2", "ln_ffn_g_2", "ln_ffn_b_2", "ab_w_in_2", "ab_b_f_2", "ab_w_out_2",
        "c_w_qkv_2", "c_sinks_2", "c_w_out_2", "ffn_w_gate_up_2", "ffn_w_down_2", "router_w_2", "router_b_2",
        "moe_w_gate_up_2", "moe_w_down_2", "ple_w_gate_2", "ple_w_proj_2"]
UPTO = "end"


def kernel(**inputs):
    import numpy as np
    import concourse.bacc as bacc
    from concourse.bass_utils import run_bass_kernel_spmd as run

    nc = bacc.Bacc("TRN2", target_bir_lowering=False, num_devices=1)
    arrays, args = {}, {}
    for name in _INS:
        arr = np.ascontiguousarray(inputs[name])
        arrays[f"in_{name}"] = arr
        args[name] = nc.dram_tensor(f"in_{name}", arr.shape, mybir.dt.from_np(arr.dtype), kind="ExternalInput").ap()
    inv = np.float32(500000.0) ** (-np.arange(ROPE_HALF, dtype=np.float32) * np.float32(2.0) / np.float32(16.0))
    ang = np.arange(SEQ, dtype=np.float32)[:, None] * inv[None, :].astype(np.float32)
    arrays["in_rope"] = np.stack([np.cos(ang), np.sin(ang)]).astype(np.float32)
    args["rope"] = nc.dram_tensor("in_rope", (2, SEQ, ROPE_HALF), F32, kind="ExternalInput").ap()
    out = nc.dram_tensor("out", (1, SEQ, D), F32, kind="ExternalOutput").ap()
    build(nc, args, out, UPTO)
    r = run(nc, [arrays], core_ids=[0])
    return r.results[0]["out"]
```

```python
from contextlib import ExitStack

import concourse.bass as bass
from concourse import mybir

ALU = mybir.AluOpType
ACT = mybir.ActivationFunctionType
F32 = mybir.dt.float32
F32R = mybir.dt.float32r
I32 = mybir.dt.int32
U32 = mybir.dt.uint32
AX_X = mybir.AxisListType.X

P = 128
SEQ, D = 256, 1024
NT = SEQ // P
KD = D // P
NB = 512
RING = 4
CHUNK = 2048

D_HALF = 512
GLA_HEADS, HEAD_K, HEAD_V, GLA_CHUNK, RANK = 4, 64, 128, 64, 16
N_GK = GLA_HEADS * HEAD_K
C_GB, C_GC, C_GV, C_Q, C_K, C_V, C_GO, C_LR = 0, 512, 1024, 1536, 1792, 2048, 2560, 3072
D_IN = 3104
D_FF = 2816
KF = D_FF // P
KP = -(-D_FF // 512)
RMS_EPS, LN_EPS = 1e-6, 1e-5
DH = 64
N_AB = 8
FOX_W = N_AB * DH
AB_IN = 6 * FOX_W + N_AB
AB_QA, AB_KA, AB_VA, AB_FA = 0, FOX_W, 2 * FOX_W, 3 * FOX_W
AB_QS, AB_KS, AB_VS = 3 * FOX_W + N_AB, 4 * FOX_W + N_AB, 5 * FOX_W + N_AB
N_SWA, N_KV = 16, 2
SWA_IN = (N_SWA + 2 * N_KV) * DH
SWA_K, SWA_V = N_SWA * DH, (N_SWA + N_KV) * DH
ROPE_HALF = 8
N_EXP, D_EXP, D_PLE = 8, 3584, 256
KE = D_EXP // P
ITEMS = N_EXP + 3
ALPHA = 4.0 ** 0.25
SCW = 3 * P
NEG = -1.0e30
DECAY = 1.0 / 16.0


N_STREAM = ["w_in", "w_out", "w_up", "w_down", "ab_in", "ab_out", "ffn_up", "ffn_down", "ple0", "qkv", "c_out",
            "moe", "ple1"]


def weight_plan(w):

    def wide(m, k, n0, n):
        step = min(k, CHUNK // n) if n < NB else CHUNK // NB
        return (n0, n, [(k0, min(step, k - k0), m) for k0 in range(0, k, step)])

    def project(m, k, n):
        return [wide(m, k, n0, min(NB, n - n0)) for n0 in range(0, n, NB)]

    def gated(m):
        out = []
        for n0 in range(0, D_FF, NB):
            n = min(NB, D_FF - n0)
            out += [wide(m, KD, n0, n), wide(m, KD, D_FF + n0, n)]
        return out

    def ple(i):
        out = []
        for n0 in range(0, D, NB):
            out += [wide(w["ple_gate"][i], KD, n0, NB), wide(w["ple_proj"][i], D_PLE // P, n0, NB)]
        return out

    return [
        ("w_in", project(w["w_in"], KD, D_IN)), ("w_out", project(w["w_out"], KD, D)),
        ("w_up", gated(w["w_up"])), ("w_down", project(w["w_down"], KF, D)),
        ("ab_in", project(w["ab_in"], KD, AB_IN)), ("ab_out", project(w["ab_out"], KD, D)),
        ("ffn_up", gated(w["ffn_up"])), ("ffn_down", project(w["ffn_down"], KF, D)),
        ("ple0", ple(0)),
        ("qkv", project(w["qkv"], KD, SWA_IN)), ("c_out", project(w["c_out"], KD, D)),
        ("moe", []), ("ple1", ple(1)),
    ]


MOE_PAIRS = D_EXP // NB
MOE_DOWN = [4] * 6 + [2, 2]
MOE_UP_CHUNKS = MOE_PAIRS * 4
MOE_CHUNKS = MOE_UP_CHUNKS + 2 * len(MOE_DOWN)


def build(nc, a, out, upto="end"):
    weights = dict(
        w_in=a["w_in"][0], w_out=a["w_out"][0], w_up=a["w_up"][0], w_down=a["w_down"][0],
        ab_in=a["ab_w_in_2"][0], ab_out=a["ab_w_out_2"][0], ffn_up=a["ffn_w_gate_up_2"][0],
        ffn_down=a["ffn_w_down_2"][0], qkv=a["c_w_qkv_2"][0], c_out=a["c_w_out_2"][0],
        ple_gate=[a["ple_w_gate_2"][0], a["ple_w_gate_2"][1]],
        ple_proj=[a["ple_w_proj_2"][0], a["ple_w_proj_2"][1]],
    )
    moe_up, moe_down = a["moe_w_gate_up_2"][0], a["moe_w_down_2"][0]
    stop = len(N_STREAM) if upto == "end" else N_STREAM.index(upto) + 1
    plan = weight_plan(weights)[:stop]
    live = set(N_STREAM[:stop])

    phase, chunk0 = {}, {}
    c = b = 0
    for name, blocks in plan:
        phase[name], chunk0[name] = [], c
        for n0, n, pieces in blocks:
            phase[name].append((b, c, n0, n, pieces))
            b, c = b + 1, c + len(pieces)
    N_STATIC = c
    width = {cc + i: n * nk for bl in phase.values() for _, cc, _, n, ps in bl for i, (_, nk, _) in enumerate(ps)}
    LOOPS = {"w_in": (3, 2 * NB), "ab_in": (3, 2 * NB), "w_up": (5, NB), "ffn_up": (5, NB)}

    with ExitStack() as ctx:
        free = [-(-nc.sbuf_base // 64) * 64]
        TOP = 229344

        def nbytes(shape):
            n = 4
            for s in shape[1:]:
                n *= s
            return -(-n // 32) * 32

        def at(name, shape, dt, offset):
            assert offset + nbytes(shape) <= TOP, (name, offset + nbytes(shape), TOP)
            return nc.alloc_sbuf_tensor_at(name, shape, dt, offset=offset)

        def sb(name, shape, dt=F32):
            t = at(name, shape, dt, free[0])
            free[0] += nbytes(shape)
            return t

        def layout(first, *specs):
            made = []
            for name, shape, dt in specs:
                made.append(at(name, shape, dt, first))
                first += nbytes(shape)
            return made

        sems = {}

        def S(name):
            if name not in sems:
                sems[name] = ctx.enter_context(nc.semaphore(name))
            return sems[name]

        w_raw = sb("w_raw", [P, RING, CHUNK])
        w_hi = sb("w_hi", [P, RING, CHUNK], F32R)
        w_lo = sb("w_lo", [P, RING, CHUNK], F32R)
        x = sb("x", [P, NT, D])
        y = sb("y", [P, NT, D])
        gain = sb("gain", [P, 2, D])
        ident = sb("ident", [P, P])
        ones = sb("ones", [P, P])
        tri_incl = sb("tri_incl", [P, P])
        tri_excl = sb("tri_excl", [P, P])
        neg_from = sb("neg_from", [P, P])
        neg_ones = sb("neg_ones", [P, P])
        tri_fwd = sb("tri_fwd", [P, P])
        tri_bwd = sb("tri_bwd", [P, P])
        slot_row = sb("slot_row", [P, P])
        head_gain = sb("head_gain", [P, HEAD_V])
        rb_row = sb("rb_row", [P, N_EXP])
        stat = sb("stat", [P, 16])
        bn = sb("bn", [P, NT, 2, 6])
        route = sb("route", [P, 256])
        route_u = sb("route_u", [P, NT, 8], U32)
        route_i = sb("route_i", [P, 4], I32)
        at_xt = free[0]
        at_phase = at_xt + 2 * nbytes([P, KD, SEQ])

        xt_hi, xt_lo = layout(at_xt, ("xt_hi", [P, KD, SEQ], F32R), ("xt_lo", [P, KD, SEQ], F32R))
        (junk,) = layout(at_xt, ("junk", [P, NT, D], F32))

        (p0, logd, tmp0, cum, e1, e2, e3, qk0, conv_w, gate_w, dec, ss8) = layout(
            at_phase, ("p0", [P, NT, D_IN], F32), ("logd", [P, NT, NB], F32), ("tmp0", [P, NT, NB], F32),
            ("cum", [P, 4, SEQ], F32), ("e1", [P, 4, SEQ], F32), ("e2", [P, 4, SEQ], F32),
            ("e3", [P, 4, SEQ], F32), ("qk0", [P, 4, SEQ], F32), ("conv_w", [P, 3, D_HALF], F32),
            ("gate_w", [2 * RANK + 1, 2 * N_GK], F32), ("dec", [P, 4, 4], F32), ("ss8", [P, 3, 8], F32))
        o_logd = at_phase + nbytes([P, NT, D_IN])
        (kout, st, lrt) = layout(
            o_logd, ("kout", [P, NT, NB], F32),
            ("st", [P, 2, 2, 2 * NT, P], F32),
            ("lrt", [2 * RANK + 1, SEQ], F32))
        (state, q_half) = layout(
            at_xt, ("state", [P, 4, 4, HEAD_V], F32), ("q_half", [P, 2, 4, SEQ], F32))
        (ht_hi, ht_lo, ug, uv, cw, cw_rows) = layout(
            at_phase, ("ht_hi", [P, KF, SEQ], F32R), ("ht_lo", [P, KF, SEQ], F32R), ("ug", [P, 4, SEQ], F32),
            ("uv", [P, 4, SEQ], F32), ("cw", [P, 3, 2 * KF], F32), ("cw_rows", [2 * KF, 3, P], F32))
        (p1, qk1, pt, sba, mask_fox, neg_head, ct, fbias, lf, cq, smx, mask_sb, keep_sb) = layout(
            at_phase, ("p1", [P, NT, AB_IN], F32), ("qk1", [P, 8, SEQ], F32), ("pt", [P, 2, SCW], F32),
            ("sba", [P, 4, SCW], F32), ("mask_fox", [P, SCW], F32), ("neg_head", [P, N_AB, P], F32),
            ("ct", [P, SEQ], F32), ("fbias", [P, N_AB], F32), ("lf", [P, 3, NT, N_AB], F32),
            ("cq", [P, NT, N_AB], F32), ("smx", [P, 6, NT, N_AB], F32), ("mask_sb", [P, SCW], F32),
            ("keep_sb", [P, SCW], F32))
        (s_all,) = layout(at_xt, ("s_all", [P, N_AB, SCW], F32))
        (sbb,) = layout(at_xt, ("sbb", [P, 4, SCW], F32))
        (p2, qk2, pt2, mask_swa, kdup, rope, rtmp, smx2, sink) = layout(
            at_phase, ("p2", [P, NT, SWA_IN], F32), ("qk2", [P, 10, SEQ], F32), ("pt2", [P, 2, SCW], F32),
            ("mask_swa", [P, SCW], F32), ("kdup", [P, NT, N_KV, 2, DH], F32),
            ("rope", [P, 2, NT, ROPE_HALF], F32), ("rtmp", [P, 4, NT, 18 * ROPE_HALF], F32),
            ("smx2", [P, 6, NT, 8], F32), ("sink", [P, N_SWA], F32))
        (pn, ppt_hi, ppt_lo, sig) = layout(
            at_phase, ("pn", [P, NT, D_PLE], F32), ("ppt_hi", [P, 2, SEQ], F32R), ("ppt_lo", [P, 2, SEQ], F32R),
            ("sig", [P, NT, NB], F32))
        (xn_hi, xn_lo, xg_hi, xg_lo, mh_hi, mh_lo, mg, mh, rw) = layout(
            at_phase, ("xn_hi", [P, NT, D], F32R), ("xn_lo", [P, NT, D], F32R), ("xg_hi", [P, KD, P], F32R),
            ("xg_lo", [P, KD, P], F32R), ("mh_hi", [P, KE, P], F32R), ("mh_lo", [P, KE, P], F32R),
            ("mg", [P, NB], F32), ("mh", [P, 2, NB], F32), ("rw", [P, KD, N_EXP], F32))
        (ys_hi, ys_lo, sel, selt, gslot) = layout(
            at_xt, ("ys_hi", [P, D], F32R), ("ys_lo", [P, D], F32R), ("sel", [P, NT, P], F32R),
            ("selt", [P, SEQ], F32R), ("gslot", [P, 1], F32))

        psum = ctx.enter_context(nc.psum_tensor("psum", [P, 8, NB], F32))
        acc = [[psum[:, 2 * s + t, :] for t in range(NT)] for s in range(2)]
        scr = psum[:, 4:8, :]

        def acc_t(s, c_):
            return psum[:, 2 * s + c_ // 2, (c_ % 2) * SEQ:(c_ % 2 + 1) * SEQ]

        def acc_tall(s, nc_):
            return psum[:, 2 * s:2 * s + -(-nc_ // 2), :].rearrange("p b (f n) -> p (b f) n", n=SEQ)

        N_BEFORE_MOE = chunk0.get("moe", N_STATIC)
        R_ITEM = MOE_CHUNKS // RING

        def item_width(k):
            down = MOE_UP_CHUNKS <= k < MOE_CHUNKS
            return NB * MOE_DOWN[(k - MOE_UP_CHUNKS) % len(MOE_DOWN)] if down else CHUNK

        block = ctx.enter_context(nc.Block())

        class Place:
            chunk, cap, looping = 0, N_BEFORE_MOE, False

        def split_loop(eng, name, body, me=None, unroll=False):
            bl = phase[name]
            if name in LOOPS and not unroll:
                trips, _ = LOOPS[name]
                with eng.Fori(0, trips) as i:
                    if me:
                        me.looping, before = True, me.chunk
                    body(bl[0:2], i)
                if me:
                    assert me.chunk == before + RING
                    me.looping, me.chunk = False, before + RING * trips
                bl = bl[2 * trips:]
            for i in range(0, len(bl), 2):
                body(bl[i:i + 2], 0)

        def ncol(name, n0, r):
            return n0 if isinstance(r, int) else r * LOOPS[name][1] + n0

        def sl(n0, n):
            return slice(n0, n0 + n) if isinstance(n0, int) else bass.ds(n0, n)

        def wait_used(eng, c, r=0):
            eng.wait_ge(S("w_used"), RING + c + RING * r)

        def wait_evacuated(eng, bb, r=0):
            eng.wait_ge(S(f"acc_free{bb % 2}"), bb // 2 + 2 + r)

        def last_block(name):
            return phase[name][-1][0]

        def wait_phase_evacuated(eng, name):
            wait_evacuated(eng, last_block(name))
            wait_evacuated(eng, last_block(name) - 1)

        def end_chunk(name):
            _, cc, _, _, ps = phase[name][-1]
            return cc + len(ps)

        @block.sync
        def _(sp):
            for t in range(NT):
                sp.dma_start(x[:, t, :], a["x"][0, t * P:(t + 1) * P, :]).then_inc(S(f"x_landed{t}"), 16)

            def load(k, r, src, nk, n):
                sp.wait_ge(S("lo_ready"), k + 1 + RING * r)
                sp.dma_start(w_raw[:, k % RING, 0:nk * n].rearrange("p (k n) -> p k n", n=n), src)\
                  .then_inc(S(f"w_landed{k % RING}"), 16)

            def loads(name, r0=0):
                def body(blocks, r):
                    for _, cc, n0, n, ps in blocks:
                        for i, (k0, nk, m) in enumerate(ps):
                            load(cc + i, r + r0, m[k0 * P:(k0 + nk) * P, sl(ncol(name, n0, r), n)]
                                 .rearrange("(k p) n -> p k n", p=P), nk, n)
                split_loop(sp, name, body)

            for name in N_STREAM[:min(stop, 11)]:
                loads(name)
            if "moe" in live:
                def expert(e, r):
                    k = N_BEFORE_MOE
                    for j in range(MOE_PAIRS):
                        for n0 in (j * NB, D_EXP + j * NB):
                            for k0 in (0, 4):
                                load(k, r, moe_up[bass.ds(e, 1), k0 * P:(k0 + 4) * P, n0:n0 + NB]
                                     .rearrange("e (k p) n -> p (e k) n", p=P), 4, NB)
                                k += 1
                    for n0 in (0, NB):
                        k0 = 0
                        for nk in MOE_DOWN:
                            load(k, r, moe_down[bass.ds(e, 1), k0 * P:(k0 + nk) * P, n0:n0 + NB]
                                 .rearrange("e (k p) n -> p (e k) n", p=P), nk, NB)
                            k, k0 = k + 1, k0 + nk

                with sp.Fori(0, N_EXP) as i:
                    expert(i, i * R_ITEM)
                sp.wait_ge(S("routed"), 1)
                n_items = sp.value_load(route_i[0:1, 3:4], min_val=N_EXP, max_val=ITEMS)
                for j in range(ITEMS - N_EXP):
                    with sp.If(n_items > N_EXP + j):
                        e = sp.value_load(route_i[0:1, j:j + 1], min_val=0, max_val=N_EXP - 1)
                        expert(e, (N_EXP + j) * R_ITEM)
                    sp.end_ifs()
                if "ple1" in live:
                    loads("ple1", n_items * R_ITEM)
            sp.wait_ge(S("x_done"), 1)
            sp.dma_start(out[0].rearrange("(t p) n -> p t n", p=P), x[:]).then_inc(S("out_landed"), 16)
            sp.wait_ge(S("out_landed"), 16)

        def kv_place(g, c_):
            order = [[(0, 0), (1, 0), (0, 2), (1, 2), (2, 2), (3, 2)], [(0, 1), (1, 1), (2, 3), (3, 3), (2, 1), (3, 1)]]
            i = order[c_ % 2].index((g, c_))
            return scr[:, 2 * (c_ % 2) + i // 4, (i % 4) * P:(i % 4 + 1) * P]

        gains = [("norm_mix_pre", 0), ("norm_mix_post", 0), ("norm_ffn_pre", 0), ("norm_ffn_post", 0),
                 ("ln_mix_g_2", 0), ("ln_mix_b_2", 0), ("ln_ffn_g_2", 0), ("ln_ffn_b_2", 0),
                 ("ln_mix_g_2", 1), ("ln_mix_b_2", 1), ("ln_ffn_g_2", 1), ("ln_ffn_b_2", 1)]

        @block.gpsimd
        def _(pool):
            def one(ins):
                pool.drain()

            def gain_row(i):
                if i >= 2:
                    pool.wait_ge(S("gain_used"), i - 1)
                g, l = gains[i]
                pool.dma_start(gain[:, i % 2, :], a[g][l:l + 1, :].broadcast_to([P, D]))\
                    .then_inc(S(f"gain_landed{i % 2}"), 16)

            def keep(t, pattern, first, per_row, fill=0.0, op=ALU.is_ge):
                one(pool.affine_select(out=t, in_=t, pattern=pattern, compare_op=op, fill=fill, base=first,
                                       channel_multiplier=per_row))

            gain_row(0)
            gain_row(1)
            pool.memset(ident[:], 0.0)
            one(None)
            pool.affine_select(out=ident[:], in_=ident[:], pattern=[[-1, P]], compare_op=ALU.not_equal, fill=1.0,
                               base=0, channel_multiplier=1).then_inc(S("ident_ready"), 1)
            pool.dma_start(conv_w[:], a["conv_a"].broadcast_to([P, 3, D_HALF])).then_inc(S("conv_w_landed"), 16)
            pool.dma_start(head_gain[:], a["gla_head_norm"].broadcast_to([P, HEAD_V])).then_inc(S("head_gain_landed"), 16)
            pool.dma_start(rb_row[:], a["router_b_2"].broadcast_to([P, N_EXP])).then_inc(S("rb_landed"), 16)
            pool.memset(gate_w[:], 0.0)
            for t, v in ((ones, 1.0), (tri_incl, 1.0), (tri_excl, 1.0), (neg_from, -1.0), (neg_ones, -1.0),
                         (tri_fwd, DECAY), (tri_bwd, DECAY)):
                pool.memset(t[:], v)
            pool.iota(slot_row[:], pattern=[[1, P]], base=0, channel_multiplier=0,
                      allow_small_or_imprecise_dtypes=True)
            one(None)
            for src, r, cc in (("gate_up_fwd", 0, 0), ("gate_up_bwd", RANK, N_GK)):
                pool.dma_start(gate_w[r:r + RANK, cc:cc + N_GK], a[src][0]).then_inc(S("gate_w_landed"), 16)
            for src, cc in (("gate_bias_fwd", 0), ("gate_bias_bwd", N_GK)):
                pool.dma_start(gate_w[2 * RANK:2 * RANK + 1, cc:cc + N_GK], a[src]).then_inc(S("gate_w_landed"), 16)
            keep(tri_incl[:], [[1, P]], 0, -1)
            keep(tri_excl[:], [[1, P]], -1, -1)
            keep(neg_from[:], [[-1, P]], 0, 1)
            keep(tri_fwd[:], [[1, P]], 0, -1)
            keep(tri_bwd[:], [[-1, P]], 0, 1)
            keep(tri_fwd[:, GLA_CHUNK:P], [[0, P - GLA_CHUNK]], -GLA_CHUNK, 1)
            keep(tri_bwd[:, 0:GLA_CHUNK], [[0, GLA_CHUNK]], GLA_CHUNK - 1, -1)
            pool.drain().then_inc(S("tri_ready"), 1)

            for bb in (0, 1, 2):
                wait_evacuated(pool, bb)
            pool.wait_ge(S("conv_w_landed"), 16)
            gc, gv = p0[:, :, C_GC:C_GC + D_HALF], p0[:, :, C_GV:C_GV + D_HALF]
            ya = y[:, :, 0:D_HALF]
            one(pool.tensor_tensor(gc, gc, gv, ALU.mult))
            pool.memset(gv, 0.0)
            one(pool.memset(ya, 0.0))
            for dst, src in ((gv[1:P, :, :], gc[0:P - 1, :, :]), (gv[0:1, 1:2, :], gc[P - 1:P, 0:1, :]),
                             (ya[0:P - 1, :, :], gc[1:P, :, :]), (ya[P - 1:P, 0:1, :], gc[0:1, 1:2, :])):
                pool.dma_start(dst, src).then_inc(S("shift_landed"), 16)
            pool.wait_ge(S("shift_landed"), 64)
            for dst, tap in ((ya, 2), (gv, 0), (gc, 1)):
                for t in range(NT):
                    pool.tensor_tensor(dst[:, t, :], dst[:, t, :], conv_w[:, tap, :], ALU.mult)
            one(None)
            one(pool.tensor_tensor(gv, gv, gc, ALU.add))
            one(pool.tensor_tensor(ya, ya, gv, ALU.add))
            pool.tensor_tensor(ya, ya, p0[:, :, C_GB:C_GB + D_HALF], ALU.mult).then_inc(S("ya_ready"), 1)

            if "w_up" in live:
                pool.wait_ge(S("t_source"), 2 * NT)
                pool.dma_start(cw_rows[:], a["conv_ffn"][0].rearrange("j (k p) -> k j p", p=P)).then_inc(S("cw_landed"), 16)
            gain_row(2)
            if "w_up" in live:
                gain_row(3)
            if "ab_in" in live:
                for i in (4, 5):
                    gain_row(i)
                wait_phase_evacuated(pool, "w_down")
                pool.dma_start(fbias[:], a["ab_b_f_2"].broadcast_to([P, N_AB])).then_inc(S("fbias_landed"), 16)
                for t, v in ((mask_fox[:], 0.0), (mask_sb[:], 0.0), (keep_sb[:], 1.0), (neg_head[:], -1.0), (ct[:], 0.0)):
                    pool.memset(t, v)
                one(None)
                keep(mask_fox[:, 0:P], [[-1, P]], 0, 1, NEG)
                keep(mask_fox[:, P:SCW], [[-1, SEQ]], P, 1, NEG)
                for t, fill in ((mask_sb, NEG), (keep_sb, 0.0)):
                    keep(t[:, 0:SEQ], [[1, SEQ]], -1, -1, fill)
                    keep(t[:, SEQ:SCW], [[1, P]], -1, -1, fill)
                keep(neg_head[:], [[1, N_AB], [0, P]], 0, -1, 0.0)
                keep(neg_head[:], [[-1, N_AB], [0, P]], 0, 1, 0.0)
                pool.drain().then_inc(S("ab_masks_ready"), 1)
            if "ffn_up" in live:
                for i in (6, 7):
                    gain_row(i)
            if "ple0" in live:
                wait_phase_evacuated(pool, "ffn_down")
                pool.dma_start(pn[:], a["p_2"][0, 0].rearrange("(t p) n -> p t n", p=P)).then_inc(S("p_landed"), 16)
            if "qkv" in live:
                for i in (8, 9):
                    gain_row(i)
                pool.wait_ge(S("ple_x"), 1)
                pool.dma_start(rope[:], a["rope"].rearrange("c (t p) n -> p c t n", p=P)).then_inc(S("rope_landed"), 16)
                pool.dma_start(sink[:], a["c_sinks_2"].broadcast_to([P, N_SWA])).then_inc(S("sink_landed"), 16)
                one(pool.memset(mask_swa[:], 0.0))
                keep(mask_swa[:, 0:P], [[-1, P]], 0, 1, NEG)
                keep(mask_swa[:, P:SCW], [[-1, SEQ]], P, 1, NEG)
                keep(mask_swa[:, P:SCW], [[1, SEQ]], -1, -1, NEG)
                pool.drain().then_inc(S("swa_mask_ready"), 1)
            if "moe" in live:
                for i in (10, 11):
                    gain_row(i)
                wait_phase_evacuated(pool, "c_out")
                pool.dma_start(rw[:], a["router_w_2"][0].rearrange("(k p) e -> p k e", p=P)).then_inc(S("rw_landed"), 16)
            if "ple1" in live:
                pool.wait_ge(S("moe_x"), 1)
                pool.dma_start(pn[:], a["p_2"][1, 0].rearrange("(t p) n -> p t n", p=P)).then_inc(S("p_landed"), 16)

        @block.scalar
        def _(act):
            me = Place()
            for s in range(2):
                act.sem_inc(S(f"acc_free{s}"), 1)

            def copy(o, i, func=ACT.Copy, **kw):
                return act.activation(o, i, func, **kw)

            def round_chunk(k, r, n):
                act.wait_ge(S(f"w_landed{k % RING}"), 16 * (k // RING + 1) + 16 * r)
                wait_used(act, k - RING + 1, r)
                copy(w_hi[:, k % RING, 0:n], w_raw[:, k % RING, 0:n]).then_inc(S("hi_ready"), 1)

            def round_to(c, r=0):
                while me.chunk < (c if me.looping else min(c, me.cap)):
                    round_chunk(me.chunk, r, CHUNK if me.looping else width[me.chunk])
                    me.chunk += 1

            def root(n):
                act.wait_ge(S("ms_ready"), n + 1)
                copy(stat[:, 2:4], stat[:, 0:2], ACT.Sqrt).then_inc(S("root_ready"), 1)

            def operand(m):
                for j in range(4):
                    act.wait_ge(S("t_ready"), 4 * m + j + 1)
                    copy(xt_hi[:, 4 * (j % 2):4 * (j % 2) + 4, (j // 2) * P:(j // 2 + 1) * P],
                         scr[:, j, :].rearrange("p (k n) -> p k n", n=P)).then_inc(S("xt_hi_ready"), 1)

            def evacuate(name, dst):
                def body(blocks, r):
                    for bb, cc, n0, n, ps in blocks:
                        round_to(cc + len(ps) + 2, r)
                        wait_used(act, cc + len(ps), r)
                        for t in range(NT):
                            i = copy(dst[:, t, sl(ncol(name, n0, r), n)], acc[bb % 2][t][:, 0:n])
                        i.then_inc(S(f"acc_free{bb % 2}"), 1)
                split_loop(act, name, body, me)

            def log_sigmoid_tail(o, z):
                copy(o, z, ACT.Abs)
                act.drain()
                copy(o, o, ACT.Exp, scale=-1.0)
                act.drain()
                return copy(o, o, ACT.Ln, bias=1.0)

            def squares(name):
                for bb, cc, n0, n, ps in phase[name]:
                    round_to(cc + len(ps) + 2)
                    wait_used(act, cc + len(ps))
                    for t in range(NT):
                        col = 8 + NT * (n0 // NB) + t
                        copy(y[:, t, n0:n0 + n], acc[bb % 2][t][:, 0:n], ACT.Square, accum_out=stat[:, col:col + 1])
                    act.drain().then_inc(S("sq_ready"), 1)

            def squares_x(ready):
                for t in range(NT):
                    ready(t)
                    copy(junk[:, t, :], x[:, t, :], ACT.Square, accum_out=stat[:, 6 + t:7 + t])
                    act.drain().then_inc(S("sq_ready"), 1)

            def pace(name):
                for bb, cc, n0, n, ps in phase[name]:
                    round_to(cc + len(ps) + 2)

            squares_x(lambda t: act.wait_ge(S(f"x_landed{t}"), 16))
            root(0)
            operand(0)
            round_to(2)
            evacuate("w_in", p0)
            act.wait_ge(S("lr_t"), 1)
            copy(lrt[0:2 * RANK, :], scr[0:2 * RANK, 0, 0:SEQ]).then_inc(S("lrt_ready"), 1)
            act.wait_ge(S("qk_t"), 1)
            copy(qk0[:, 0:2, :], scr[:, 1, :].rearrange("p (f n) -> p f n", n=SEQ), scale=HEAD_K ** -0.5)
            copy(qk0[:, 2:4, :], scr[:, 2, :].rearrange("p (f n) -> p f n", n=SEQ)).then_inc(S("qk0_ready"), 1)
            act.wait_ge(S("gate_pre"), 1)
            log_sigmoid_tail(tmp0[:], psum[:, 0:2, :]).then_inc(S("gate_ln"), 1)
            act.wait_ge(S("cum_ready"), 1)
            copy(e1[:], cum[:], ACT.Exp).then_inc(S("gla_exp"), 1)
            copy(e2[:], cum[:], ACT.Exp, scale=-1.0).then_inc(S("gla_exp"), 1)
            act.wait_ge(S("cum_rest"), 1)
            copy(e3[:], e3[:], ACT.Exp).then_inc(S("gla_exp"), 1)
            act.wait_ge(S("q_in"), 1)
            act.wait_ge(S("q_half_zero"), 1)
            for par in range(2):
                v = lambda t: t.rearrange("p g (c q n) -> p (g c) q n", q=2, n=GLA_CHUNK)[:, :, par, :]
                i = copy(v(q_half[:, par]), v(e1[:]))
            i.then_inc(S("q_half_ready"), 1)
            for t in range(NT):
                act.wait_ge(S("kout_t"), t + 1)
                copy(kout[:, t, :], scr[:, 3 * t, :]).then_inc(S("kout_ready"), 1)
            go = p0[:, :, C_GO:C_GO + D_HALF]
            wait_evacuated(act, 5)
            copy(go, go, ACT.Silu).then_inc(S("go_ready"), 1)
            act.wait_ge(S("gla_o"), NT)
            act.wait_ge(S("e2_free"), 1)
            copy(e2[:], psum[:, 0:4, 0:SEQ], ACT.Square).then_inc(S("o_sq"), 1)
            act.wait_ge(S("o_ms"), 1)
            copy(ss8[:, 1, :], ss8[:, 0, :], ACT.Sqrt).then_inc(S("o_root"), 1)
            operand(1)
            squares("w_out")
            root(1)

            def up_conv(blocks, r):
                (bg, cg, n0, n, _), (bv, cv, _, _, _) = blocks
                j, nc_ = n0 // NB, n // P
                end = cv + (cv - cg)

                def middle_tap(h, u, bb):
                    for k in range(nc_):
                        ch = h * KF + 4 * j + k
                        i = copy(u[:, k, :], acc_t(bb % 2, k), scale=cw[:, 1, ch:ch + 1])
                    i.then_inc(S("tap_mid"), 1)

                round_to(cv + 2)
                wait_used(act, cv)
                if j:
                    act.wait_ge(S("ht_ready"), j)
                else:
                    act.wait_ge(S("cw_ready"), 1)
                middle_tap(0, ug, bg)
                act.wait_ge(S("gate_conv"), j + 1)
                copy(ug[:, 0:nc_, :], ug[:, 0:nc_, :], ACT.Silu)
                act.drain().then_inc(S("silu_ready"), 1)
                round_to(end + 2)
                wait_used(act, end)
                middle_tap(1, uv, bv)
                act.wait_ge(S("h_ready"), j + 1)
                copy(ht_hi[:, 4 * j:4 * j + nc_, :], uv[:, 0:nc_, :]).then_inc(S("ht_hi_ready"), 1)

            if "w_up" in live:
                squares_x(lambda t: act.wait_ge(S("x_tile"), t + 1))
                root(2)
                operand(2)
                split_loop(act, "w_up", up_conv, me, unroll=True)
            if "w_down" in live:
                squares("w_down")
                root(3)

            def softmax(q, smx_, sink_=False):
                act.wait_ge(S("at_negm"), q + 1)
                for h in range(8):
                    for t, (c0, c1) in enumerate(((0, P), (P, SCW))):
                        i = copy(s_all[:, h, c0:c1], s_all[:, h, c0:c1], ACT.Exp, bias=smx_[:, 1, t, h:h + 1],
                                 accum_out=smx_[:, 2, t, h:h + 1])
                    act.drain().then_inc(S("at_p"), 1)
                if sink_:
                    copy(smx_[:, 4, :, :], smx_[:, 3, :, :], ACT.Exp)
                act.drain().then_inc(S("at_sum"), 1)

            if "ab_in" in live:
                operand(3)
                evacuate("ab_in", p1)
                act.wait_ge(S("lf_pre"), 1)
                log_sigmoid_tail(lf[:, 1, :, :], lf[:, 0, :, :]).then_inc(S("lf_ln"), 1)
                for g in range(2):
                    for tile in range(4):
                        act.wait_ge(S("ab_t"), 4 * g + tile + 1)
                        copy(qk1[:, 2 * tile:2 * tile + 2, :], scr[:, tile, :].rearrange("p (f n) -> p f n", n=SEQ),
                             scale=DH ** -0.5 if tile < 2 else 1.0).then_inc(S("qk1_ready"), 1)
                    if g == 0:
                        softmax(0, smx)
                for g in range(2):
                    act.wait_ge(S("sb_z"), g + 1)
                    log_sigmoid_tail(sba[:], scr[:, :, 0:SCW]).then_inc(S("sb_ln"), 1)
                    act.wait_ge(S("sb_masked"), g + 1)
                    copy(sba[:], sba[:], ACT.Exp).then_inc(S("sb_a"), 1)
            if "ab_out" in live:
                operand(4)
                pace("ab_out")
                root(4)

            def up_gated(blocks, r):
                (bg, cg, n0, n, _), (bv, cv, _, _, _) = blocks
                j, nc_ = n0 // NB, n // P
                round_to(cv + 2)
                wait_used(act, cv)
                if j:
                    act.wait_ge(S("h_ready"), KP + j)
                copy(ug[:, 0:nc_, :], acc_tall(bg % 2, nc_), ACT.Silu).then_inc(S(f"acc_free{bg % 2}"), 1)
                round_to(cv + (cv - cg) + 2)
                act.wait_ge(S("h_ready"), KP + j + 1)
                copy(ht_hi[:, 4 * j:4 * j + nc_, :], uv[:, 0:nc_, :]).then_inc(S("ht_hi_ready"), 1)

            if "ffn_up" in live:
                operand(5)
                split_loop(act, "ffn_up", up_gated, me, unroll=True)
            if "ffn_down" in live:
                pace("ffn_down")
                root(5)

            def ple(i, m, r=0):
                operand(m)
                act.wait_ge(S("p_t"), i + 1)
                copy(ppt_hi[:], scr[:, 0, :].rearrange("p (k n) -> p k n", n=SEQ)).then_inc(S("ppt_hi_ready"), 1)
                name = f"ple{i}"
                for q in range(2):
                    (bg, cg, _, _, _), (bp, cp, _, _, psp) = phase[name][2 * q:2 * q + 2]
                    round_to(cp + 1, r)
                    wait_used(act, cp, r)
                    if q or i:
                        act.wait_ge(S("ple_added"), 2 * i + q)
                    for t in range(NT):
                        j = copy(sig[:, t, :], acc[bg % 2][t], ACT.Sigmoid)
                    j.then_inc(S(f"acc_free{bg % 2}"), 1)
                    round_to(cp + 3, r)

            if "ple0" in live:
                ple(0, 6)
            if "qkv" in live:
                operand(7)
                evacuate("qkv", p2)
                for j in range(3):
                    act.wait_ge(S("swa_t"), j + 1)
                    nb = 4 if j < 2 else 2
                    if j < 2:
                        copy(qk2[:, 4 * j:4 * j + 4, :], scr[:, 2 * (j % 2):2 * (j % 2) + 2, :]
                             .rearrange("p b (f n) -> p (b f) n", n=SEQ), scale=DH ** -0.5)\
                            .then_inc(S("qk2_ready"), 1)
                    else:
                        copy(qk2[:, 8:10, :], scr[:, 0, :].rearrange("p (f n) -> p f n", n=SEQ))\
                            .then_inc(S("qk2_ready"), 1)
                for g in range(2):
                    softmax(1 + g, smx2, True)
            if "c_out" in live:
                operand(8)
                pace("c_out")
                root(6)

            def rounds(k0, k1, r):
                for k in range(k0, k1):
                    round_chunk(N_BEFORE_MOE + k, r, item_width(k))

            def take_item(n, k, r):
                act.wait_ge(S("gathered"), 3 * n + 1)
                copy(xg_hi[:], scr[:, 2:4, :].rearrange("p b (k n) -> p (b k) n", n=P)).then_inc(S("xg_hi_ready"), 1)
                rounds(k, k + 2, r)
                act.wait_ge(S("gathered"), 3 * n + 3)
                copy(selt[:], scr[:, 2, 0:SEQ])
                copy(gslot[:], scr[:, 2, SEQ:SEQ + 1]).then_inc(S("selt_ready"), 1)

            def item(i):
                c0, r = N_BEFORE_MOE, i * R_ITEM
                for j in range(MOE_PAIRS):
                    wait_used(act, c0 + 4 * j + 2, r)
                    if j:
                        act.wait_ge(S("mh_ready"), MOE_PAIRS * i + j)
                    copy(mg[:], psum[:, 2 * (j % 2), :], ACT.Silu).then_inc(S("mg_ready"), 1)
                    rounds(4 * j + 4, 4 * j + 6, r)
                    if j:
                        act.wait_ge(S("mh_t"), MOE_PAIRS * i + j)
                        copy(mh_hi[:, 4 * j - 4:4 * j, :], psum[:, 6 + (j - 1) % 2, :].rearrange("p (k n) -> p k n", n=P))\
                            .then_inc(S("mh_hi_ready"), 1)
                    rounds(4 * j + 6, 4 * j + 8, r)
                j = MOE_PAIRS
                act.wait_ge(S("mh_t"), MOE_PAIRS * i + j)
                copy(mh_hi[:, 4 * j - 4:4 * j, :], psum[:, 6 + (j - 1) % 2, :].rearrange("p (k n) -> p k n", n=P))\
                    .then_inc(S("mh_hi_ready"), 1)
                k = 4 * j + 4
                for n in range(2):
                    end = MOE_UP_CHUNKS + len(MOE_DOWN) * (n + 1)
                    rounds(k, end + 2, r)
                    k = end + 2
                    wait_used(act, c0 + end, r)
                    copy(ys_hi[:, n * NB:(n + 1) * NB], psum[:, 4 + n, :], scale=gslot[:, 0:1])\
                        .then_inc(S("ys_hi_ready"), 1)
                take_item(i + 1, k, r)

            if "moe" in live:
                operand(9)
                copy(xn_hi[:], x[:]).then_inc(S("xn_hi_ready"), 1)
                act.wait_ge(S("top_gap"), 1)
                copy(route[:, 142:144], route[:, 140:142], ACT.Exp).then_inc(S("top_exp"), 1)
                act.wait_ge(S("routed"), 1)
                n_items = act.value_load(route_i[0:1, 3:4], min_val=N_EXP, max_val=ITEMS)
                rounds(0, 2, 0)
                take_item(0, 2, 0)
                with act.Fori(0, ITEMS) as i:
                    with act.If(i < n_items):
                        item(i)
                    act.end_ifs()
                me.cap = N_STATIC
                root(7)
            if "ple1" in live:
                me.chunk += RING
                ple(1, 10, n_items * R_ITEM)

        @block.vector
        def _(dve):
            me = Place()
            dve.sem_inc(S("lo_ready"), RING)
            TT, STT, TS = dve.tensor_tensor, dve.scalar_tensor_tensor, dve.tensor_scalar
            used_rows = [0]

            def split_chunk(k, r, n):
                dve.wait_ge(S("hi_ready"), k + 1 + RING * r)
                TT(w_lo[:, k % RING, 0:n], w_raw[:, k % RING, 0:n], w_hi[:, k % RING, 0:n].bitcast(F32), ALU.subtract)\
                    .then_inc(S("lo_ready"), 1)

            def round_to(c, r=0):
                while me.chunk < (c if me.looping else min(c, me.cap)):
                    split_chunk(me.chunk, r, CHUNK if me.looping else width[me.chunk])
                    me.chunk += 1

            def operand(m):
                for j in range(4):
                    dve.wait_ge(S("xt_hi_ready"), 4 * m + j + 1)
                    o = (slice(None), slice(4 * (j % 2), 4 * (j % 2) + 4), slice((j // 2) * P, (j // 2 + 1) * P))
                    TT(xt_lo[o], scr[:, j, :].rearrange("p (k n) -> p k n", n=P), xt_hi[o].bitcast(F32), ALU.subtract)\
                        .then_inc(S("xt_ready"), 1)

            def row(i):
                dve.wait_ge(S(f"gain_landed{i % 2}"), 16 * (i // 2 + 1))
                return gain[:, i % 2, :]

            def inverse_root(n):
                dve.drain().then_inc(S("ms_ready"), 1)
                dve.wait_ge(S("root_ready"), n + 1)
                dve.reciprocal(stat[:, 4:6], stat[:, 2:4])
                dve.drain()

            def rms_root(n):
                TS(stat[:, 0:2], stat[:, 6:8], 1.0 / D, RMS_EPS, ALU.mult, ALU.add)
                inverse_root(n)

            def rms_before(n, i):
                dve.wait_ge(S("sq_ready"), 2 * (n + 1))
                rms_root(n)
                g = row(i)
                for t in range(NT):
                    STT(y[:, t, :], x[:, t, :], stat[:, 4 + t:5 + t], g, ALU.mult, ALU.mult)
                    dve.drain().then_inc(S("t_source"), 1)
                dve.sem_inc(S("gain_used"), 1)

            def rms_after(n, i, name, done):
                dve.wait_ge(S("sq_ready"), 2 * (n + 1))
                TT(stat[:, 6:8], stat[:, 8:10], stat[:, 10:12], ALU.add)
                dve.drain()
                rms_root(n)
                g = row(i)
                for t in range(NT):
                    for bb, _, n0, w_, _ in phase[name]:
                        k = STT(y[:, t, n0:n0 + w_], acc[bb % 2][t], stat[:, 4 + t:5 + t], g[:, n0:n0 + w_], ALU.mult, ALU.mult)
                        if t == NT - 1:
                            k.then_inc(S(f"acc_free{bb % 2}"), 1)
                    dve.drain()
                    TT(x[:, t, :], x[:, t, :], y[:, t, :], ALU.add)
                    dve.drain().then_inc(S(done), 1)
                dve.sem_inc(S("gain_used"), 1)

            def add_half(h, part):
                cols = slice(h * NB, (h + 1) * NB)
                for t in range(NT):
                    k = STT(x[:, t, cols], x[:, t, cols], ALPHA, part(t), ALU.mult, ALU.add)
                dve.drain()
                for t in range(NT):
                    dve.bn_stats(bn[:, t, h, :], x[:, t, cols])

            def follow_add(name):
                for bb, cc, n0, n, ps in phase[name]:
                    round_to(cc + len(ps) + 2)
                    wait_used(dve, cc + len(ps))
                    add_half(n0 // NB, lambda t: acc[bb % 2][t])
                    dve.sem_inc(S(f"acc_free{bb % 2}"), 1)

            def layer_norm(n, i):
                dve.drain()
                for t in range(NT):
                    dve.bn_aggr(stat[:, 8 + 2 * t:10 + 2 * t], bn[:, t, :, :])
                dve.drain()
                TS(stat[:, 0:2], stat[:, 9:12:2], LN_EPS, None, ALU.add)
                inverse_root(n)
                g, b_ = row(i), row(i + 1)
                for t in range(NT):
                    STT(x[:, t, :], x[:, t, :], stat[:, 8 + 2 * t:9 + 2 * t], g, ALU.subtract, ALU.mult)
                    dve.drain()
                    STT(x[:, t, :], x[:, t, :], stat[:, 4 + t:5 + t], b_, ALU.mult, ALU.add)
                    dve.drain().then_inc(S("t_source"), 1)
                dve.sem_inc(S("gain_used"), 2)

            def follow(name):
                def body(blocks, r):
                    for bb, cc, n0, n, ps in blocks:
                        round_to(cc + len(ps) + 2, r)
                split_loop(dve, name, body, me)

            rms_before(0, 0)
            operand(0)
            round_to(2)
            follow("w_in")
            wait_phase_evacuated(dve, "w_in")
            dve.memset(q_half[:], 0.0).then_inc(S("q_half_zero"), 1)
            dve.memset(lrt[2 * RANK:2 * RANK + 1, :], 1.0).then_inc(S("lrt_ones"), 1)
            dve.wait_ge(S("gate_ln"), 1)
            STT(logd[:], psum[:, 0:2, :], 0.0, tmp0[:], ALU.min, ALU.subtract).then_inc(S("logd_ready"), 1)
            dve.wait_ge(S("cum_t"), 1)
            cum_ps = psum[:, 2:4, :].rearrange("p b (f n) -> p (b f) n", n=SEQ)
            dve.tensor_copy(cum[:], cum_ps)
            dve.drain().then_inc(S("cum_ready"), 1)
            chunks = lambda t: t.rearrange("p f (c n) -> p f c n", n=GLA_CHUNK)
            for d, last in ((0, GLA_CHUNK - 1), (1, 0)):
                for f in (2 * d, 2 * d + 1):
                    v = chunks(cum[:])[:, f, :, :]
                    i = TT(chunks(e3[:])[:, f, :, :], v[:, :, last:last + 1].broadcast_to([P, 4, GLA_CHUNK]), v, ALU.subtract)
            i.then_inc(S("cum_rest"), 1)
            dve.wait_ge(S("gla_exp"), 1)
            for d, last in ((0, GLA_CHUNK - 1), (1, 0)):
                dve.tensor_copy(dec[:, 2 * d:2 * d + 2, :], chunks(e1[:])[:, 2 * d:2 * d + 2, :, last])
            dve.drain()
            dve.wait_ge(S("qk0_ready"), 1)
            for n, (e, q) in enumerate(((e1, 0), (e2, 2), (e3, 2))):
                dve.wait_ge(S("gla_exp"), n + 1)
                for d in range(2):
                    i = TT(e[:, 2 * d:2 * d + 2, :], e[:, 2 * d:2 * d + 2, :], qk0[:, q:q + 2, :], ALU.mult)
                i.then_inc(S(("q_in", "k_in", "k_out")[n]), 1)
            dve.memset(st[:], 0.0)
            dve.drain()
            for d, tri in ((0, tri_fwd), (1, tri_bwd)):
                dve.wait_ge(S("gla_scores"), d + 1)
                dve.copy_predicated(st[:, d].rearrange("p a b n -> p (a b) n"),
                                    tri[:].bitcast(I32).unsqueeze(1).broadcast_to([P, 8, P]),
                                    psum[:, 2 * d:2 * d + 2, :].rearrange("p b (k n) -> p (b k) n", n=P))\
                    .then_inc(S("st_ready"), 1)
            dve.wait_ge(S("gla_kv"), 1)
            for step in range(3):
                for g in range(4):
                    src, dst = (step, step + 1) if g < 2 else (3 - step, 2 - step)
                    kv = kv_place(g, src)
                    if step == 0:
                        dve.tensor_copy(state[:, g, dst, :], kv)
                    else:
                        STT(state[:, g, dst, :], state[:, g, src, :], dec[:, g, src:src + 1], kv, ALU.mult, ALU.add)
                dve.drain()
            dve.sem_inc(S("state_ready"), 1)
            dve.sem_inc(S("e2_free"), 1)
            dve.wait_ge(S("o_sq"), 1)
            dve.reduce_sum(ss8[:, 2, :], e2[:].rearrange("p a (b n) -> p (a b) n", n=HEAD_V), AX_X)
            dve.drain()
            TS(ss8[:, 0, :], ss8[:, 2, :], 1.0 / HEAD_V, RMS_EPS, ALU.mult, ALU.add).then_inc(S("o_ms"), 1)
            dve.wait_ge(S("o_root"), 1)
            dve.reciprocal(ss8[:, 2, :], ss8[:, 1, :])
            dve.drain()
            o8 = e3[:].rearrange("p a (b n) -> p (a b) n", n=HEAD_V)
            for t in range(NT):
                TT(o8[:, 4 * t:4 * t + 4, :].rearrange("p (a b) n -> p a b n", b=2),
                   psum[:, 2 * t:2 * t + 2, 0:SEQ].rearrange("p a (b n) -> p a b n", n=HEAD_V),
                   ss8[:, 2, 4 * t:4 * t + 4].rearrange("p (a b) -> p a b", b=2).unsqueeze(3).broadcast_to([P, 2, 2, HEAD_V]),
                   ALU.mult)
            dve.drain()
            dve.wait_ge(S("head_gain_landed"), 16)
            TT(o8, o8, head_gain[:].unsqueeze(1).broadcast_to([P, 8, HEAD_V]), ALU.mult)
            dve.drain()
            dve.wait_ge(S("go_ready"), 1)
            dve.wait_ge(S("ya_ready"), 1)
            for t in range(NT):
                heads = lambda v: v.rearrange("p (b a n) -> p a b n", a=2, n=HEAD_V)
                TT(heads(y[:, t, D_HALF:D]), o8[:, 4 * t:4 * t + 4, :].rearrange("p (a b) n -> p a b n", b=2),
                   heads(p0[:, t, C_GO:C_GO + D_HALF]), ALU.mult)
                dve.drain().then_inc(S("t_source"), 1)
            operand(1)
            follow("w_out")
            rms_after(1, 1, "w_out", "x_tile")

            def up_conv(blocks, r):
                (bg, cg, n0, n, _), (bv, cv, _, _, _) = blocks
                j, nc_ = n0 // NB, n // P

                def outer_taps(h, u, bb):
                    dve.wait_ge(S("tap_mid"), 2 * j + h + 1)
                    for tap in (0, 2):
                        o, s = (slice(1, SEQ), slice(0, SEQ - 1)) if tap == 0 else (slice(0, SEQ - 1), slice(1, SEQ))
                        for k in range(nc_):
                            ch = h * KF + 4 * j + k
                            STT(u[:, k, o], acc_t(bb % 2, k)[:, s], cw[:, tap, ch:ch + 1], u[:, k, o], ALU.mult, ALU.add)
                        dve.drain()
                    dve.sem_inc(S(f"acc_free{bb % 2}"), 1)

                round_to(cv + 2)
                outer_taps(0, ug, bg)
                dve.sem_inc(S("gate_conv"), 1)
                round_to(cv + (cv - cg) + 2)
                outer_taps(1, uv, bv)
                dve.wait_ge(S("silu_ready"), j + 1)
                TT(uv[:, 0:nc_, :], ug[:, 0:nc_, :], uv[:, 0:nc_, :], ALU.mult)
                dve.drain().then_inc(S("h_ready"), 1)
                split_h(j, j, nc_)

            def split_h(q, j, nc_):
                dve.wait_ge(S("ht_hi_ready"), q + 1)
                o = (slice(None), slice(4 * j, 4 * j + nc_))
                TT(ht_lo[o], uv[:, 0:nc_, :], ht_hi[o].bitcast(F32), ALU.subtract).then_inc(S("ht_ready"), 1)

            if "w_up" in live:
                rms_before(2, 2)
                dve.wait_ge(S("cw_turned"), 1)
                dve.tensor_copy(cw[:].rearrange("p j k -> p (j k)"), psum[:, 0, 0:3 * 2 * KF]).then_inc(S("cw_ready"), 1)
                operand(2)
                split_loop(dve, "w_up", up_conv, me, unroll=True)
            if "w_down" in live:
                follow("w_down")
                rms_after(3, 3, "w_down", "t_source")

            def softmax(q, smx_, mask, column):
                for h in range(8):
                    dve.wait_ge(S("at_qk"), 8 * q + h + 1)
                    if q == 0:
                        for t, (c0, c1) in enumerate(((0, P), (P, SCW))):
                            i = STT(s_all[:, h, c0:c1], scr[:, h % 4, c0:c1], cq[:, t, h:h + 1], mask[:, c0:c1],
                                    ALU.add, ALU.add)
                    else:
                        i = TT(s_all[:, h, :], scr[:, h % 4, 0:SCW], mask[:], ALU.add)
                    i.then_inc(S("at_s"), 1)
                dve.drain()
                dve.reduce_max(smx_[:, 0, 0, :], s_all[:, :, 0:P], AX_X)
                dve.reduce_max(smx_[:, 0, 1, :], s_all[:, :, P:SCW], AX_X)
                dve.drain()
                if q:
                    s8 = sink[:, 8 * (q - 1):8 * q].unsqueeze(1).broadcast_to([P, NT, 8])
                    TT(smx_[:, 0], smx_[:, 0], s8, ALU.max)
                    dve.drain()
                    TT(smx_[:, 3], s8, smx_[:, 0], ALU.subtract)
                TS(smx_[:, 1], smx_[:, 0], -1.0, None, ALU.mult)
                dve.drain().then_inc(S("at_negm"), 1)
                for h in range(8):
                    dve.wait_ge(S("at_t"), 8 * q + h + 1)
                    dve.tensor_copy((pt if q == 0 else pt2)[:, h % 2, :], psum[:, h % 2, 0:SCW]).then_inc(S("at_pt"), 1)
                dve.wait_ge(S("at_sum"), q + 1)
                if q:
                    TT(smx_[:, 2], smx_[:, 2], smx_[:, 4], ALU.add)
                    dve.drain()
                dve.reciprocal(smx_[:, 5], smx_[:, 2])
                dve.drain()
                dve.wait_ge(S("at_o"), q + 1)
                for t in range(NT):
                    i = TT(y[:, t, column:column + 8 * DH].rearrange("p (h n) -> p h n", n=DH),
                           psum[:, 2 + t, :].rearrange("p (h n) -> p h n", n=DH),
                           smx_[:, 5, t, :].unsqueeze(2).broadcast_to([P, 8, DH]), ALU.mult)
                dve.drain().then_inc(S("at_y"), 1)

            if "ab_in" in live:
                operand(3)
                follow("ab_in")
                wait_phase_evacuated(dve, "ab_in")
                dve.wait_ge(S("fbias_landed"), 16)
                TT(lf[:, 0, :, :], p1[:, :, AB_FA:AB_FA + N_AB], fbias[:].unsqueeze(1).broadcast_to([P, NT, N_AB]), ALU.add)
                dve.drain().then_inc(S("lf_pre"), 1)
                dve.wait_ge(S("lf_ln"), 1)
                STT(lf[:, 2, :, :], lf[:, 0, :, :], 0.0, lf[:, 1, :, :], ALU.min, ALU.subtract)
                dve.drain().then_inc(S("lf_ready"), 1)
                dve.wait_ge(S("ab_masks_ready"), 1)
                dve.wait_ge(S("lf_cum"), 1)
                dve.tensor_copy(cq[:], psum[:, 0, 0:NT * N_AB].rearrange("p (t h) -> p t h", h=N_AB))
                dve.tensor_copy(ct[0:N_AB, :], psum[0:N_AB, 1, 0:SEQ])
                dve.drain().then_inc(S("fox_cum_ready"), 1)
                softmax(0, smx, mask_fox, 0)
                for g in range(2):
                    dve.wait_ge(S("sb_ln"), g + 1)
                    z = scr[:, :, 0:SCW]
                    wide = lambda m: m[:].unsqueeze(1).broadcast_to([P, 4, SCW])
                    STT(sbb[:], z, 0.0, sba[:], ALU.max, ALU.add)
                    dve.drain()
                    TT(sbb[:], sbb[:], wide(keep_sb), ALU.mult)
                    dve.drain().then_inc(S("sb_sp"), 1)
                    dve.wait_ge(S("sb_exponent"), g + 1)
                    TT(sba[:], z, wide(mask_sb), ALU.add)
                    dve.drain().then_inc(S("sb_masked"), 1)
                dve.wait_ge(S("sb_o"), 1)
                for t in range(NT):
                    dve.tensor_copy(y[:, t, FOX_W:2 * FOX_W], psum[:, 2 + t, :])
                dve.drain()
                dve.sem_inc(S("t_source"), NT)
            if "ab_out" in live:
                operand(4)
                follow_add("ab_out")
                layer_norm(4, 4)

            def up_gated(blocks, r):
                (bg, cg, n0, n, _), (bv, cv, _, _, _) = blocks
                j, nc_ = n0 // NB, n // P
                round_to(cv + (cv - cg) + 2)
                wait_evacuated(dve, bg)
                wait_used(dve, cv + (cv - cg))
                dve.drain()
                TT(uv[:, 0:nc_, :], ug[:, 0:nc_, :], acc_tall(bv % 2, nc_), ALU.mult).then_inc(S(f"acc_free{bv % 2}"), 1)
                dve.drain().then_inc(S("h_ready"), 1)
                split_h(KP + j, j, nc_)

            if "ffn_up" in live:
                operand(5)
                split_loop(dve, "ffn_up", up_gated, me, unroll=True)
            if "ffn_down" in live:
                follow_add("ffn_down")
                layer_norm(5, 6)

            def ple(i, m, r=0):
                operand(m)
                dve.wait_ge(S("ppt_hi_ready"), i + 1)
                TT(ppt_lo[:], scr[:, 0, :].rearrange("p (k n) -> p k n", n=SEQ), ppt_hi[:].bitcast(F32), ALU.subtract)\
                    .then_inc(S("ppt_ready"), 1)
                for q in range(2):
                    (bg, cg, n0, _, _), (bp, cp, _, _, psp) = phase[f"ple{i}"][2 * q:2 * q + 2]
                    round_to(cp + 3, r)
                    wait_evacuated(dve, bg)
                    wait_used(dve, cp + 1, r)
                    for t in range(NT):
                        j = TT(sig[:, t, :], sig[:, t, :], acc[bp % 2][t], ALU.mult)
                    j.then_inc(S(f"acc_free{bp % 2}"), 1)
                    dve.drain()
                    TT(x[:, :, n0:n0 + NB], x[:, :, n0:n0 + NB], sig[:], ALU.add)
                    dve.drain().then_inc(S("ple_added"), 1)

            if "ple0" in live:
                ple(0, 6)
                dve.sem_inc(S("ple_x"), 1)
            if "qkv" in live:
                dve.sem_inc(S("t_source"), NT)
                operand(7)
                follow("qkv")
                wait_phase_evacuated(dve, "qkv")
                dve.wait_ge(S("rope_landed"), 16)
                hd = p2[:, :, 0:SWA_V].rearrange("p t (h n) -> p t h n", n=DH)
                x1, x2 = hd[:, :, :, 0:ROPE_HALF], hd[:, :, :, ROPE_HALF:2 * ROPE_HALF]
                rt = [rtmp[:, k].rearrange("p t (h n) -> p t h n", n=ROPE_HALF) for k in range(4)]
                for t in range(NT):
                    cs = [rope[:, k, t, :].unsqueeze(1).broadcast_to([P, 18, ROPE_HALF]) for k in range(2)]
                    for k, (v, f) in enumerate(((x1, 0), (x2, 1), (x2, 0), (x1, 1))):
                        TT(rt[k][:, t], v[:, t], cs[f], ALU.mult)
                dve.drain()
                TT(x1, rt[0], rt[1], ALU.subtract)
                TT(x2, rt[2], rt[3], ALU.add)
                dve.drain()
                for u in range(2):
                    dve.tensor_copy(kdup[:, :, :, u, :], p2[:, :, SWA_K:SWA_V].rearrange("p t (g n) -> p t g n", n=DH))
                dve.drain().then_inc(S("rotated"), 1)
                dve.wait_ge(S("swa_mask_ready"), 1)
                dve.wait_ge(S("sink_landed"), 16)
                for g in range(2):
                    softmax(1 + g, smx2, mask_swa, g * 8 * DH)
                dve.sem_inc(S("t_source"), NT)
            if "c_out" in live:
                operand(8)
                follow_add("c_out")
                layer_norm(6, 8)

            def splits(k0, k1, r):
                for k in range(k0, k1):
                    split_chunk(N_BEFORE_MOE + k, r, item_width(k))

            def select(n):
                for t in range(NT):
                    dve.tensor_copy(cur[:, t:t + 1], slotc[:, bass.ds(n + t * ITEMS, 1)])
                    dve.tensor_copy(cur[:, 2 + t:3 + t], combc[:, bass.ds(n + t * ITEMS, 1)])
                dve.drain()
                for t in range(NT):
                    TS(sel[:, t, :], slot_row[:], cur[:, t:t + 1], None, ALU.is_equal)
                dve.drain().then_inc(S("sel_ready"), 1)

            def take_item(n, k, r):
                dve.wait_ge(S("gathered"), 3 * n + 2)
                dve.tensor_copy(xg_lo[:], scr[:, 0:2, :].rearrange("p b (k n) -> p (b k) n", n=P)).then_inc(S("xg_ready"), 1)
                splits(k, k + 2, r)

            def item(i):
                c0, r = N_BEFORE_MOE, i * R_ITEM
                for j in range(MOE_PAIRS):
                    splits(4 * j + 4, 4 * j + 6, r)
                    if j:
                        lo_h(i, j - 1)
                    dve.wait_ge(S("mg_ready"), MOE_PAIRS * i + j + 1)
                    wait_used(dve, c0 + 4 * j + 4, r)
                    if j >= 2:
                        dve.wait_ge(S("mh_t"), MOE_PAIRS * i + j - 1)
                    TT(mh[:, j % 2, :], mg[:], psum[:, 2 * (j % 2) + 1, :], ALU.mult).then_inc(S("mh_ready"), 1)
                    splits(4 * j + 6, 4 * j + 8, r)
                    if j == 1:
                        dve.wait_ge(S("gathered"), 3 * i + 3)
                        select(i + 1)
                lo_h(i, MOE_PAIRS - 1)
                k = 4 * MOE_PAIRS + 4
                for n in range(2):
                    end = MOE_UP_CHUNKS + len(MOE_DOWN) * (n + 1)
                    splits(k, end + 2, r)
                    k = end + 2
                    dve.wait_ge(S("ys_hi_ready"), 2 * i + n + 1)
                    o = slice(n * NB, (n + 1) * NB)
                    STT(ys_lo[:, o], psum[:, 4 + n, :], gslot[:, 0:1], ys_hi[:, o].bitcast(F32), ALU.mult, ALU.subtract)\
                        .then_inc(S("ys_ready"), 1)
                for t in range(NT):
                    dve.wait_ge(S("scattered"), 2 * i + t + 1)
                    TT(y[:, t, :], y[:, t, :], psum[:, 2 * t:2 * t + 2, :].rearrange("p b n -> p (b n)"), ALU.add)\
                        .then_inc(S("y_added"), 1)
                take_item(i + 1, k, r)
                dve.drain()

            def lo_h(i, j):
                dve.wait_ge(S("mh_hi_ready"), MOE_PAIRS * i + j + 1)
                TT(mh_lo[:, 4 * j:4 * j + 4, :], psum[:, 6 + j % 2, :].rearrange("p (k n) -> p k n", n=P),
                   mh_hi[:, 4 * j:4 * j + 4, :].bitcast(F32), ALU.subtract).then_inc(S("mh_split"), 1)

            tok = lambda c, w=N_EXP: route[:, c:c + NT * w].rearrange("p (t e) -> p t e", e=w)
            logits, top8, hot1, hot2, comb, selm, rank1 = (tok(16 * k) for k in range(7))
            top8 = tok(16)
            slotc, combc = route[:, 112:135], route[:, 148:171]
            gap, gap_e, g1, g2 = (route[:, c:c + 2] for c in (140, 142, 144, 146))
            row8 = lambda k: route[:, 170 + 8 * k:178 + 8 * k]
            cnt, over, over_before, pick, tmp8, eid8, one8 = (row8(k) for k in range(7))
            eidf = route[:, 226:230]
            cur = route[:, 230:234]
            idxf = route[:, 234:250].rearrange("p (t e) -> p t e", e=8)

            if "moe" in live:
                operand(9)
                dve.wait_ge(S("xn_hi_ready"), 1)
                TT(xn_lo[:], x[:], xn_hi[:].bitcast(F32), ALU.subtract)
                dve.memset(y[:], 0.0)
                dve.memset(slotc[:, NT * ITEMS:], 0.0)
                dve.sem_inc(S("y_added"), 2)
                dve.memset(one8, 1.0)
                dve.tensor_copy(eid8, slot_row[:, 0:N_EXP])
                dve.wait_ge(S("logits"), 1)
                dve.wait_ge(S("rb_landed"), 16)
                TT(logits, scr[:, 0, 0:NT * N_EXP].rearrange("p (t e) -> p t e", e=N_EXP),
                   rb_row[:].unsqueeze(1).broadcast_to([P, NT, N_EXP]), ALU.add)
                dve.drain()
                for t in range(NT):
                    dve.max(top8[:, t, :], logits[:, t, :])
                dve.drain()
                TT(gap.unsqueeze(2), top8[:, :, 1:2], top8[:, :, 0:1], ALU.subtract)
                for t in range(NT):
                    dve.max_index(route_u[:, t, :], top8[:, t, :], logits[:, t, :])
                dve.drain().then_inc(S("top_gap"), 1)
                dve.tensor_copy(idxf, route_u[:])
                dve.drain()
                for k, hot in ((0, hot1), (1, hot2)):
                    TT(hot, eid8.unsqueeze(1).broadcast_to([P, NT, N_EXP]), idxf[:, :, k:k + 1].broadcast_to([P, NT, N_EXP]),
                       ALU.is_equal)
                dve.drain()
                TT(selm, hot1, hot2, ALU.add)
                dve.drain().then_inc(S("chosen"), 1)
                dve.wait_ge(S("top_exp"), 1)
                TS(g2, gap_e, 1.0, None, ALU.add)
                dve.drain()
                dve.reciprocal(g1, g2)
                dve.drain()
                TT(g2, g1, gap_e, ALU.mult)
                dve.drain()
                for hot, g in ((hot1, g1), (hot2, g2)):
                    TT(hot, hot, g.unsqueeze(2).broadcast_to([P, NT, N_EXP]), ALU.mult)
                dve.drain()
                TT(comb, hot1, hot2, ALU.add)
                dve.wait_ge(S("ranks"), 1)
                TS(rank1, scr[:, 1, 0:NT * N_EXP].rearrange("p (t e) -> p t e", e=N_EXP), 1.0, None, ALU.add)
                dve.tensor_copy(cnt, scr[:, 1, 16:24])
                dve.drain()
                TT(rank1, rank1, selm, ALU.mult)
                TS(over, cnt, float(P), None, ALU.is_gt)
                dve.drain()
                dve.tensor_tensor_scan(over_before, one8, over, 0.0, ALU.mult, ALU.add)
                sc, cc_ = (v.rearrange("p (t i) -> p t i", i=ITEMS) for v in (slotc[:, 0:NT * ITEMS], combc[:, 0:NT * ITEMS]))
                TS(sc[:, :, 0:N_EXP], rank1, -1.0, None, ALU.add)
                dve.tensor_copy(cc_[:, :, 0:N_EXP], comb)
                dve.drain()
                TT(over_before, over_before, over, ALU.subtract)
                dve.reduce_sum(eidf[:, 3:4], over, AX_X)
                dve.drain()
                TS(eidf[:, 3:4], eidf[:, 3:4], float(N_EXP), None, ALU.add)
                for k in range(ITEMS - N_EXP):
                    TS(pick, over_before, float(k), None, ALU.is_equal)
                    dve.drain()
                    TT(pick, pick, over, ALU.mult)
                    dve.drain()
                    TT(tmp8, pick, eid8, ALU.mult)
                    dve.drain()
                    dve.reduce_sum(eidf[:, k:k + 1], tmp8, AX_X)
                    for src, dst in ((rank1, sc), (comb, cc_)):
                        TT(hot1, src, pick.unsqueeze(1).broadcast_to([P, NT, N_EXP]), ALU.mult)
                        dve.drain()
                        dve.reduce_sum(dst[:, :, N_EXP + k], hot1, AX_X)
                        dve.drain()
                    TS(sc[:, :, N_EXP + k], sc[:, :, N_EXP + k], -1.0 - P, None, ALU.add)
                    dve.drain()
                dve.tensor_copy(route_i[:], eidf)
                dve.drain().then_inc(S("routed"), 1)
                n_items = dve.value_load(route_i[0:1, 3:4], min_val=N_EXP, max_val=ITEMS)
                select(0)
                splits(0, 2, 0)
                take_item(0, 2, 0)
                with dve.Fori(0, ITEMS) as i:
                    with dve.If(i < n_items):
                        item(i)
                    dve.end_ifs()
                me.cap = N_STATIC
                dve.sem_inc(S("moe_x"), 1)
                for h in range(2):
                    add_half(h, lambda t: y[:, t, h * NB:(h + 1) * NB])
                layer_norm(7, 10)
            if "ple1" in live:
                r = n_items * R_ITEM
                me.chunk += RING
                ple(1, 10, r)
            dve.drain()
            dve.sem_inc(S("x_done"), 1)

        @block.tensor
        def _(pe):
            pe.sem_inc(S("w_used"), RING)
            mm = pe.matmul

            def products(bl, r, hi, lo, r4=None, used=None):
                bb, cc, n0, n, ps = bl
                ra = 0 if r4 is not None else r
                rc = r if r4 is None else r4
                pe.wait_ge(S(f"acc_free{bb % 2}"), bb // 2 + 1 + ra)
                kmax = ps[-1][0] + ps[-1][1] - 1
                for i, (k0, nk, _) in enumerate(ps):
                    slot = (cc + i) % RING
                    pe.wait_ge(S("lo_ready"), RING + cc + i + 1 + RING * rc)
                    if used:
                        used(k0)
                    for kk in range(nk):
                        k = k0 + kk
                        wh = w_hi[:, slot, kk * n:(kk + 1) * n]
                        wl = w_lo[:, slot, kk * n:(kk + 1) * n]
                        for t in range(NT):
                            o = acc[bb % 2][t][:, 0:n]
                            mm(o, hi(k, t), wh, start=(k == 0), stop=False)
                            mm(o, hi(k, t), wl, start=False, stop=False)
                            m = mm(o, lo(k, t), wh, start=False, stop=(k == kmax))
                    m.then_inc(S("w_used"), 1)

            def products_t(bl, r):
                bb, cc, n0, n, ps = bl
                pe.wait_ge(S(f"acc_free{bb % 2}"), bb // 2 + 1 + r)
                for i, (k0, nk, _) in enumerate(ps):
                    slot = (cc + i) % RING
                    pe.wait_ge(S("lo_ready"), RING + cc + i + 1 + RING * r)
                    for kk in range(nk):
                        k = k0 + kk
                        for c_ in range(n // P):
                            cols = slice(kk * n + c_ * P, kk * n + (c_ + 1) * P)
                            o = acc_t(bb % 2, c_)
                            mm(o, w_hi[:, slot, cols], xt_hi[:, k, :], start=(k == 0 and c_ % 2 == 0), stop=False,
                               skip_group_check=True)
                            mm(o, w_hi[:, slot, cols], xt_lo[:, k, :], start=False, stop=False, skip_group_check=True)
                            m = mm(o, w_lo[:, slot, cols], xt_hi[:, k, :], start=False, stop=(k == KD - 1),
                                   skip_group_check=True)
                    m.then_inc(S("w_used"), 1)

            xh = lambda k, t: xt_hi[:, k, t * P:(t + 1) * P]
            xl = lambda k, t: xt_lo[:, k, t * P:(t + 1) * P]
            hh = lambda k, t: ht_hi[:, k, t * P:(t + 1) * P]
            hl = lambda k, t: ht_lo[:, k, t * P:(t + 1) * P]

            def turn(o, i):
                return pe.transpose(o, i, ident[:])

            def operand(m, src):
                if m == 0:
                    pe.wait_ge(S("ident_ready"), 1)
                for t in range(NT):
                    pe.wait_ge(S("t_source"), NT * m + t + 1)
                    for g in range(2):
                        for k in range(4):
                            i = turn(scr[:, 2 * t + g, k * P:(k + 1) * P], src[:, t, (4 * g + k) * P:(4 * g + k + 1) * P])
                        i.then_inc(S("t_ready"), 1)
                pe.wait_ge(S("xt_ready"), 4 * (m + 1))

            def project(name, hi, lo, used=None):
                split_loop(pe, name, lambda blocks, r: [products(b_, r, hi, lo, used=used) for b_ in blocks])

            operand(0, y)
            project("w_in", xh, xl)
            wait_evacuated(pe, 6)
            wait_evacuated(pe, 5)
            for t in range(NT):
                i = turn(scr[0:2 * RANK, 0, t * P:(t + 1) * P], p0[:, t, C_LR:C_LR + 2 * RANK])
            i.then_inc(S("lr_t"), 1)
            for f in range(4):
                for t in range(NT):
                    i = turn(scr[:, 1 + f // 2, (f % 2) * SEQ + t * P:(f % 2) * SEQ + (t + 1) * P],
                             p0[:, t, C_Q + f * P:C_Q + (f + 1) * P])
            i.then_inc(S("qk_t"), 1)
            pe.wait_ge(S("lrt_ready"), 1)
            pe.wait_ge(S("lrt_ones"), 1)
            pe.wait_ge(S("gate_w_landed"), 64)
            for t in range(NT):
                i = mm(psum[:, t, :], lrt[:, t * P:(t + 1) * P], gate_w[:], start=True, stop=True)
            i.then_inc(S("gate_pre"), 1)
            pe.wait_ge(S("logd_ready"), 1)
            pe.wait_ge(S("tri_ready"), 1)
            for g in range(4):
                for t in range(NT):
                    o = (g % 2) * SEQ + t * P
                    i = mm(psum[:, 2 + g // 2, o:o + P], logd[:, t, g * P:(g + 1) * P], (tri_fwd if g < 2 else tri_bwd)[:],
                           start=True, stop=True)
            i.then_inc(S("cum_t"), 1)
            pe.wait_ge(S("q_in"), 1)
            pe.wait_ge(S("k_in"), 1)
            for d in range(2):
                for h in range(GLA_HEADS):
                    lane = slice(HEAD_K * (h % 2), HEAD_K * (h % 2 + 1))
                    for t in range(NT):
                        o = ((h // 2) * NT + t) * P
                        i = mm(psum[:, 2 * d + h % 2, o:o + P], e2[lane, 2 * d + h // 2, t * P:(t + 1) * P],
                               e1[lane, 2 * d + h // 2, t * P:(t + 1) * P], start=True, stop=True)
                i.then_inc(S("gla_scores"), 1)
            pe.wait_ge(S("k_out"), 1)
            for t in range(NT):
                for g in range(4):
                    i = turn(scr[:, 3 * t, g * P:(g + 1) * P], e3[:, g, t * P:(t + 1) * P])
                i.then_inc(S("kout_t"), 1)
            pe.wait_ge(S("kout_ready"), 2)
            for g in range(4):
                for c_ in ((0, 1, 2) if g < 2 else (3, 2, 1)):
                    lane = slice(GLA_CHUNK * (c_ % 2), GLA_CHUNK * (c_ % 2 + 1))
                    for hp in range(2):
                        h = 2 * (g % 2) + hp
                        i = mm(kv_place(g, c_)[HEAD_K * hp:HEAD_K * (hp + 1), :],
                               kout[lane, c_ // 2, g * P + hp * HEAD_K:g * P + (hp + 1) * HEAD_K],
                               p0[lane, c_ // 2, C_V + h * HEAD_V:C_V + (h + 1) * HEAD_V], start=True, stop=True)
            i.then_inc(S("gla_kv"), 1)
            pe.wait_ge(S("st_ready"), 2)
            pe.wait_ge(S("q_half_ready"), 1)
            pe.wait_ge(S("state_ready"), 1)
            for t in range(NT):
                for h in range(GLA_HEADS):
                    o = psum[:, 2 * t + h % 2, (h // 2) * HEAD_V:(h // 2 + 1) * HEAD_V]
                    v = p0[:, t, C_V + h * HEAD_V:C_V + (h + 1) * HEAD_V]
                    lane = slice(HEAD_K * (h % 2), HEAD_K * (h % 2 + 1))
                    parts = [(st[:, d, h % 2, (h // 2) * NT + t, :], v) for d in range(2)]
                    for c_ in (2 * t, 2 * t + 1):
                        for d in range(2):
                            if c_ != (0 if d == 0 else 3):
                                g = 2 * d + h // 2
                                parts.append((q_half[lane, c_ % 2, g, t * P:(t + 1) * P], state[lane, g, c_, :]))
                    for k, (l, r_) in enumerate(parts):
                        i = mm(o, l, r_, start=(k == 0), stop=(k == len(parts) - 1))
                i.then_inc(S("gla_o"), 1)
            operand(1, y)
            project("w_out", xh, xl)

            def up(blocks, r):
                for b_ in blocks:
                    products_t(b_, r)

            if "w_up" in live:
                pe.wait_ge(S("cw_landed"), 16)
                wait_phase_evacuated(pe, "w_out")
                for j in range(3):
                    i = pe.transpose(psum[:, 0, j * 2 * KF:(j + 1) * 2 * KF], cw_rows[:, j, :], ident[0:2 * KF, 0:2 * KF])
                i.then_inc(S("cw_turned"), 1)
                operand(2, y)
                pe.wait_ge(S("cw_ready"), 1)
                split_loop(pe, "w_up", up)
            if "w_down" in live:
                project("w_down", hh, hl, lambda k0: pe.wait_ge(S("ht_ready"), k0 // 4 + 1))

            def attend(q, queries, keys, values, pt_):
                def pv(h):
                    pe.wait_ge(S("at_pt"), 8 * q + h + 1)
                    o = slice(h * DH, (h + 1) * DH)
                    mm(psum[:, 2, o], pt_[:, h % 2, 0:P], values(h, 0), start=True, stop=True)
                    mm(psum[:, 3, o], pt_[:, h % 2, P:SEQ], values(h, 0), start=True, stop=False)
                    return mm(psum[:, 3, o], pt_[:, h % 2, SEQ:SCW], values(h, 1), start=False, stop=True)

                for h in range(8):
                    if q or h >= 4:
                        pe.wait_ge(S("at_s"), 8 * q + h - 3 if h >= 4 else 8 * q)
                    b_ = scr[:, h % 4, :]
                    for t, (c0, c1) in enumerate(((0, P), (P, SCW))):
                        i = mm(b_[:, c0:c1], queries(h)[:, t * P:(t + 1) * P], keys(h)[:, 0:c1 - c0], start=True, stop=(q > 0))
                        if q == 0:
                            i = mm(b_[:, c0:c1], neg_head[:, h, :], ct[:, 0:c1 - c0], start=False, stop=True)
                    i.then_inc(S("at_qk"), 1)
                if q:
                    pe.wait_ge(S("at_y"), q)
                for h in range(8):
                    pe.wait_ge(S("at_p"), 8 * q + h + 1)
                    if h >= 2:
                        pe.wait_ge(S("at_pt"), 8 * q + h - 1)
                    for k in range(3):
                        i = turn(psum[:, h % 2, k * P:(k + 1) * P], s_all[:, h, k * P:(k + 1) * P])
                    i.then_inc(S("at_t"), 1)
                    if h:
                        pv(h - 1)
                pv(7).then_inc(S("at_o"), 1)

            if "ab_in" in live:
                operand(3, x)
                project("ab_in", xh, xl)
                wait_phase_evacuated(pe, "ab_in")
                pe.wait_ge(S("lf_ready"), 1)
                l0, l1 = lf[:, 2, 0, :], lf[:, 2, 1, :]
                mm(psum[:, 0, 0:N_AB], tri_incl[:], l0, start=True, stop=True)
                mm(psum[:, 0, N_AB:2 * N_AB], ones[:], l0, start=True, stop=False)
                mm(psum[:, 0, N_AB:2 * N_AB], tri_incl[:], l1, start=False, stop=True)
                mm(psum[0:N_AB, 1, 0:P], l0, tri_incl[:], start=True, stop=True)
                mm(psum[0:N_AB, 1, P:SEQ], l0, ones[:], start=True, stop=False)
                mm(psum[0:N_AB, 1, P:SEQ], l1, tri_incl[:], start=False, stop=True).then_inc(S("lf_cum"), 1)

                def turn_qk(g, cq_, ck_):
                    for tile in range(4):
                        for f in range(2):
                            for t in range(NT):
                                c_ = (cq_ if tile < 2 else ck_) + (2 * (tile % 2) + f) * P
                                i = turn(scr[:, tile, f * SEQ + t * P:f * SEQ + (t + 1) * P], p1[:, t, c_:c_ + P])
                        i.then_inc(S("ab_t"), 1)
                    pe.wait_ge(S("qk1_ready"), 4 * (g + 1))

                def qh(h):
                    return qk1[DH * (h % 2):DH * (h % 2 + 1), h // 2, :]

                def kh(h):
                    return qk1[DH * (h % 2):DH * (h % 2 + 1), 4 + h // 2, :]

                turn_qk(0, AB_QA, AB_KA)
                pe.wait_ge(S("fox_cum_ready"), 1)
                attend(0, qh, kh, lambda h, t: p1[:, t, AB_VA + h * DH:AB_VA + (h + 1) * DH], pt)
                pe.wait_ge(S("at_s"), 8)
                turn_qk(1, AB_QS, AB_KS)
                pe.wait_ge(S("at_y"), 1)
                for g in range(2):
                    if g:
                        pe.wait_ge(S("sb_masked"), g)
                    for u in range(4):
                        h = 4 * g + u
                        mm(scr[:, u, 0:SEQ], kh(h)[:, 0:P], qh(h), start=True, stop=True)
                        i = mm(scr[:, u, SEQ:SCW], kh(h)[:, P:SEQ], qh(h)[:, P:SEQ], start=True, stop=True)
                    i.then_inc(S("sb_z"), 1)
                    pe.wait_ge(S("sb_sp"), g + 1)
                    for u in range(4):
                        s0, s1 = sbb[:, u, 0:SEQ], sbb[:, u, SEQ:SCW]
                        h = 4 * g + u
                        mm(scr[:, u, 0:SEQ], kh(h)[:, 0:P], qh(h), start=True, stop=False)
                        mm(scr[:, u, P:SEQ], neg_ones[:], s1, start=False, stop=False, skip_group_check=True)
                        mm(scr[:, u, 0:SEQ], neg_from[:], s0, start=False, stop=True)
                        mm(scr[:, u, SEQ:SCW], kh(h)[:, P:SEQ], qh(h)[:, P:SEQ], start=True, stop=False)
                        i = mm(scr[:, u, SEQ:SCW], neg_from[:], s1, start=False, stop=True)
                    i.then_inc(S("sb_exponent"), 1)
                    pe.wait_ge(S("sb_a"), g + 1)
                    for u in range(4):
                        h = 4 * g + u
                        o = slice(h * DH, (h + 1) * DH)
                        v = lambda t: p1[:, t, AB_VS + h * DH:AB_VS + (h + 1) * DH]
                        mm(psum[:, 2, o], sba[:, u, 0:P], v(0), start=True, stop=True)
                        mm(psum[:, 3, o], sba[:, u, P:SEQ], v(0), start=True, stop=False)
                        i = mm(psum[:, 3, o], sba[:, u, SEQ:SCW], v(1), start=False, stop=True)
                i.then_inc(S("sb_o"), 1)
            if "ab_out" in live:
                operand(4, y)
                project("ab_out", xh, xl)

            if "ffn_up" in live:
                operand(5, x)
                split_loop(pe, "ffn_up", up)
            if "ffn_down" in live:
                project("ffn_down", hh, hl, lambda k0: pe.wait_ge(S("ht_ready"), KP + k0 // 4 + 1))

            def ple(i, m, r=0):
                operand(m, x)
                pe.wait_ge(S("p_landed"), 16 * (i + 1))
                for k in range(2):
                    for t in range(NT):
                        j = turn(scr[:, 0, k * SEQ + t * P:k * SEQ + (t + 1) * P], pn[:, t, k * P:(k + 1) * P])
                j.then_inc(S("p_t"), 1)
                for q in range(4):
                    if q == 1:
                        pe.wait_ge(S("ppt_ready"), i + 1)
                    hi, lo = (xh, xl) if q % 2 == 0 else (lambda k, t: ppt_hi[:, k, t * P:(t + 1) * P],
                                                         lambda k, t: ppt_lo[:, k, t * P:(t + 1) * P])
                    products(phase[f"ple{i}"][q], 0, hi, lo, r4=r)

            if "ple0" in live:
                ple(0, 6)
            if "qkv" in live:
                operand(7, x)
                project("qkv", xh, xl)
                pe.wait_ge(S("rotated"), 1)
                for j in range(3):
                    if j == 2:
                        pe.wait_ge(S("qk2_ready"), 1)
                    for f in range(4 if j < 2 else 2):
                        for t in range(NT):
                            src = p2[:, t, (4 * j + f) * P:(4 * j + f + 1) * P] if j < 2 else \
                                kdup[:, t, f, :, :].rearrange("p u n -> p (u n)")
                            o = (f % 2) * SEQ + t * P
                            i = turn(scr[:, (2 * j if j < 2 else 0) + f // 2, o:o + P], src)
                    i.then_inc(S("swa_t"), 1)
                pe.wait_ge(S("qk2_ready"), 3)
                for g in range(2):
                    lane = lambda h: slice(DH * (h % 2), DH * (h % 2 + 1))
                    attend(1 + g, lambda h: qk2[lane(h), 4 * g + h // 2, :], lambda h: qk2[lane(h), 8 + g, :],
                           lambda h, t: p2[:, t, SWA_V + g * DH:SWA_V + (g + 1) * DH], pt2)
            if "c_out" in live:
                operand(8, y)
                project("c_out", xh, xl)

            def gather(part, b0):
                for k in range(KD):
                    for t in range(NT):
                        m = mm(psum[:, b0 + k // 4, (k % 4) * P:(k % 4 + 1) * P], part[:, t, k * P:(k + 1) * P],
                               sel[:, t, :], start=(t == 0), stop=(t == NT - 1))
                m.then_inc(S("gathered"), 1)

            def turn_sel(n):
                pe.wait_ge(S("xg_hi_ready"), n + 1)
                for t in range(NT):
                    turn(psum[:, 6, t * P:(t + 1) * P], sel[:, t, :].bitcast(F32))
                for t in range(NT):
                    m = mm(psum[:, 6, SEQ:SEQ + 1], sel[:, t, :].bitcast(F32), cur_pe[:, t:t + 1], start=(t == 0), stop=(t == NT - 1))
                m.then_inc(S("gathered"), 1)

            def item(i):
                c0, r = N_BEFORE_MOE, i * R_ITEM
                pe.wait_ge(S("xg_ready"), i + 1)

                def chunk(k, o, hi, lo, k0, nk, first, last):
                    pe.wait_ge(S("lo_ready"), RING + c0 + k + 1 + RING * r)
                    slot = (c0 + k) % RING
                    for kk in range(nk):
                        wh, wl = (w[:, slot, kk * NB:(kk + 1) * NB] for w in (w_hi, w_lo))
                        q = k0 + kk
                        mm(o, hi[:, q, :], wh, start=(q == first), stop=False)
                        mm(o, hi[:, q, :], wl, start=False, stop=False)
                        m = mm(o, lo[:, q, :], wh, start=False, stop=(q == last))
                    m.then_inc(S("w_used"), 1)

                def turn_h(j):
                    if j == 0:
                        pe.wait_ge(S("selt_ready"), i + 1)
                    pe.wait_ge(S("mh_ready"), MOE_PAIRS * i + j + 1)
                    if j >= 2:
                        pe.wait_ge(S("mh_split"), MOE_PAIRS * i + j - 1)
                    for k in range(4):
                        m = turn(psum[:, 6 + j % 2, k * P:(k + 1) * P], mh[:, j % 2, k * P:(k + 1) * P])
                    m.then_inc(S("mh_t"), 1)

                for j in range(MOE_PAIRS):
                    if j >= 2:
                        pe.wait_ge(S("mh_ready"), MOE_PAIRS * i + j - 1)
                    else:
                        pe.wait_ge(S("y_added"), 2 * i + j + 1)
                    for h in range(2):
                        for u in range(2):
                            chunk(4 * j + 2 * h + u, psum[:, 2 * (j % 2) + h, :], xg_hi, xg_lo, 4 * u, 4, 0, KD - 1)
                        if h == 0 and j:
                            turn_h(j - 1)
                k = MOE_UP_CHUNKS
                for n in range(2):
                    k0 = 0
                    for nk in MOE_DOWN:
                        pe.wait_ge(S("mh_split"), MOE_PAIRS * i + k0 // 4 + 1)
                        chunk(k, psum[:, 4 + n, :], mh_hi, mh_lo, k0, nk, 0, KE - 1)
                        if k == MOE_UP_CHUNKS:
                            turn_h(MOE_PAIRS - 1)
                        k, k0 = k + 1, k0 + nk
                pe.wait_ge(S("sel_ready"), i + 2)
                gather(xn_hi, 6)
                pe.wait_ge(S("ys_ready"), 2 * i + 2)
                for t in range(NT):
                    for n in range(2):
                        for q, part in enumerate((ys_hi, ys_lo)):
                            m = mm(psum[:, 2 * t + n, :], selt[:, t * P:(t + 1) * P], part[:, n * NB:(n + 1) * NB],
                                   start=(q == 0), stop=(q == 1))
                    m.then_inc(S("scattered"), 1)
                gather(xn_lo, 4)
                turn_sel(i + 1)

            cur_pe = route[:, 232:234]
            if "moe" in live:
                operand(9, x)
                pe.wait_ge(S("rw_landed"), 16)
                for t in range(NT):
                    for k in range(KD):
                        for q, part in enumerate((xt_hi, xt_lo)):
                            m = mm(scr[:, 0, t * N_EXP:(t + 1) * N_EXP], part[:, k, t * P:(t + 1) * P].bitcast(F32), rw[:, k, :],
                                   start=(k == 0 and q == 0), stop=(k == KD - 1 and q == 1))
                m.then_inc(S("logits"), 1)
                pe.wait_ge(S("chosen"), 1)
                sm = lambda t: route[:, 80 + 8 * t:88 + 8 * t]
                mm(scr[:, 1, 0:8], tri_excl[:], sm(0), start=True, stop=True)
                mm(scr[:, 1, 8:16], ones[:], sm(0), start=True, stop=False)
                mm(scr[:, 1, 8:16], tri_excl[:], sm(1), start=False, stop=True)
                mm(scr[:, 1, 16:24], ones[:], sm(0), start=True, stop=False)
                mm(scr[:, 1, 16:24], ones[:], sm(1), start=False, stop=True).then_inc(S("ranks"), 1)
                pe.wait_ge(S("routed"), 1)
                n_items = pe.value_load(route_i[0:1, 3:4], min_val=N_EXP, max_val=ITEMS)
                pe.wait_ge(S("sel_ready"), 1)
                gather(xn_hi, 6)
                gather(xn_lo, 4)
                turn_sel(0)
                with pe.Fori(0, ITEMS) as i:
                    with pe.If(i < n_items):
                        item(i)
                    pe.end_ifs()
            if "ple1" in live:
                ple(1, 10, n_items * R_ITEM)


_INS = ["x", "norm_mix_pre", "norm_mix_post", "norm_ffn_pre", "norm_ffn_post", "w_in", "conv_a", "gate_up_fwd",
        "gate_bias_fwd", "gate_up_bwd", "gate_bias_bwd", "gla_head_norm", "w_out", "w_up", "conv_ffn", "w_down",
        "p_2", "ln_mix_g_2", "ln_mix_b_2", "ln_ffn_g_2", "ln_ffn_b_2", "ab_w_in_2", "ab_b_f_2", "ab_w_out_2",
        "c_w_qkv_2", "c_sinks_2", "c_w_out_2", "ffn_w_gate_up_2", "ffn_w_down_2", "router_w_2", "router_b_2",
        "moe_w_gate_up_2", "moe_w_down_2", "ple_w_gate_2", "ple_w_proj_2"]
UPTO = "end"


def kernel(**inputs):
    import numpy as np
    import concourse.bacc as bacc
    from concourse.bass_utils import run_bass_kernel_spmd as run

    nc = bacc.Bacc("TRN2", target_bir_lowering=False, num_devices=1)
    arrays, args = {}, {}
    for name in _INS:
        arr = np.ascontiguousarray(inputs[name])
        arrays[f"in_{name}"] = arr
        args[name] = nc.dram_tensor(f"in_{name}", arr.shape, mybir.dt.from_np(arr.dtype), kind="ExternalInput").ap()
    inv = np.float32(500000.0) ** (-np.arange(ROPE_HALF, dtype=np.float32) * np.float32(2.0) / np.float32(16.0))
    ang = np.arange(SEQ, dtype=np.float32)[:, None] * inv[None, :].astype(np.float32)
    arrays["in_rope"] = np.stack([np.cos(ang), np.sin(ang)]).astype(np.float32)
    args["rope"] = nc.dram_tensor("in_rope", (2, SEQ, ROPE_HALF), F32, kind="ExternalInput").ap()
    out = nc.dram_tensor("out", (1, SEQ, D), F32, kind="ExternalOutput").ap()
    build(nc, args, out, UPTO)
    r = run(nc, [arrays], core_ids=[0])
    return r.results[0]["out"]
```

```python
from contextlib import ExitStack

import concourse.bass as bass
from concourse import mybir

ALU = mybir.AluOpType
ACT = mybir.ActivationFunctionType
F32 = mybir.dt.float32
F32R = mybir.dt.float32r
I32 = mybir.dt.int32
U32 = mybir.dt.uint32
AX_X = mybir.AxisListType.X

P = 128
SEQ, D = 256, 1024
NT = SEQ // P
KD = D // P
NB = 512
RING = 4
CHUNK = 2048

D_HALF = 512
GLA_HEADS, HEAD_K, HEAD_V, GLA_CHUNK, RANK = 4, 64, 128, 64, 16
N_GK = GLA_HEADS * HEAD_K
C_GB, C_GC, C_GV, C_Q, C_K, C_V, C_GO, C_LR = 0, 512, 1024, 1536, 1792, 2048, 2560, 3072
D_IN = 3104
D_FF = 2816
KF = D_FF // P
KP = -(-D_FF // 512)
RMS_EPS, LN_EPS = 1e-6, 1e-5
DH = 64
N_AB = 8
FOX_W = N_AB * DH
AB_IN = 6 * FOX_W + N_AB
AB_QA, AB_KA, AB_VA, AB_FA = 0, FOX_W, 2 * FOX_W, 3 * FOX_W
AB_QS, AB_KS, AB_VS = 3 * FOX_W + N_AB, 4 * FOX_W + N_AB, 5 * FOX_W + N_AB
N_SWA, N_KV = 16, 2
SWA_IN = (N_SWA + 2 * N_KV) * DH
SWA_K, SWA_V = N_SWA * DH, (N_SWA + N_KV) * DH
ROPE_HALF = 8
N_EXP, D_EXP, D_PLE = 8, 3584, 256
KE = D_EXP // P
ITEMS = N_EXP + 3
ALPHA = 4.0 ** 0.25
SB_SETS = 3
SCW = 3 * P
NEG = -1.0e30
DECAY = 1.0 / 16.0


N_STREAM = ["w_lr", "w_in", "w_out", "w_up", "w_down", "ab_in", "ab_out", "ffn_up", "ffn_down", "ple0", "qkv", "c_out",
            "moe", "ple1"]


def weight_plan(w):

    def wide(m, k, n0, n):
        step = min(k, CHUNK // n) if n < NB else CHUNK // NB
        return (n0, n, [(k0, min(step, k - k0), m) for k0 in range(0, k, step)])

    def project(m, k, n):
        return [wide(m, k, n0, min(NB, n - n0)) for n0 in range(0, n, NB)]

    def gated(m):
        out = []
        for n0 in range(0, D_FF, NB):
            n = min(NB, D_FF - n0)
            out += [wide(m, KD, n0, n), wide(m, KD, D_FF + n0, n)]
        return out

    def ple(i):
        return [wide(w["ple_proj"][i], D_PLE // P, n0, NB) for n0 in range(0, D, NB)] + \
            [wide(w["ple_gate"][i], KD, n0, NB) for n0 in range(0, D, NB)]

    return [
        ("w_lr", [wide(w["w_in"], KD, C_LR, 2 * RANK)]),
        ("w_in", project(w["w_in"], KD, C_LR)), ("w_out", project(w["w_out"], KD, D)),
        ("w_up", gated(w["w_up"])), ("w_down", project(w["w_down"], KF, D)),
        ("ab_in", project(w["ab_in"], KD, AB_IN)), ("ab_out", project(w["ab_out"], KD, D)),
        ("ffn_up", gated(w["ffn_up"])), ("ffn_down", project(w["ffn_down"], KF, D)),
        ("ple0", ple(0)),
        ("qkv", project(w["qkv"], KD, SWA_IN)), ("c_out", project(w["c_out"], KD, D)),
        ("moe", []), ("ple1", ple(1)),
    ]


MOE_PAIRS = D_EXP // NB
MOE_DOWN = [4] * 6 + [2, 2]
MOE_UP_CHUNKS = MOE_PAIRS * 4
MOE_CHUNKS = MOE_UP_CHUNKS + 2 * len(MOE_DOWN)


def build(nc, a, out, upto="end"):
    weights = dict(
        w_in=a["w_in"][0], w_out=a["w_out"][0], w_up=a["w_up"][0], w_down=a["w_down"][0],
        ab_in=a["ab_w_in_2"][0], ab_out=a["ab_w_out_2"][0], ffn_up=a["ffn_w_gate_up_2"][0],
        ffn_down=a["ffn_w_down_2"][0], qkv=a["c_w_qkv_2"][0], c_out=a["c_w_out_2"][0],
        ple_gate=[a["ple_w_gate_2"][0], a["ple_w_gate_2"][1]],
        ple_proj=[a["ple_w_proj_2"][0], a["ple_w_proj_2"][1]],
    )
    moe_up, moe_down = a["moe_w_gate_up_2"][0], a["moe_w_down_2"][0]
    stop = len(N_STREAM) if upto == "end" else N_STREAM.index(upto) + 1
    plan = weight_plan(weights)[:stop]
    live = set(N_STREAM[:stop])

    phase, chunk0 = {}, {}
    c = b = 0
    for name, blocks in plan:
        phase[name], chunk0[name] = [], c
        for n0, n, pieces in blocks:
            phase[name].append((b, c, n0, n, pieces))
            b, c = b + 1, c + len(pieces)
    N_STATIC = c
    width = {cc + i: n * nk for bl in phase.values() for _, cc, _, n, ps in bl for i, (_, nk, _) in enumerate(ps)}
    LOOPS = {"w_in": (3, 2 * NB), "ab_in": (3, 2 * NB), "w_up": (5, NB), "ffn_up": (5, NB)}

    with ExitStack() as ctx:
        free = [-(-nc.sbuf_base // 64) * 64]
        TOP = 229344

        def nbytes(shape):
            n = 4
            for s in shape[1:]:
                n *= s
            return -(-n // 32) * 32

        def at(name, shape, dt, offset):
            assert offset + nbytes(shape) <= TOP, (name, offset + nbytes(shape), TOP)
            return nc.alloc_sbuf_tensor_at(name, shape, dt, offset=offset)

        def sb(name, shape, dt=F32):
            t = at(name, shape, dt, free[0])
            free[0] += nbytes(shape)
            return t

        def layout(first, *specs):
            made = []
            for name, shape, dt in specs:
                made.append(at(name, shape, dt, first))
                first += nbytes(shape)
            return made

        sems = {}

        def S(name):
            if name not in sems:
                sems[name] = ctx.enter_context(nc.semaphore(name))
            return sems[name]

        w_raw = sb("w_raw", [P, RING, CHUNK])
        w_hi = sb("w_hi", [P, RING, CHUNK], F32R)
        w_lo = sb("w_lo", [P, RING, CHUNK], F32R)
        x = sb("x", [P, NT, D])
        y = sb("y", [P, NT, D])
        gain = sb("gain", [P, 2, D])
        ident = sb("ident", [P, P])
        ones = sb("ones", [P, P])
        tri_incl = sb("tri_incl", [P, P])
        tri_excl = sb("tri_excl", [P, P])
        neg_from = sb("neg_from", [P, P])
        neg_ones = sb("neg_ones", [P, P])
        tri_fwd = sb("tri_fwd", [P, P])
        tri_bwd = sb("tri_bwd", [P, P])
        slot_row = sb("slot_row", [P, P])
        head_gain = sb("head_gain", [P, HEAD_V])
        rb_row = sb("rb_row", [P, N_EXP])
        stat = sb("stat", [P, 16])
        bn = sb("bn", [P, NT, 2, 6])
        route = sb("route", [P, 256])
        route_u = sb("route_u", [P, NT, 8], U32)
        route_i = sb("route_i", [P, 4], I32)
        at_xt = free[0]
        at_phase = at_xt + 2 * nbytes([P, KD, SEQ])

        xt_hi, xt_lo = layout(at_xt, ("xt_hi", [P, KD, SEQ], F32R), ("xt_lo", [P, KD, SEQ], F32R))
        (junk,) = layout(at_xt, ("junk", [P, NT, D], F32))

        (p0, logd, tmp0, cum, e1, e2, e3, qk0, conv_w, gate_w, dec, ss8) = layout(
            at_phase, ("p0", [P, NT, D_IN], F32), ("logd", [P, NT, NB], F32), ("tmp0", [P, NT, NB], F32),
            ("cum", [P, 4, SEQ], F32), ("e1", [P, 4, SEQ], F32), ("e2", [P, 4, SEQ], F32),
            ("e3", [P, 4, SEQ], F32), ("qk0", [P, 4, SEQ], F32), ("conv_w", [P, 3, D_HALF], F32),
            ("gate_w", [2 * RANK + 1, 2 * N_GK], F32), ("dec", [P, 4, 4], F32), ("ss8", [P, 3, 8], F32))
        o_logd = at_phase + nbytes([P, NT, D_IN])
        (kout, st, lrt) = layout(
            o_logd, ("kout", [P, NT, NB], F32),
            ("st", [P, 2, 2, 2 * NT, P], F32),
            ("lrt", [2 * RANK + 1, SEQ], F32))
        (state, q_half) = layout(
            at_xt, ("state", [P, 4, 4, HEAD_V], F32), ("q_half", [P, 2, 4, SEQ], F32))
        (ht_hi, ht_lo, ug, uv, cw, cw_rows) = layout(
            at_phase, ("ht_hi", [P, KF, SEQ], F32R), ("ht_lo", [P, KF, SEQ], F32R), ("ug", [P, 4, SEQ], F32),
            ("uv", [P, 4, SEQ], F32), ("cw", [P, 3, 2 * KF], F32), ("cw_rows", [2 * KF, 3, P], F32))
        (p1, qk1, pt, stick, mask_fox, neg_head, ct, fbias, lf, cq, smx, mask_sb, keep_sb) = layout(
            at_phase, ("p1", [P, NT, AB_IN], F32), ("qk1", [P, 8, SEQ], F32), ("pt", [P, 2, SCW], F32),
            ("stick", [P, SB_SETS, 2, SCW], F32), ("mask_fox", [P, SCW], F32), ("neg_head", [P, N_AB, P], F32),
            ("ct", [P, SEQ], F32), ("fbias", [P, N_AB], F32), ("lf", [P, 3, NT, N_AB], F32),
            ("cq", [P, NT, N_AB], F32), ("smx", [P, 6, NT, N_AB], F32), ("mask_sb", [P, SCW], F32),
            ("keep_sb", [P, SCW], F32))
        (s_all,) = layout(at_xt, ("s_all", [P, N_AB, SCW], F32))
        (p2, qk2, pt2, mask_swa, kdup, rope, rtmp, smx2, sink, s_more) = layout(
            at_phase, ("p2", [P, NT, SWA_IN], F32), ("qk2", [P, 10, SEQ], F32), ("pt2", [P, 2, SCW], F32),
            ("mask_swa", [P, SCW], F32), ("kdup", [P, NT, N_KV, 2, DH], F32),
            ("rope", [P, 2, NT, ROPE_HALF], F32), ("rtmp", [P, 4, NT, 18 * ROPE_HALF], F32),
            ("smx2", [P, 2, 6, NT, 8], F32), ("sink", [P, N_SWA], F32), ("s_more", [P, N_AB, SCW], F32))
        (pn, ppt_hi, ppt_lo) = layout(
            TOP - 3 * nbytes([P, NT, D_PLE]), ("pn", [P, NT, D_PLE], F32), ("ppt_hi", [P, 2, SEQ], F32R),
            ("ppt_lo", [P, 2, SEQ], F32R))
        (sig, p_out) = layout(at_phase, ("sig", [P, 2, NT, NB], F32), ("p_out", [P, NT, D], F32))
        (xn_hi, xn_lo, xg_hi, xg_lo, mh_hi, mh_lo, mg, mh, rw) = layout(
            at_phase, ("xn_hi", [P, NT, D], F32R), ("xn_lo", [P, NT, D], F32R), ("xg_hi", [P, KD, P], F32R),
            ("xg_lo", [P, KD, P], F32R), ("mh_hi", [P, KE, P], F32R), ("mh_lo", [P, KE, P], F32R),
            ("mg", [P, NB], F32), ("mh", [P, 2, NB], F32), ("rw", [P, KD, N_EXP], F32))
        (ys_hi, ys_lo, sel, selt, gslot) = layout(
            at_xt, ("ys_hi", [P, D], F32R), ("ys_lo", [P, D], F32R), ("sel", [P, NT, P], F32R),
            ("selt", [P, SEQ], F32R), ("gslot", [P, 1], F32))

        psum = ctx.enter_context(nc.psum_tensor("psum", [P, 8, NB], F32))
        acc = [[psum[:, 2 * s + t, :] for t in range(NT)] for s in range(2)]
        scr = psum[:, 4:8, :]

        def sb_bank(g, u):
            return psum[:, (4, 6, 0)[g % SB_SETS] + u, :]

        def sb_banks(g):
            b_ = (4, 6, 0)[g % SB_SETS]
            return psum[:, b_:b_ + 2, 0:SCW]

        def acc_t(s, c_):
            return psum[:, 2 * s + c_ // 2, (c_ % 2) * SEQ:(c_ % 2 + 1) * SEQ]

        def acc_tall(s, nc_):
            return psum[:, 2 * s:2 * s + -(-nc_ // 2), :].rearrange("p b (f n) -> p (b f) n", n=SEQ)

        N_BEFORE_MOE = chunk0.get("moe", N_STATIC)
        R_ITEM = MOE_CHUNKS // RING

        def item_width(k):
            down = MOE_UP_CHUNKS <= k < MOE_CHUNKS
            return NB * MOE_DOWN[(k - MOE_UP_CHUNKS) % len(MOE_DOWN)] if down else CHUNK

        block = ctx.enter_context(nc.Block())

        class Place:
            chunk, cap, looping = 0, N_BEFORE_MOE, False

        def split_loop(eng, name, body, me=None, unroll=False):
            bl = phase[name]
            if name in LOOPS and not unroll:
                trips, _ = LOOPS[name]
                with eng.Fori(0, trips) as i:
                    if me:
                        me.looping, before = True, me.chunk
                    body(bl[0:2], i)
                if me:
                    assert me.chunk == before + RING
                    me.looping, me.chunk = False, before + RING * trips
                bl = bl[2 * trips:]
            for i in range(0, len(bl), 2):
                body(bl[i:i + 2], 0)

        def ncol(name, n0, r):
            return n0 if isinstance(r, int) else r * LOOPS[name][1] + n0

        def sl(n0, n):
            return slice(n0, n0 + n) if isinstance(n0, int) else bass.ds(n0, n)

        def wait_used(eng, c, r=0):
            eng.wait_ge(S("w_used"), RING + c + RING * r)

        def wait_evacuated(eng, bb, r=0):
            eng.wait_ge(S(f"acc_free{bb % 2}"), bb // 2 + 2 + r)

        def last_block(name):
            return phase[name][-1][0]

        def wait_phase_evacuated(eng, name):
            wait_evacuated(eng, last_block(name))
            if len(phase[name]) > 1:
                wait_evacuated(eng, last_block(name) - 1)

        @block.sync
        def _(sp):
            for t in range(NT):
                sp.dma_start(x[:, t, :], a["x"][0, t * P:(t + 1) * P, :]).then_inc(S(f"x_landed{t}"), 16)

            def load(k, r, src, nk, n):
                sp.wait_ge(S("lo_ready"), k + 1 + RING * r)
                sp.dma_start(w_raw[:, k % RING, 0:nk * n].rearrange("p (k n) -> p k n", n=n), src)\
                  .then_inc(S(f"w_landed{k % RING}"), 16)

            def loads(name, r0=0):
                def body(blocks, r):
                    for _, cc, n0, n, ps in blocks:
                        for i, (k0, nk, m) in enumerate(ps):
                            load(cc + i, r + r0, m[k0 * P:(k0 + nk) * P, sl(ncol(name, n0, r), n)]
                                 .rearrange("(k p) n -> p k n", p=P), nk, n)
                split_loop(sp, name, body)

            for name in N_STREAM[:min(stop, N_STREAM.index("moe"))]:
                loads(name)
            if "moe" in live:
                def expert(e, r):
                    k = N_BEFORE_MOE
                    for j in range(MOE_PAIRS):
                        for n0 in (j * NB, D_EXP + j * NB):
                            for k0 in (0, 4):
                                load(k, r, moe_up[bass.ds(e, 1), k0 * P:(k0 + 4) * P, n0:n0 + NB]
                                     .rearrange("e (k p) n -> p (e k) n", p=P), 4, NB)
                                k += 1
                    for n0 in (0, NB):
                        k0 = 0
                        for nk in MOE_DOWN:
                            load(k, r, moe_down[bass.ds(e, 1), k0 * P:(k0 + nk) * P, n0:n0 + NB]
                                 .rearrange("e (k p) n -> p (e k) n", p=P), nk, NB)
                            k, k0 = k + 1, k0 + nk

                with sp.Fori(0, N_EXP) as i:
                    expert(i, i * R_ITEM)
                sp.wait_ge(S("routed"), 1)
                n_items = sp.value_load(route_i[0:1, 3:4], min_val=N_EXP, max_val=ITEMS)
                for j in range(ITEMS - N_EXP):
                    with sp.If(n_items > N_EXP + j):
                        e = sp.value_load(route_i[0:1, j:j + 1], min_val=0, max_val=N_EXP - 1)
                        expert(e, (N_EXP + j) * R_ITEM)
                    sp.end_ifs()
                if "ple1" in live:
                    loads("ple1", n_items * R_ITEM)
            for q in range(2):
                sp.wait_ge(S("ple_added"), 3 + q)
                sp.dma_start(out[0, :, q * NB:(q + 1) * NB].rearrange("(t p) n -> p t n", p=P), x[:, :, q * NB:(q + 1) * NB])\
                  .then_inc(S("out_landed"), 16)
            sp.wait_ge(S("out_landed"), 32)

        def kv_place(g, c_):
            order = [[(0, 0), (1, 0), (0, 2), (1, 2), (2, 2), (3, 2)], [(0, 1), (1, 1), (2, 3), (3, 3), (2, 1), (3, 1)]]
            i = order[c_ % 2].index((g, c_))
            return scr[:, 2 * (c_ % 2) + i // 4, (i % 4) * P:(i % 4 + 1) * P]

        gains = [("norm_mix_pre", 0), ("norm_mix_post", 0), ("norm_ffn_pre", 0), ("norm_ffn_post", 0),
                 ("ln_mix_g_2", 0), ("ln_mix_b_2", 0), ("ln_ffn_g_2", 0), ("ln_ffn_b_2", 0),
                 ("ln_mix_g_2", 1), ("ln_mix_b_2", 1), ("ln_ffn_g_2", 1), ("ln_ffn_b_2", 1)]

        @block.gpsimd
        def _(pool):
            def one(ins):
                pool.drain()

            def gain_row(i):
                if i >= 2:
                    pool.wait_ge(S("gain_used"), i - 1)
                g, l = gains[i]
                pool.dma_start(gain[:, i % 2, :], a[g][l:l + 1, :].broadcast_to([P, D]))\
                    .then_inc(S(f"gain_landed{i % 2}"), 16)

            def keep(t, pattern, first, per_row, fill=0.0, op=ALU.is_ge):
                one(pool.affine_select(out=t, in_=t, pattern=pattern, compare_op=op, fill=fill, base=first,
                                       channel_multiplier=per_row))

            gain_row(0)
            gain_row(1)
            pool.memset(ident[:], 0.0)
            one(None)
            pool.affine_select(out=ident[:], in_=ident[:], pattern=[[-1, P]], compare_op=ALU.not_equal, fill=1.0,
                               base=0, channel_multiplier=1).then_inc(S("ident_ready"), 1)
            pool.dma_start(conv_w[:], a["conv_a"].broadcast_to([P, 3, D_HALF])).then_inc(S("conv_w_landed"), 16)
            pool.dma_start(head_gain[:], a["gla_head_norm"].broadcast_to([P, HEAD_V])).then_inc(S("head_gain_landed"), 16)
            pool.dma_start(rb_row[:], a["router_b_2"].broadcast_to([P, N_EXP])).then_inc(S("rb_landed"), 16)
            pool.memset(gate_w[:], 0.0)
            for t, v in ((ones, 1.0), (tri_incl, 1.0), (tri_excl, 1.0), (neg_from, -1.0), (neg_ones, -1.0),
                         (tri_fwd, DECAY), (tri_bwd, DECAY)):
                pool.memset(t[:], v)
            pool.iota(slot_row[:], pattern=[[1, P]], base=0, channel_multiplier=0,
                      allow_small_or_imprecise_dtypes=True)
            one(None)
            for src, r, cc in (("gate_up_fwd", 0, 0), ("gate_up_bwd", RANK, N_GK)):
                pool.dma_start(gate_w[r:r + RANK, cc:cc + N_GK], a[src][0]).then_inc(S("gate_w_landed"), 16)
            for src, cc in (("gate_bias_fwd", 0), ("gate_bias_bwd", N_GK)):
                pool.dma_start(gate_w[2 * RANK:2 * RANK + 1, cc:cc + N_GK], a[src]).then_inc(S("gate_w_landed"), 16)
            keep(tri_incl[:], [[1, P]], 0, -1)
            keep(tri_excl[:], [[1, P]], -1, -1)
            keep(neg_from[:], [[-1, P]], 0, 1)
            keep(tri_fwd[:], [[1, P]], 0, -1)
            keep(tri_bwd[:], [[-1, P]], 0, 1)
            keep(tri_fwd[:, GLA_CHUNK:P], [[0, P - GLA_CHUNK]], -GLA_CHUNK, 1)
            keep(tri_bwd[:, 0:GLA_CHUNK], [[0, GLA_CHUNK]], GLA_CHUNK - 1, -1)
            pool.drain().then_inc(S("tri_ready"), 1)

            for bb in (1, 2, 3):
                wait_evacuated(pool, bb)
            pool.wait_ge(S("conv_w_landed"), 16)
            gc, gv = p0[:, :, C_GC:C_GC + D_HALF], p0[:, :, C_GV:C_GV + D_HALF]
            ya = y[:, :, 0:D_HALF]
            one(pool.tensor_tensor(gc, gc, gv, ALU.mult))
            pool.memset(gv, 0.0)
            one(pool.memset(ya, 0.0))
            for dst, src in ((gv[1:P, :, :], gc[0:P - 1, :, :]), (gv[0:1, 1:2, :], gc[P - 1:P, 0:1, :]),
                             (ya[0:P - 1, :, :], gc[1:P, :, :]), (ya[P - 1:P, 0:1, :], gc[0:1, 1:2, :])):
                pool.dma_start(dst, src).then_inc(S("shift_landed"), 16)
            pool.wait_ge(S("shift_landed"), 64)
            for dst, tap in ((ya, 2), (gv, 0), (gc, 1)):
                for t in range(NT):
                    pool.tensor_tensor(dst[:, t, :], dst[:, t, :], conv_w[:, tap, :], ALU.mult)
            one(None)
            one(pool.tensor_tensor(gv, gv, gc, ALU.add))
            one(pool.tensor_tensor(ya, ya, gv, ALU.add))
            pool.tensor_tensor(ya, ya, p0[:, :, C_GB:C_GB + D_HALF], ALU.mult).then_inc(S("ya_ready"), 1)

            if "w_up" in live:
                pool.wait_ge(S("t_source"), 2 * NT)
                pool.dma_start(cw_rows[:], a["conv_ffn"][0].rearrange("j (k p) -> k j p", p=P)).then_inc(S("cw_landed"), 16)
                pool.dma_start(rw[:], a["router_w_2"][0].rearrange("(k p) e -> p k e", p=P)).then_inc(S("rw_landed"), 16)
                pool.dma_start(pn[:], a["p_2"][0, 0].rearrange("(t p) n -> p t n", p=P)).then_inc(S("p_landed"), 16)
            gain_row(2)
            if "w_up" in live:
                gain_row(3)
            if "ab_in" in live:
                for i in (4, 5):
                    gain_row(i)
                wait_phase_evacuated(pool, "w_down")
                pool.dma_start(fbias[:], a["ab_b_f_2"].broadcast_to([P, N_AB])).then_inc(S("fbias_landed"), 16)
                for t, v in ((mask_fox[:], 0.0), (mask_sb[:], 0.0), (keep_sb[:], 1.0), (neg_head[:], -1.0), (ct[:], 0.0)):
                    pool.memset(t, v)
                one(None)
                keep(mask_fox[:, 0:P], [[-1, P]], 0, 1, NEG)
                keep(mask_fox[:, P:SCW], [[-1, SEQ]], P, 1, NEG)
                for t, fill in ((mask_sb, NEG), (keep_sb, 0.0)):
                    keep(t[:, 0:SEQ], [[1, SEQ]], -1, -1, fill)
                    keep(t[:, SEQ:SCW], [[1, P]], -1, -1, fill)
                keep(neg_head[:], [[1, N_AB], [0, P]], 0, -1, 0.0)
                keep(neg_head[:], [[-1, N_AB], [0, P]], 0, 1, 0.0)
                pool.drain().then_inc(S("ab_masks_ready"), 1)
            if "ffn_up" in live:
                for i in (6, 7):
                    gain_row(i)
            if "qkv" in live:
                pool.wait_ge(S("p_t"), 1)
                pool.dma_start(pn[:], a["p_2"][1, 0].rearrange("(t p) n -> p t n", p=P)).then_inc(S("p_landed"), 16)
                for i in (8, 9):
                    gain_row(i)
                pool.wait_ge(S("ple_x"), 1)
                pool.dma_start(rope[:], a["rope"].rearrange("c (t p) n -> p c t n", p=P)).then_inc(S("rope_landed"), 16)
                pool.dma_start(sink[:], a["c_sinks_2"].broadcast_to([P, N_SWA])).then_inc(S("sink_landed"), 16)
                one(pool.memset(mask_swa[:], 0.0))
                keep(mask_swa[:, 0:P], [[-1, P]], 0, 1, NEG)
                keep(mask_swa[:, P:SCW], [[-1, SEQ]], P, 1, NEG)
                keep(mask_swa[:, P:SCW], [[1, SEQ]], -1, -1, NEG)
                pool.drain().then_inc(S("swa_mask_ready"), 1)
            if "moe" in live:
                for i in (10, 11):
                    gain_row(i)


        @block.scalar
        def _(act):
            me = Place()
            for s in range(2):
                act.sem_inc(S(f"acc_free{s}"), 1)

            def copy(o, i, func=ACT.Copy, **kw):
                return act.activation(o, i, func, **kw)

            def round_chunk(k, r, n):
                act.wait_ge(S(f"w_landed{k % RING}"), 16 * (k // RING + 1) + 16 * r)
                wait_used(act, k - RING + 1, r)
                copy(w_hi[:, k % RING, 0:n], w_raw[:, k % RING, 0:n]).then_inc(S("hi_ready"), 1)

            def round_to(c, r=0):
                while me.chunk < (c if me.looping else min(c, me.cap)):
                    round_chunk(me.chunk, r, CHUNK if me.looping else width[me.chunk])
                    me.chunk += 1

            def root(n):
                act.wait_ge(S("ms_ready"), n + 1)
                copy(stat[:, 2:4], stat[:, 0:2], ACT.Sqrt).then_inc(S("root_ready"), 1)

            def operand(m):
                for j in range(4):
                    act.wait_ge(S("t_ready"), 4 * m + j + 1)
                    copy(xt_hi[:, 4 * (j % 2):4 * (j % 2) + 4, (j // 2) * P:(j // 2 + 1) * P],
                         scr[:, j, :].rearrange("p (k n) -> p k n", n=P)).then_inc(S("xt_hi_ready"), 1)

            def evacuate(name, dst):
                def body(blocks, r):
                    for bb, cc, n0, n, ps in blocks:
                        round_to(cc + len(ps) + 2, r)
                        wait_used(act, cc + len(ps), r)
                        for t in range(NT):
                            i = copy(dst[:, t, sl(ncol(name, n0, r), n)], acc[bb % 2][t][:, 0:n])
                        i.then_inc(S(f"acc_free{bb % 2}"), 1)
                split_loop(act, name, body, me)

            def log_sigmoid_tail(o, z):
                copy(o, z, ACT.Abs)
                act.drain()
                copy(o, o, ACT.Exp, scale=-1.0)
                act.drain()
                return copy(o, o, ACT.Ln, bias=1.0)

            def squares(name):
                for bb, cc, n0, n, ps in phase[name]:
                    round_to(cc + len(ps) + 2)
                    wait_used(act, cc + len(ps))
                    for t in range(NT):
                        col = 8 + NT * (n0 // NB) + t
                        copy(y[:, t, n0:n0 + n], acc[bb % 2][t][:, 0:n], ACT.Square, accum_out=stat[:, col:col + 1])
                    act.drain().then_inc(S("sq_ready"), 1)

            def squares_x(ready):
                for t in range(NT):
                    ready(t)
                    copy(junk[:, t, :], x[:, t, :], ACT.Square, accum_out=stat[:, 6 + t:7 + t])
                    act.drain().then_inc(S("sq_ready"), 1)

            def pace(name):
                for bb, cc, n0, n, ps in phase[name]:
                    round_to(cc + len(ps) + 2)

            squares_x(lambda t: act.wait_ge(S(f"x_landed{t}"), 16))
            root(0)
            operand(0)
            evacuate("w_lr", p0)
            act.wait_ge(S("lr_t"), 1)
            copy(lrt[0:2 * RANK, :], scr[0:2 * RANK, 0, 0:SEQ])\
                .then_inc(S("lrt_ready"), 1)
            act.wait_ge(S("gate_pre"), 1)
            log_sigmoid_tail(tmp0[:], scr[:, 2:4, :]).then_inc(S("gate_ln"), 1)
            evacuate("w_in", p0)
            act.wait_ge(S("qk_t"), 1)
            copy(qk0[:, 0:2, :], scr[:, 1, :].rearrange("p (f n) -> p f n", n=SEQ), scale=HEAD_K ** -0.5)
            copy(qk0[:, 2:4, :], scr[:, 2, :].rearrange("p (f n) -> p f n", n=SEQ)).then_inc(S("qk0_ready"), 1)
            act.wait_ge(S("cum_ready"), 1)
            copy(e1[:], cum[:], ACT.Exp).then_inc(S("gla_exp"), 1)
            copy(e2[:], cum[:], ACT.Exp, scale=-1.0).then_inc(S("gla_exp"), 1)
            act.wait_ge(S("cum_rest"), 1)
            copy(e3[:], e3[:], ACT.Exp).then_inc(S("gla_exp"), 1)
            act.wait_ge(S("q_in"), 1)
            act.wait_ge(S("q_half_zero"), 1)
            for par in range(2):
                v = lambda t: t.rearrange("p g (c q n) -> p (g c) q n", q=2, n=GLA_CHUNK)[:, :, par, :]
                i = copy(v(q_half[:, par]), v(e1[:]))
            i.then_inc(S("q_half_ready"), 1)
            for t in range(NT):
                act.wait_ge(S("kout_t"), t + 1)
                copy(kout[:, t, :], scr[:, 3 * t, :]).then_inc(S("kout_ready"), 1)
            go = p0[:, :, C_GO:C_GO + D_HALF]
            copy(go, go, ACT.Silu).then_inc(S("go_ready"), 1)
            act.wait_ge(S("gla_o"), NT)
            act.wait_ge(S("e2_free"), 1)
            copy(e2[:], psum[:, 0:4, 0:SEQ], ACT.Square).then_inc(S("o_sq"), 1)
            act.wait_ge(S("o_ms"), 1)
            copy(ss8[:, 1, :], ss8[:, 0, :], ACT.Sqrt).then_inc(S("o_root"), 1)
            operand(1)
            squares("w_out")
            root(1)

            def up_conv(blocks, r):
                (bg, cg, n0, n, _), (bv, cv, _, _, _) = blocks
                j, nc_ = n0 // NB, n // P
                end = cv + (cv - cg)

                def middle_tap(h, u, bb):
                    for k in range(nc_):
                        ch = h * KF + 4 * j + k
                        i = copy(u[:, k, :], acc_t(bb % 2, k), scale=cw[:, 1, ch:ch + 1])
                    i.then_inc(S("tap_mid"), 1)

                round_to(cv + 2)
                wait_used(act, cv)
                if j:
                    act.wait_ge(S("ht_ready"), j)
                else:
                    act.wait_ge(S("cw_ready"), 1)
                middle_tap(0, ug, bg)
                act.wait_ge(S("gate_conv"), j + 1)
                copy(ug[:, 0:nc_, :], ug[:, 0:nc_, :], ACT.Silu)
                act.drain().then_inc(S("silu_ready"), 1)
                round_to(end + 2)
                wait_used(act, end)
                middle_tap(1, uv, bv)
                act.wait_ge(S("h_ready"), j + 1)
                copy(ht_hi[:, 4 * j:4 * j + nc_, :], uv[:, 0:nc_, :]).then_inc(S("ht_hi_ready"), 1)

            if "w_up" in live:
                squares_x(lambda t: act.wait_ge(S("x_tile"), t + 1))
                root(2)
                operand(2)
                split_loop(act, "w_up", up_conv, me, unroll=True)
            if "w_down" in live:
                squares("w_down")
                root(3)

            def softmax(q, probs, smx_, sink_=False):
                act.wait_ge(S("at_negm"), q + 1)
                for h in range(8):
                    for t, (c0, c1) in enumerate(((0, P), (P, SCW))):
                        i = copy(probs[:, h, c0:c1], probs[:, h, c0:c1], ACT.Exp, bias=smx_[:, 1, t, h:h + 1],
                                 accum_out=smx_[:, 2, t, h:h + 1])
                    act.drain().then_inc(S("at_p"), 1)
                if sink_:
                    copy(smx_[:, 4, :, :], smx_[:, 3, :, :], ACT.Exp)
                act.drain().then_inc(S("at_sum"), 1)

            if "ab_in" in live:
                operand(3)
                evacuate("ab_in", p1)
                act.wait_ge(S("lf_pre"), 1)
                log_sigmoid_tail(lf[:, 1, :, :], lf[:, 0, :, :]).then_inc(S("lf_ln"), 1)
                for g in range(2):
                    for tile in range(4):
                        act.wait_ge(S("ab_t"), 4 * g + tile + 1)
                        copy(qk1[:, 2 * tile:2 * tile + 2, :], scr[:, tile, :].rearrange("p (f n) -> p f n", n=SEQ),
                             scale=DH ** -0.5 if tile < 2 else 1.0).then_inc(S("qk1_ready"), 1)
                softmax(0, s_all, smx)

                def sb_log(g):
                    act.wait_ge(S("sb_z"), g + 1)
                    log_sigmoid_tail(stick[:, g % SB_SETS], sb_banks(g)).then_inc(S("sb_ln"), 1)

                def sb_weights(g):
                    act.wait_ge(S("sb_masked"), g + 1)
                    a_ = stick[:, g % SB_SETS]
                    copy(a_, a_, ACT.Exp).then_inc(S("sb_a"), 1)

                for g in range(SB_SETS):
                    sb_log(g)
                sb_weights(0)
                sb_weights(1)
                act.wait_ge(S("sb_o"), 1)
                sb_log(3)
                sb_weights(2)
                sb_weights(3)
            if "ab_out" in live:
                operand(4)
                pace("ab_out")
                root(4)

            def up_gated(blocks, r):
                (bg, cg, n0, n, _), (bv, cv, _, _, _) = blocks
                j, nc_ = n0 // NB, n // P
                round_to(cv + 2)
                wait_used(act, cv)
                if j:
                    act.wait_ge(S("h_ready"), KP + j)
                copy(ug[:, 0:nc_, :], acc_tall(bg % 2, nc_), ACT.Silu).then_inc(S(f"acc_free{bg % 2}"), 1)
                round_to(cv + (cv - cg) + 2)
                act.wait_ge(S("h_ready"), KP + j + 1)
                copy(ht_hi[:, 4 * j:4 * j + nc_, :], uv[:, 0:nc_, :]).then_inc(S("ht_hi_ready"), 1)

            def round_p(i):
                act.wait_ge(S("p_t"), i + 1)
                copy(ppt_hi[:], scr[:, 3, :].rearrange("p (k n) -> p k n", n=SEQ)).then_inc(S("ppt_hi_ready"), 1)

            if "ffn_up" in live:
                operand(5)
                round_p(0)
                split_loop(act, "ffn_up", up_gated, me, unroll=True)
            if "ffn_down" in live:
                pace("ffn_down")
                root(5)

            def ple(i, m, r=0):
                blocks = phase[f"ple{i}"]
                round_to(blocks[0][1] + RING, r)
                for bb, cc, n0, n, ps in blocks[0:2]:
                    wait_used(act, cc + len(ps), r)
                    for t in range(NT):
                        j = copy(p_out[:, t, n0:n0 + n], acc[bb % 2][t])
                    j.then_inc(S(f"acc_free{bb % 2}"), 1)
                operand(m)
                for q, (bb, cc, n0, n, ps) in enumerate(blocks[2:4]):
                    round_to(cc + len(ps) + 2, r)
                    wait_used(act, cc + len(ps), r)
                    for t in range(NT):
                        copy(sig[:, q, t, :], acc[bb % 2][t], ACT.Sigmoid).then_inc(S("sig_ready"), 1)
                    act.drain().then_inc(S(f"acc_free{bb % 2}"), 1)

            if "ple0" in live:
                ple(0, 6)
            if "qkv" in live:
                operand(7)
                evacuate("qkv", p2)
                for j in range(3):
                    act.wait_ge(S("swa_t"), j + 1)
                    nb = 4 if j < 2 else 2
                    if j < 2:
                        copy(qk2[:, 4 * j:4 * j + 4, :], scr[:, 2 * (j % 2):2 * (j % 2) + 2, :]
                             .rearrange("p b (f n) -> p (b f) n", n=SEQ), scale=DH ** -0.5)\
                            .then_inc(S("qk2_ready"), 1)
                    else:
                        copy(qk2[:, 8:10, :], scr[:, 0, :].rearrange("p (f n) -> p f n", n=SEQ))\
                            .then_inc(S("qk2_ready"), 1)
                for g in range(2):
                    softmax(1 + g, (s_all, s_more)[g], smx2[:, g], True)
            if "c_out" in live:
                operand(8)
                pace("c_out")
                root(6)

            def rounds(k0, k1, r):
                for k in range(k0, k1):
                    round_chunk(N_BEFORE_MOE + k, r, item_width(k))

            def take_item(n, k, r):
                act.wait_ge(S("gathered"), 3 * n + 1)
                copy(xg_hi[:], scr[:, 2:4, :].rearrange("p b (k n) -> p (b k) n", n=P)).then_inc(S("xg_hi_ready"), 1)
                rounds(k, k + 2, r)
                act.wait_ge(S("gathered"), 3 * n + 3)
                copy(selt[:], scr[:, 2, 0:SEQ])
                copy(gslot[:], scr[:, 2, SEQ:SEQ + 1]).then_inc(S("selt_ready"), 1)

            def item(i):
                c0, r = N_BEFORE_MOE, i * R_ITEM
                for j in range(MOE_PAIRS):
                    wait_used(act, c0 + 4 * j + 2, r)
                    if j:
                        act.wait_ge(S("mh_ready"), MOE_PAIRS * i + j)
                    copy(mg[:], psum[:, 2 * (j % 2), :], ACT.Silu).then_inc(S("mg_ready"), 1)
                    rounds(4 * j + 4, 4 * j + 6, r)
                    if j:
                        act.wait_ge(S("mh_t"), MOE_PAIRS * i + j)
                        copy(mh_hi[:, 4 * j - 4:4 * j, :], psum[:, 6 + (j - 1) % 2, :].rearrange("p (k n) -> p k n", n=P))\
                            .then_inc(S("mh_hi_ready"), 1)
                    rounds(4 * j + 6, 4 * j + 8, r)
                j = MOE_PAIRS
                act.wait_ge(S("mh_t"), MOE_PAIRS * i + j)
                copy(mh_hi[:, 4 * j - 4:4 * j, :], psum[:, 6 + (j - 1) % 2, :].rearrange("p (k n) -> p k n", n=P))\
                    .then_inc(S("mh_hi_ready"), 1)
                k = 4 * j + 4
                for n in range(2):
                    end = MOE_UP_CHUNKS + len(MOE_DOWN) * (n + 1)
                    rounds(k, end + 2, r)
                    k = end + 2
                    wait_used(act, c0 + end, r)
                    copy(ys_hi[:, n * NB:(n + 1) * NB], psum[:, 4 + n, :], scale=gslot[:, 0:1])\
                        .then_inc(S("ys_hi_ready"), 1)
                take_item(i + 1, k, r)

            if "moe" in live:
                operand(9)
                copy(xn_hi[:], x[:]).then_inc(S("xn_hi_ready"), 1)
                round_p(1)
                rounds(0, 2, 0)
                act.wait_ge(S("top_gap"), 1)
                copy(route[:, 142:144], route[:, 140:142], ACT.Exp).then_inc(S("top_exp"), 1)
                act.wait_ge(S("counted"), 1)
                n_items = act.value_load(route_i[0:1, 3:4], min_val=N_EXP, max_val=ITEMS)
                take_item(0, 2, 0)
                with act.Fori(0, ITEMS) as i:
                    with act.If(i < n_items):
                        item(i)
                    act.end_ifs()
                me.cap = N_STATIC
                root(7)
            if "ple1" in live:
                me.chunk += RING
                ple(1, 10, n_items * R_ITEM)

        @block.vector
        def _(dve):
            me = Place()
            dve.sem_inc(S("lo_ready"), RING)
            TT, STT, TS = dve.tensor_tensor, dve.scalar_tensor_tensor, dve.tensor_scalar

            def split_chunk(k, r, n):
                dve.wait_ge(S("hi_ready"), k + 1 + RING * r)
                TT(w_lo[:, k % RING, 0:n], w_raw[:, k % RING, 0:n], w_hi[:, k % RING, 0:n].bitcast(F32), ALU.subtract)\
                    .then_inc(S("lo_ready"), 1)

            def round_to(c, r=0):
                while me.chunk < (c if me.looping else min(c, me.cap)):
                    split_chunk(me.chunk, r, CHUNK if me.looping else width[me.chunk])
                    me.chunk += 1

            def operand(m):
                for j in range(4):
                    dve.wait_ge(S("xt_hi_ready"), 4 * m + j + 1)
                    o = (slice(None), slice(4 * (j % 2), 4 * (j % 2) + 4), slice((j // 2) * P, (j // 2 + 1) * P))
                    TT(xt_lo[o], scr[:, j, :].rearrange("p (k n) -> p k n", n=P), xt_hi[o].bitcast(F32), ALU.subtract)\
                        .then_inc(S("xt_ready"), 1)

            def row(i):
                dve.wait_ge(S(f"gain_landed{i % 2}"), 16 * (i // 2 + 1))
                return gain[:, i % 2, :]

            def inverse_root(n):
                dve.drain().then_inc(S("ms_ready"), 1)
                dve.wait_ge(S("root_ready"), n + 1)
                dve.reciprocal(stat[:, 4:6], stat[:, 2:4])
                dve.drain()

            def rms_root(n):
                TS(stat[:, 0:2], stat[:, 6:8], 1.0 / D, RMS_EPS, ALU.mult, ALU.add)
                inverse_root(n)

            def rms_before(n, i):
                dve.wait_ge(S("sq_ready"), 2 * (n + 1))
                rms_root(n)
                g = row(i)
                for t in range(NT):
                    STT(y[:, t, :], x[:, t, :], stat[:, 4 + t:5 + t], g, ALU.mult, ALU.mult)
                    dve.drain().then_inc(S("t_source"), 1)
                dve.sem_inc(S("gain_used"), 1)

            def rms_after(n, i, name, done):
                dve.wait_ge(S("sq_ready"), 2 * (n + 1))
                TT(stat[:, 6:8], stat[:, 8:10], stat[:, 10:12], ALU.add)
                dve.drain()
                rms_root(n)
                g = row(i)
                for t in range(NT):
                    for bb, _, n0, w_, _ in phase[name]:
                        k = STT(y[:, t, n0:n0 + w_], acc[bb % 2][t], stat[:, 4 + t:5 + t], g[:, n0:n0 + w_], ALU.mult, ALU.mult)
                        if t == NT - 1:
                            k.then_inc(S(f"acc_free{bb % 2}"), 1)
                    dve.drain()
                    TT(x[:, t, :], x[:, t, :], y[:, t, :], ALU.add)
                    dve.drain().then_inc(S(done), 1)
                dve.sem_inc(S("gain_used"), 1)

            def add_half(h, part):
                cols = slice(h * NB, (h + 1) * NB)
                for t in range(NT):
                    k = STT(x[:, t, cols], x[:, t, cols], ALPHA, part(t), ALU.mult, ALU.add)
                dve.drain()
                for t in range(NT):
                    dve.bn_stats(bn[:, t, h, :], x[:, t, cols])

            def follow_add(name):
                for bb, cc, n0, n, ps in phase[name]:
                    round_to(cc + len(ps) + 2)
                    wait_used(dve, cc + len(ps))
                    add_half(n0 // NB, lambda t: acc[bb % 2][t])
                    dve.sem_inc(S(f"acc_free{bb % 2}"), 1)

            def layer_norm(n, i, src=x):
                dve.drain()
                for t in range(NT):
                    dve.bn_aggr(stat[:, 8 + 2 * t:10 + 2 * t], bn[:, t, :, :])
                dve.drain()
                TS(stat[:, 0:2], stat[:, 9:12:2], LN_EPS, None, ALU.add)
                inverse_root(n)
                g, b_ = row(i), row(i + 1)
                for t in range(NT):
                    STT(x[:, t, :], src[:, t, :], stat[:, 8 + 2 * t:9 + 2 * t], g, ALU.subtract, ALU.mult)
                    dve.drain()
                    STT(x[:, t, :], x[:, t, :], stat[:, 4 + t:5 + t], b_, ALU.mult, ALU.add)
                    dve.drain().then_inc(S("t_source"), 1)
                dve.sem_inc(S("gain_used"), 2)

            def follow(name):
                def body(blocks, r):
                    for bb, cc, n0, n, ps in blocks:
                        round_to(cc + len(ps) + 2, r)
                split_loop(dve, name, body, me)

            rms_before(0, 0)
            dve.memset(lrt[2 * RANK:2 * RANK + 1, :], 1.0).then_inc(S("lrt_ones"), 1)
            operand(0)
            follow("w_lr")
            dve.wait_ge(S("gate_ln"), 1)
            STT(logd[:], scr[:, 2:4, :], 0.0, tmp0[:], ALU.min, ALU.subtract).then_inc(S("logd_ready"), 1)
            follow("w_in")
            wait_phase_evacuated(dve, "w_in")
            dve.memset(q_half[:], 0.0).then_inc(S("q_half_zero"), 1)
            dve.wait_ge(S("cum_t"), 1)
            cum_ps = psum[:, 2:4, :].rearrange("p b (f n) -> p (b f) n", n=SEQ)
            dve.tensor_copy(cum[:], cum_ps)
            dve.drain().then_inc(S("cum_ready"), 1)
            chunks = lambda t: t.rearrange("p f (c n) -> p f c n", n=GLA_CHUNK)
            for d, last in ((0, GLA_CHUNK - 1), (1, 0)):
                for f in (2 * d, 2 * d + 1):
                    v = chunks(cum[:])[:, f, :, :]
                    i = TT(chunks(e3[:])[:, f, :, :], v[:, :, last:last + 1].broadcast_to([P, 4, GLA_CHUNK]), v, ALU.subtract)
            i.then_inc(S("cum_rest"), 1)
            dve.wait_ge(S("gla_exp"), 1)
            for d, last in ((0, GLA_CHUNK - 1), (1, 0)):
                dve.tensor_copy(dec[:, 2 * d:2 * d + 2, :], chunks(e1[:])[:, 2 * d:2 * d + 2, :, last])
            dve.drain()
            dve.wait_ge(S("qk0_ready"), 1)
            for n, (e, q) in enumerate(((e1, 0), (e2, 2), (e3, 2))):
                dve.wait_ge(S("gla_exp"), n + 1)
                for d in range(2):
                    i = TT(e[:, 2 * d:2 * d + 2, :], e[:, 2 * d:2 * d + 2, :], qk0[:, q:q + 2, :], ALU.mult)
                i.then_inc(S(("q_in", "k_in", "k_out")[n]), 1)
            dve.memset(st[:], 0.0)
            dve.drain()
            for d, tri in ((0, tri_fwd), (1, tri_bwd)):
                dve.wait_ge(S("gla_scores"), d + 1)
                dve.copy_predicated(st[:, d].rearrange("p a b n -> p (a b) n"),
                                    tri[:].bitcast(I32).unsqueeze(1).broadcast_to([P, 8, P]),
                                    psum[:, 2 * d:2 * d + 2, :].rearrange("p b (k n) -> p (b k) n", n=P))\
                    .then_inc(S("st_ready"), 1)
            dve.wait_ge(S("gla_kv"), 1)
            for step in range(3):
                for g in range(4):
                    src, dst = (step, step + 1) if g < 2 else (3 - step, 2 - step)
                    kv = kv_place(g, src)
                    if step == 0:
                        dve.tensor_copy(state[:, g, dst, :], kv)
                    else:
                        STT(state[:, g, dst, :], state[:, g, src, :], dec[:, g, src:src + 1], kv, ALU.mult, ALU.add)
                dve.drain()
            dve.sem_inc(S("state_ready"), 1)
            dve.sem_inc(S("e2_free"), 1)
            dve.wait_ge(S("head_gain_landed"), 16)
            dve.wait_ge(S("go_ready"), 1)
            for t in range(NT):
                go = p0[:, t, C_GO:C_GO + D_HALF].rearrange("p (b n) -> p b n", n=HEAD_V)
                TT(go, go, head_gain[:].unsqueeze(1).broadcast_to([P, GLA_HEADS, HEAD_V]), ALU.mult)
            dve.wait_ge(S("o_sq"), 1)
            dve.reduce_sum(ss8[:, 2, :], e2[:].rearrange("p a (b n) -> p (a b) n", n=HEAD_V), AX_X)
            dve.drain()
            TS(ss8[:, 0, :], ss8[:, 2, :], 1.0 / HEAD_V, RMS_EPS, ALU.mult, ALU.add).then_inc(S("o_ms"), 1)
            dve.wait_ge(S("o_root"), 1)
            dve.reciprocal(ss8[:, 2, :], ss8[:, 1, :])
            dve.drain()
            o8 = e3[:].rearrange("p a (b n) -> p (a b) n", n=HEAD_V)
            for t in range(NT):
                TT(o8[:, 4 * t:4 * t + 4, :].rearrange("p (a b) n -> p a b n", b=2),
                   psum[:, 2 * t:2 * t + 2, 0:SEQ].rearrange("p a (b n) -> p a b n", n=HEAD_V),
                   ss8[:, 2, 4 * t:4 * t + 4].rearrange("p (a b) -> p a b", b=2).unsqueeze(3).broadcast_to([P, 2, 2, HEAD_V]),
                   ALU.mult)
            dve.drain()
            dve.wait_ge(S("ya_ready"), 1)
            for t in range(NT):
                heads = lambda v: v.rearrange("p (b a n) -> p a b n", a=2, n=HEAD_V)
                TT(heads(y[:, t, D_HALF:D]), o8[:, 4 * t:4 * t + 4, :].rearrange("p (a b) n -> p a b n", b=2),
                   heads(p0[:, t, C_GO:C_GO + D_HALF]), ALU.mult)
                dve.drain().then_inc(S("t_source"), 1)
            operand(1)
            follow("w_out")
            rms_after(1, 1, "w_out", "x_tile")

            def up_conv(blocks, r):
                (bg, cg, n0, n, _), (bv, cv, _, _, _) = blocks
                j, nc_ = n0 // NB, n // P

                def outer_taps(h, u, bb):
                    dve.wait_ge(S("tap_mid"), 2 * j + h + 1)
                    for tap in (0, 2):
                        o, s = (slice(1, SEQ), slice(0, SEQ - 1)) if tap == 0 else (slice(0, SEQ - 1), slice(1, SEQ))
                        for k in range(nc_):
                            ch = h * KF + 4 * j + k
                            STT(u[:, k, o], acc_t(bb % 2, k)[:, s], cw[:, tap, ch:ch + 1], u[:, k, o], ALU.mult, ALU.add)
                        dve.drain()
                    dve.sem_inc(S(f"acc_free{bb % 2}"), 1)

                round_to(cv + 2)
                outer_taps(0, ug, bg)
                dve.sem_inc(S("gate_conv"), 1)
                round_to(cv + (cv - cg) + 2)
                outer_taps(1, uv, bv)
                dve.wait_ge(S("silu_ready"), j + 1)
                TT(uv[:, 0:nc_, :], ug[:, 0:nc_, :], uv[:, 0:nc_, :], ALU.mult)
                dve.drain().then_inc(S("h_ready"), 1)
                split_h(j, j, nc_)

            def split_h(q, j, nc_):
                dve.wait_ge(S("ht_hi_ready"), q + 1)
                o = (slice(None), slice(4 * j, 4 * j + nc_))
                TT(ht_lo[o], uv[:, 0:nc_, :], ht_hi[o].bitcast(F32), ALU.subtract).then_inc(S("ht_ready"), 1)

            if "w_up" in live:
                rms_before(2, 2)
                dve.wait_ge(S("cw_turned"), 1)
                dve.tensor_copy(cw[:].rearrange("p j k -> p (j k)"), psum[:, 0, 0:3 * 2 * KF]).then_inc(S("cw_ready"), 1)
                operand(2)
                split_loop(dve, "w_up", up_conv, me, unroll=True)
            if "w_down" in live:
                follow("w_down")
                rms_after(3, 3, "w_down", "t_source")

            def masked_scores(q, s_, smx_, mask):
                for h in range(8):
                    dve.wait_ge(S("at_qk"), 8 * q + h + 1)
                    if q == 0:
                        for t, (c0, c1) in enumerate(((0, P), (P, SCW))):
                            i = STT(s_[:, h, c0:c1], scr[:, h % 4, c0:c1], cq[:, t, h:h + 1], mask[:, c0:c1],
                                    ALU.add, ALU.add)
                    else:
                        i = TT(s_[:, h, :], scr[:, h % 4, 0:SCW], mask[:], ALU.add)
                    i.then_inc(S("at_s"), 1)
                dve.drain()
                dve.reduce_max(smx_[:, 0, 0, :], s_[:, :, 0:P], AX_X)
                dve.reduce_max(smx_[:, 0, 1, :], s_[:, :, P:SCW], AX_X)
                dve.drain()
                if q:
                    s8 = sink[:, 8 * (q - 1):8 * q].unsqueeze(1).broadcast_to([P, NT, 8])
                    TT(smx_[:, 0], smx_[:, 0], s8, ALU.max)
                    dve.drain()
                    TT(smx_[:, 3], s8, smx_[:, 0], ALU.subtract)
                TS(smx_[:, 1], smx_[:, 0], -1.0, None, ALU.mult)
                dve.drain().then_inc(S("at_negm"), 1)

            def turned_probs(q):
                for h in range(8):
                    dve.wait_ge(S("at_t"), 8 * q + h + 1)
                    dve.tensor_copy((pt if q == 0 else pt2)[:, h % 2, :], psum[:, h % 2, 0:SCW]).then_inc(S("at_pt"), 1)

            def attended(q, smx_, column):
                dve.wait_ge(S("at_sum"), q + 1)
                if q:
                    TT(smx_[:, 2], smx_[:, 2], smx_[:, 4], ALU.add)
                    dve.drain()
                dve.reciprocal(smx_[:, 5], smx_[:, 2])
                dve.drain()
                dve.wait_ge(S("at_o"), q + 1)
                for t in range(NT):
                    i = TT(y[:, t, column:column + 8 * DH].rearrange("p (h n) -> p h n", n=DH),
                           psum[:, 2 + t, :].rearrange("p (h n) -> p h n", n=DH),
                           smx_[:, 5, t, :].unsqueeze(2).broadcast_to([P, 8, DH]), ALU.mult)
                dve.drain().then_inc(S("at_y"), 1)

            if "ab_in" in live:
                operand(3)
                follow("ab_in")
                wait_phase_evacuated(dve, "ab_in")
                dve.wait_ge(S("fbias_landed"), 16)
                TT(lf[:, 0, :, :], p1[:, :, AB_FA:AB_FA + N_AB], fbias[:].unsqueeze(1).broadcast_to([P, NT, N_AB]), ALU.add)
                dve.drain().then_inc(S("lf_pre"), 1)
                dve.wait_ge(S("lf_ln"), 1)
                STT(lf[:, 2, :, :], lf[:, 0, :, :], 0.0, lf[:, 1, :, :], ALU.min, ALU.subtract)
                dve.drain().then_inc(S("lf_ready"), 1)
                dve.wait_ge(S("ab_masks_ready"), 1)
                dve.wait_ge(S("lf_cum"), 1)
                dve.tensor_copy(cq[:], psum[:, 0, 0:NT * N_AB].rearrange("p (t h) -> p t h", h=N_AB))
                dve.tensor_copy(ct[0:N_AB, :], psum[0:N_AB, 1, 0:SEQ])
                dve.drain().then_inc(S("fox_cum_ready"), 1)
                masked_scores(0, s_all, smx, mask_fox)
                turned_probs(0)
                wide = lambda m: m[:].unsqueeze(1).broadcast_to([P, 2, SCW])

                def softplus(g):
                    dve.wait_ge(S("sb_ln"), g + 1)
                    s_ = stick[:, g % SB_SETS]
                    STT(s_, sb_banks(g), 0.0, s_, ALU.max, ALU.add)
                    dve.drain()
                    TT(s_, s_, wide(keep_sb), ALU.mult)
                    dve.drain().then_inc(S("sb_sp"), 1)

                def masked_exponents(g):
                    dve.wait_ge(S("sb_exponent"), g + 1)
                    TT(stick[:, g % SB_SETS], sb_banks(g), wide(mask_sb), ALU.add)
                    dve.drain().then_inc(S("sb_masked"), 1)

                softplus(0)
                attended(0, smx, 0)
                softplus(1)
                masked_exponents(0)
                softplus(2)
                masked_exponents(1)
                masked_exponents(2)
                softplus(3)
                masked_exponents(3)
                dve.wait_ge(S("sb_o"), 4)
                for t in range(NT):
                    dve.tensor_copy(y[:, t, FOX_W:2 * FOX_W], psum[:, 2 + t, :])
                dve.drain()
                dve.sem_inc(S("t_source"), NT)
            if "ab_out" in live:
                operand(4)
                follow_add("ab_out")
                layer_norm(4, 4)

            def up_gated(blocks, r):
                (bg, cg, n0, n, _), (bv, cv, _, _, _) = blocks
                j, nc_ = n0 // NB, n // P
                round_to(cv + (cv - cg) + 2)
                wait_evacuated(dve, bg)
                wait_used(dve, cv + (cv - cg))
                dve.drain()
                TT(uv[:, 0:nc_, :], ug[:, 0:nc_, :], acc_tall(bv % 2, nc_), ALU.mult).then_inc(S(f"acc_free{bv % 2}"), 1)
                dve.drain().then_inc(S("h_ready"), 1)
                split_h(KP + j, j, nc_)

            def split_p(i):
                dve.wait_ge(S("ppt_hi_ready"), i + 1)
                TT(ppt_lo[:], scr[:, 3, :].rearrange("p (k n) -> p k n", n=SEQ), ppt_hi[:].bitcast(F32), ALU.subtract)\
                    .then_inc(S("ppt_ready"), 1)

            if "ffn_up" in live:
                operand(5)
                split_p(0)
                split_loop(dve, "ffn_up", up_gated, me, unroll=True)
            if "ffn_down" in live:
                follow_add("ffn_down")
                layer_norm(5, 6)

            def ple(i, m, r=0):
                blocks = phase[f"ple{i}"]
                round_to(blocks[0][1] + RING, r)
                operand(m)
                for q, (bb, cc, n0, n, ps) in enumerate(blocks[2:4]):
                    round_to(cc + len(ps) + 2, r)
                    for t in range(NT):
                        dve.wait_ge(S("sig_ready"), 4 * i + 2 * q + t + 1)
                        TT(sig[:, q, t, :], sig[:, q, t, :], p_out[:, t, n0:n0 + n], ALU.mult)
                        dve.drain()
                        TT(x[:, t, n0:n0 + n], x[:, t, n0:n0 + n], sig[:, q, t, :], ALU.add)
                    dve.drain().then_inc(S("ple_added"), 1)

            if "ple0" in live:
                ple(0, 6)
                dve.sem_inc(S("ple_x"), 1)
            if "qkv" in live:
                dve.sem_inc(S("t_source"), NT)
                operand(7)
                follow("qkv")
                wait_phase_evacuated(dve, "qkv")
                dve.wait_ge(S("rope_landed"), 16)
                hd = p2[:, :, 0:SWA_V].rearrange("p t (h n) -> p t h n", n=DH)
                x1, x2 = hd[:, :, :, 0:ROPE_HALF], hd[:, :, :, ROPE_HALF:2 * ROPE_HALF]
                rt = [rtmp[:, k].rearrange("p t (h n) -> p t h n", n=ROPE_HALF) for k in range(4)]
                for t in range(NT):
                    cs = [rope[:, k, t, :].unsqueeze(1).broadcast_to([P, 18, ROPE_HALF]) for k in range(2)]
                    for k, (v, f) in enumerate(((x1, 0), (x2, 1), (x2, 0), (x1, 1))):
                        TT(rt[k][:, t], v[:, t], cs[f], ALU.mult)
                dve.drain()
                TT(x1, rt[0], rt[1], ALU.subtract)
                TT(x2, rt[2], rt[3], ALU.add)
                dve.drain()
                for u in range(2):
                    dve.tensor_copy(kdup[:, :, :, u, :], p2[:, :, SWA_K:SWA_V].rearrange("p t (g n) -> p t g n", n=DH))
                dve.drain().then_inc(S("rotated"), 1)
                dve.wait_ge(S("swa_mask_ready"), 1)
                dve.wait_ge(S("sink_landed"), 16)
                for g in range(2):
                    masked_scores(1 + g, (s_all, s_more)[g], smx2[:, g], mask_swa)
                for g in range(2):
                    turned_probs(1 + g)
                    attended(1 + g, smx2[:, g], g * 8 * DH)
                dve.sem_inc(S("t_source"), NT)
            if "c_out" in live:
                operand(8)
                follow_add("c_out")
                layer_norm(6, 8)

            def splits(k0, k1, r):
                for k in range(k0, k1):
                    split_chunk(N_BEFORE_MOE + k, r, item_width(k))

            def select(n):
                for t in range(NT):
                    dve.tensor_copy(cur[:, t:t + 1], slotc[:, bass.ds(n + t * ITEMS, 1)])
                    dve.tensor_copy(cur[:, 2 + t:3 + t], combc[:, bass.ds(n + t * ITEMS, 1)])
                dve.drain()
                for t in range(NT):
                    TS(sel[:, t, :], slot_row[:], cur[:, t:t + 1], None, ALU.is_equal)
                dve.drain().then_inc(S("sel_ready"), 1)

            def take_item(n):
                dve.wait_ge(S("gathered"), 3 * n + 2)
                dve.tensor_copy(xg_lo[:], psum[:, 2:4, :].rearrange("p b (k n) -> p (b k) n", n=P)).then_inc(S("xg_ready"), 1)

            def item(i):
                c0, r = N_BEFORE_MOE, i * R_ITEM
                for j in range(MOE_PAIRS):
                    splits(4 * j + 4, 4 * j + 6, r)
                    if j:
                        lo_h(i, j - 1)
                    dve.wait_ge(S("mg_ready"), MOE_PAIRS * i + j + 1)
                    wait_used(dve, c0 + 4 * j + 4, r)
                    if j >= 2:
                        dve.wait_ge(S("mh_t"), MOE_PAIRS * i + j - 1)
                    TT(mh[:, j % 2, :], mg[:], psum[:, 2 * (j % 2) + 1, :], ALU.mult).then_inc(S("mh_ready"), 1)
                    splits(4 * j + 6, 4 * j + 8, r)
                    if j == 1:
                        dve.wait_ge(S("gathered"), 3 * i + 3)
                        select(i + 1)
                lo_h(i, MOE_PAIRS - 1)
                k = 4 * MOE_PAIRS + 4
                for n in range(2):
                    end = MOE_UP_CHUNKS + len(MOE_DOWN) * (n + 1)
                    splits(k, end + 2, r)
                    k = end + 2
                    dve.wait_ge(S("ys_hi_ready"), 2 * i + n + 1)
                    o = slice(n * NB, (n + 1) * NB)
                    STT(ys_lo[:, o], psum[:, 4 + n, :], gslot[:, 0:1], ys_hi[:, o].bitcast(F32), ALU.mult, ALU.subtract)\
                        .then_inc(S("ys_ready"), 1)
                take_item(i + 1)
                for t in range(NT):
                    dve.wait_ge(S("scattered"), 2 * i + t + 1)
                    TT(y[:, t, :], y[:, t, :], psum[:, 4 * t:4 * t + 2, :].rearrange("p b n -> p (b n)"), ALU.add)\
                        .then_inc(S("y_added"), 1)
                splits(k, k + 2, r)
                dve.drain()

            def lo_h(i, j):
                dve.wait_ge(S("mh_hi_ready"), MOE_PAIRS * i + j + 1)
                TT(mh_lo[:, 4 * j:4 * j + 4, :], psum[:, 6 + j % 2, :].rearrange("p (k n) -> p k n", n=P),
                   mh_hi[:, 4 * j:4 * j + 4, :].bitcast(F32), ALU.subtract).then_inc(S("mh_split"), 1)

            tok = lambda c, w=N_EXP: route[:, c:c + NT * w].rearrange("p (t e) -> p t e", e=w)
            logits, top8, hot1, hot2, comb, selm, rank1 = (tok(16 * k) for k in range(7))
            slotc, combc = route[:, 112:135], route[:, 148:171]
            gap, gap_e, g1, g2 = (route[:, c:c + 2] for c in (140, 142, 144, 146))
            row8 = lambda k: route[:, 170 + 8 * k:178 + 8 * k]
            cnt, over, over_before, pick, tmp8, eid8, one8 = (row8(k) for k in range(7))
            eidf = route[:, 226:230]
            cur = route[:, 230:234]
            idxf = route[:, 234:250].rearrange("p (t e) -> p t e", e=8)

            if "moe" in live:
                operand(9)
                dve.wait_ge(S("xn_hi_ready"), 1)
                TT(xn_lo[:], x[:], xn_hi[:].bitcast(F32), ALU.subtract)
                TS(y[:], x[:], ALPHA, None, ALU.mult)
                dve.memset(slotc[:, NT * ITEMS:], 0.0)
                dve.sem_inc(S("y_added"), 2)
                dve.memset(one8, 1.0)
                dve.tensor_copy(eid8, slot_row[:, 0:N_EXP])
                dve.wait_ge(S("logits"), 1)
                dve.wait_ge(S("rb_landed"), 16)
                split_p(1)
                splits(0, 2, 0)
                TT(logits, scr[:, 0, 0:NT * N_EXP].rearrange("p (t e) -> p t e", e=N_EXP),
                   rb_row[:].unsqueeze(1).broadcast_to([P, NT, N_EXP]), ALU.add)
                dve.drain()
                for t in range(NT):
                    dve.max(top8[:, t, :], logits[:, t, :])
                dve.drain()
                TT(gap.unsqueeze(2), top8[:, :, 1:2], top8[:, :, 0:1], ALU.subtract)
                for t in range(NT):
                    dve.max_index(route_u[:, t, :], top8[:, t, :], logits[:, t, :])
                dve.drain().then_inc(S("top_gap"), 1)
                dve.tensor_copy(idxf, route_u[:])
                dve.drain()
                for k, hot in ((0, hot1), (1, hot2)):
                    TT(hot, eid8.unsqueeze(1).broadcast_to([P, NT, N_EXP]), idxf[:, :, k:k + 1].broadcast_to([P, NT, N_EXP]),
                       ALU.is_equal)
                dve.drain()
                TT(selm, hot1, hot2, ALU.add)
                dve.drain().then_inc(S("chosen"), 1)
                dve.wait_ge(S("top_exp"), 1)
                dve.wait_ge(S("ranks"), 1)
                sc, cc_ = (v.rearrange("p (t i) -> p t i", i=ITEMS) for v in (slotc[:, 0:NT * ITEMS], combc[:, 0:NT * ITEMS]))
                TS(rank1, scr[:, 1, 0:NT * N_EXP].rearrange("p (t e) -> p t e", e=N_EXP), 1.0, None, ALU.add)
                dve.tensor_copy(cnt, scr[:, 1, 16:24])
                TS(g2, gap_e, 1.0, None, ALU.add)
                dve.drain()
                TT(rank1, rank1, selm, ALU.mult)
                TS(over, cnt, float(P), None, ALU.is_gt)
                dve.reciprocal(g1, g2)
                dve.drain()
                TS(sc[:, :, 0:N_EXP], rank1, -1.0, None, ALU.add)
                TT(g2, g1, gap_e, ALU.mult)
                dve.tensor_tensor_scan(over_before, one8, over, 0.0, ALU.mult, ALU.add)
                dve.reduce_sum(eidf[:, 3:4], over, AX_X)
                dve.drain()
                for hot, g in ((hot1, g1), (hot2, g2)):
                    TT(hot, hot, g.unsqueeze(2).broadcast_to([P, NT, N_EXP]), ALU.mult)
                dve.drain()
                TT(comb, hot1, hot2, ALU.add)
                TT(cc_[:, :, 0:N_EXP], hot1, hot2, ALU.add)
                dve.drain()
                select(0)
                TS(route_i[:, 3:4], eidf[:, 3:4], float(N_EXP), None, ALU.add).then_inc(S("counted"), 1)
                TT(over_before, over_before, over, ALU.subtract)
                take_item(0)
                splits(2, 4, 0)
                dve.drain()
                for k in range(ITEMS - N_EXP):
                    TS(pick, over_before, float(k), None, ALU.is_equal)
                    dve.drain()
                    TT(pick, pick, over, ALU.mult)
                    dve.drain()
                    TT(tmp8, pick, eid8, ALU.mult)
                    dve.drain()
                    dve.reduce_sum(eidf[:, k:k + 1], tmp8, AX_X)
                    for src, dst in ((rank1, sc), (comb, cc_)):
                        TT(hot1, src, pick.unsqueeze(1).broadcast_to([P, NT, N_EXP]), ALU.mult)
                        dve.drain()
                        dve.reduce_sum(dst[:, :, N_EXP + k], hot1, AX_X)
                        dve.drain()
                    TS(sc[:, :, N_EXP + k], sc[:, :, N_EXP + k], -1.0 - P, None, ALU.add)
                    dve.drain()
                dve.tensor_copy(route_i[:, 0:3], eidf[:, 0:3])
                dve.drain().then_inc(S("routed"), 1)
                n_items = dve.value_load(route_i[0:1, 3:4], min_val=N_EXP, max_val=ITEMS)
                with dve.Fori(0, ITEMS) as i:
                    with dve.If(i < n_items):
                        item(i)
                    dve.end_ifs()
                me.cap = N_STATIC
                for t in range(NT):
                    for h in range(2):
                        dve.bn_stats(bn[:, t, h, :], y[:, t, h * NB:(h + 1) * NB])
                layer_norm(7, 10, y)
            if "ple1" in live:
                r = n_items * R_ITEM
                me.chunk += RING
                ple(1, 10, r)


        @block.tensor
        def _(pe):
            pe.sem_inc(S("w_used"), RING)
            mm = pe.matmul

            def products(bl, r, hi, lo, r4=None, used=None):
                bb, cc, n0, n, ps = bl
                ra = 0 if r4 is not None else r
                rc = r if r4 is None else r4
                pe.wait_ge(S(f"acc_free{bb % 2}"), bb // 2 + 1 + ra)
                kmax = ps[-1][0] + ps[-1][1] - 1
                for i, (k0, nk, _) in enumerate(ps):
                    slot = (cc + i) % RING
                    pe.wait_ge(S("lo_ready"), RING + cc + i + 1 + RING * rc)
                    if used:
                        used(k0)
                    for kk in range(nk):
                        k = k0 + kk
                        wh = w_hi[:, slot, kk * n:(kk + 1) * n]
                        wl = w_lo[:, slot, kk * n:(kk + 1) * n]
                        for t in range(NT):
                            o = acc[bb % 2][t][:, 0:n]
                            mm(o, hi(k, t), wh, start=(k == 0), stop=False)
                            mm(o, hi(k, t), wl, start=False, stop=False)
                            m = mm(o, lo(k, t), wh, start=False, stop=(k == kmax))
                    m.then_inc(S("w_used"), 1)

            def products_t(bl, r):
                bb, cc, n0, n, ps = bl
                pe.wait_ge(S(f"acc_free{bb % 2}"), bb // 2 + 1 + r)
                for i, (k0, nk, _) in enumerate(ps):
                    slot = (cc + i) % RING
                    pe.wait_ge(S("lo_ready"), RING + cc + i + 1 + RING * r)
                    for kk in range(nk):
                        k = k0 + kk
                        for c_ in range(n // P):
                            cols = slice(kk * n + c_ * P, kk * n + (c_ + 1) * P)
                            o = acc_t(bb % 2, c_)
                            mm(o, w_hi[:, slot, cols], xt_hi[:, k, :], start=(k == 0 and c_ % 2 == 0), stop=False,
                               skip_group_check=True)
                            mm(o, w_hi[:, slot, cols], xt_lo[:, k, :], start=False, stop=False, skip_group_check=True)
                            m = mm(o, w_lo[:, slot, cols], xt_hi[:, k, :], start=False, stop=(k == KD - 1),
                                   skip_group_check=True)
                    m.then_inc(S("w_used"), 1)

            xh = lambda k, t: xt_hi[:, k, t * P:(t + 1) * P]
            xl = lambda k, t: xt_lo[:, k, t * P:(t + 1) * P]
            hh = lambda k, t: ht_hi[:, k, t * P:(t + 1) * P]
            hl = lambda k, t: ht_lo[:, k, t * P:(t + 1) * P]

            def turn(o, i):
                return pe.transpose(o, i, ident[:])

            def operand(m, src):
                if m == 0:
                    pe.wait_ge(S("ident_ready"), 1)
                for t in range(NT):
                    pe.wait_ge(S("t_source"), NT * m + t + 1)
                    for g in range(2):
                        for k in range(4):
                            i = turn(scr[:, 2 * t + g, k * P:(k + 1) * P], src[:, t, (4 * g + k) * P:(4 * g + k + 1) * P])
                        i.then_inc(S("t_ready"), 1)
                pe.wait_ge(S("xt_ready"), 4 * (m + 1))

            def project(name, hi, lo, used=None):
                split_loop(pe, name, lambda blocks, r: [products(b_, r, hi, lo, used=used) for b_ in blocks])

            operand(0, y)
            project("w_lr", xh, xl)
            wait_phase_evacuated(pe, "w_lr")
            for t in range(NT):
                i = turn(scr[0:2 * RANK, 0, t * P:(t + 1) * P], p0[:, t, C_LR:C_LR + 2 * RANK])
            i.then_inc(S("lr_t"), 1)
            pe.wait_ge(S("lrt_ready"), 1)
            pe.wait_ge(S("lrt_ones"), 1)
            pe.wait_ge(S("gate_w_landed"), 64)
            for t in range(NT):
                i = mm(scr[:, 2 + t, :], lrt[:, t * P:(t + 1) * P], gate_w[:], start=True, stop=True)
            i.then_inc(S("gate_pre"), 1)
            project("w_in", xh, xl)
            wait_phase_evacuated(pe, "w_in")
            pe.wait_ge(S("logd_ready"), 1)
            pe.wait_ge(S("tri_ready"), 1)
            for g in range(4):
                for t in range(NT):
                    o = (g % 2) * SEQ + t * P
                    i = mm(psum[:, 2 + g // 2, o:o + P], logd[:, t, g * P:(g + 1) * P], (tri_fwd if g < 2 else tri_bwd)[:],
                           start=True, stop=True)
            i.then_inc(S("cum_t"), 1)
            for f in range(4):
                for t in range(NT):
                    i = turn(scr[:, 1 + f // 2, (f % 2) * SEQ + t * P:(f % 2) * SEQ + (t + 1) * P],
                             p0[:, t, C_Q + f * P:C_Q + (f + 1) * P])
            i.then_inc(S("qk_t"), 1)
            pe.wait_ge(S("q_in"), 1)
            pe.wait_ge(S("k_in"), 1)
            for d in range(2):
                for h in range(GLA_HEADS):
                    lane = slice(HEAD_K * (h % 2), HEAD_K * (h % 2 + 1))
                    for t in range(NT):
                        o = ((h // 2) * NT + t) * P
                        i = mm(psum[:, 2 * d + h % 2, o:o + P], e2[lane, 2 * d + h // 2, t * P:(t + 1) * P],
                               e1[lane, 2 * d + h // 2, t * P:(t + 1) * P], start=True, stop=True)
                i.then_inc(S("gla_scores"), 1)
            pe.wait_ge(S("k_out"), 1)
            for t in range(NT):
                for g in range(4):
                    i = turn(scr[:, 3 * t, g * P:(g + 1) * P], e3[:, g, t * P:(t + 1) * P])
                i.then_inc(S("kout_t"), 1)
            pe.wait_ge(S("kout_ready"), 2)
            for g in range(4):
                for c_ in ((0, 1, 2) if g < 2 else (3, 2, 1)):
                    lane = slice(GLA_CHUNK * (c_ % 2), GLA_CHUNK * (c_ % 2 + 1))
                    for hp in range(2):
                        h = 2 * (g % 2) + hp
                        i = mm(kv_place(g, c_)[HEAD_K * hp:HEAD_K * (hp + 1), :],
                               kout[lane, c_ // 2, g * P + hp * HEAD_K:g * P + (hp + 1) * HEAD_K],
                               p0[lane, c_ // 2, C_V + h * HEAD_V:C_V + (h + 1) * HEAD_V], start=True, stop=True)
            i.then_inc(S("gla_kv"), 1)
            pe.wait_ge(S("st_ready"), 2)
            pe.wait_ge(S("q_half_ready"), 1)
            pe.wait_ge(S("state_ready"), 1)
            for t in range(NT):
                for h in range(GLA_HEADS):
                    o = psum[:, 2 * t + h % 2, (h // 2) * HEAD_V:(h // 2 + 1) * HEAD_V]
                    v = p0[:, t, C_V + h * HEAD_V:C_V + (h + 1) * HEAD_V]
                    lane = slice(HEAD_K * (h % 2), HEAD_K * (h % 2 + 1))
                    parts = [(st[:, d, h % 2, (h // 2) * NT + t, :], v) for d in range(2)]
                    for c_ in (2 * t, 2 * t + 1):
                        for d in range(2):
                            if c_ != (0 if d == 0 else 3):
                                g = 2 * d + h // 2
                                parts.append((q_half[lane, c_ % 2, g, t * P:(t + 1) * P], state[lane, g, c_, :]))
                    for k, (l, r_) in enumerate(parts):
                        i = mm(o, l, r_, start=(k == 0), stop=(k == len(parts) - 1))
                i.then_inc(S("gla_o"), 1)
            operand(1, y)
            project("w_out", xh, xl)

            def up(blocks, r):
                for b_ in blocks:
                    products_t(b_, r)

            if "w_up" in live:
                pe.wait_ge(S("cw_landed"), 16)
                wait_phase_evacuated(pe, "w_out")
                for j in range(3):
                    i = pe.transpose(psum[:, 0, j * 2 * KF:(j + 1) * 2 * KF], cw_rows[:, j, :], ident[0:2 * KF, 0:2 * KF])
                i.then_inc(S("cw_turned"), 1)
                operand(2, y)
                pe.wait_ge(S("cw_ready"), 1)
                split_loop(pe, "w_up", up)
            if "w_down" in live:
                project("w_down", hh, hl, lambda k0: pe.wait_ge(S("ht_ready"), k0 // 4 + 1))

            def scores(q, queries, keys):
                for h in range(8):
                    if q or h >= 4:
                        pe.wait_ge(S("at_s"), 8 * q + h - 3 if h >= 4 else 8 * q)
                    b_ = scr[:, h % 4, :]
                    for t, (c0, c1) in enumerate(((0, P), (P, SCW))):
                        i = mm(b_[:, c0:c1], queries(h)[:, t * P:(t + 1) * P], keys(h)[:, 0:c1 - c0], start=True, stop=(q > 0))
                        if q == 0:
                            i = mm(b_[:, c0:c1], neg_head[:, h, :], ct[:, 0:c1 - c0], start=False, stop=True)
                    i.then_inc(S("at_qk"), 1)

            def attend(q, probs, values, pt_):
                def pv(h):
                    pe.wait_ge(S("at_pt"), 8 * q + h + 1)
                    if q and h == 0:
                        pe.wait_ge(S("at_y"), q)
                    o = slice(h * DH, (h + 1) * DH)
                    mm(psum[:, 2, o], pt_[:, h % 2, 0:P], values(h, 0), start=True, stop=True)
                    mm(psum[:, 3, o], pt_[:, h % 2, P:SEQ], values(h, 0), start=True, stop=False)
                    return mm(psum[:, 3, o], pt_[:, h % 2, SEQ:SCW], values(h, 1), start=False, stop=True)

                for h in range(8):
                    pe.wait_ge(S("at_p"), 8 * q + h + 1)
                    if 8 * q + h >= 2:
                        pe.wait_ge(S("at_pt"), 8 * q + h - 1)
                    for k in range(3):
                        i = turn(psum[:, h % 2, k * P:(k + 1) * P], probs[:, h, k * P:(k + 1) * P])
                    i.then_inc(S("at_t"), 1)
                    if h:
                        pv(h - 1)
                pv(7).then_inc(S("at_o"), 1)

            if "ab_in" in live:
                def turn_qk(g, cq_, ck_):
                    for tile in range(4):
                        for f in range(2):
                            for t in range(NT):
                                c_ = (cq_ if tile < 2 else ck_) + (2 * (tile % 2) + f) * P
                                i = turn(scr[:, tile, f * SEQ + t * P:f * SEQ + (t + 1) * P], p1[:, t, c_:c_ + P])
                        i.then_inc(S("ab_t"), 1)
                    pe.wait_ge(S("qk1_ready"), 4 * (g + 1))

                operand(3, x)
                project("ab_in", xh, xl)
                wait_phase_evacuated(pe, "ab_in")
                turn_qk(0, AB_QA, AB_KA)
                pe.wait_ge(S("lf_ready"), 1)
                l0, l1 = lf[:, 2, 0, :], lf[:, 2, 1, :]
                mm(psum[:, 0, 0:N_AB], tri_incl[:], l0, start=True, stop=True)
                mm(psum[:, 0, N_AB:2 * N_AB], ones[:], l0, start=True, stop=False)
                mm(psum[:, 0, N_AB:2 * N_AB], tri_incl[:], l1, start=False, stop=True)
                mm(psum[0:N_AB, 1, 0:P], l0, tri_incl[:], start=True, stop=True)
                mm(psum[0:N_AB, 1, P:SEQ], l0, ones[:], start=True, stop=False)
                mm(psum[0:N_AB, 1, P:SEQ], l1, tri_incl[:], start=False, stop=True).then_inc(S("lf_cum"), 1)

                def qh(h):
                    return qk1[DH * (h % 2):DH * (h % 2 + 1), h // 2, :]

                def kh(h):
                    return qk1[DH * (h % 2):DH * (h % 2 + 1), 4 + h // 2, :]

                pe.wait_ge(S("fox_cum_ready"), 1)
                scores(0, qh, kh)
                pe.wait_ge(S("at_s"), 8)
                turn_qk(1, AB_QS, AB_KS)

                def breaks(g):
                    for u in range(2):
                        h = 2 * g + u
                        mm(sb_bank(g, u)[:, 0:SEQ], kh(h)[:, 0:P], qh(h), start=True, stop=True)
                        i = mm(sb_bank(g, u)[:, SEQ:SCW], kh(h)[:, P:SEQ], qh(h)[:, P:SEQ], start=True, stop=True)
                    i.then_inc(S("sb_z"), 1)

                def exponents(g):
                    pe.wait_ge(S("sb_sp"), g + 1)
                    for u in range(2):
                        o = sb_bank(g, u)
                        s0, s1 = stick[:, g % SB_SETS, u, 0:SEQ], stick[:, g % SB_SETS, u, SEQ:SCW]
                        h = 2 * g + u
                        mm(o[:, 0:SEQ], kh(h)[:, 0:P], qh(h), start=True, stop=False)
                        mm(o[:, P:SEQ], neg_ones[:], s1, start=False, stop=False, skip_group_check=True)
                        mm(o[:, 0:SEQ], neg_from[:], s0, start=False, stop=True)
                        mm(o[:, SEQ:SCW], kh(h)[:, P:SEQ], qh(h)[:, P:SEQ], start=True, stop=False)
                        i = mm(o[:, SEQ:SCW], neg_from[:], s1, start=False, stop=True)
                    i.then_inc(S("sb_exponent"), 1)

                def weigh(g):
                    pe.wait_ge(S("sb_a"), g + 1)
                    for u in range(2):
                        h = 2 * g + u
                        o = slice(h * DH, (h + 1) * DH)
                        v = lambda t: p1[:, t, AB_VS + h * DH:AB_VS + (h + 1) * DH]
                        a_ = stick[:, g % SB_SETS, u, :]
                        mm(psum[:, 2, o], a_[:, 0:P], v(0), start=True, stop=True)
                        mm(psum[:, 3, o], a_[:, P:SEQ], v(0), start=True, stop=False)
                        i = mm(psum[:, 3, o], a_[:, SEQ:SCW], v(1), start=False, stop=True)
                    i.then_inc(S("sb_o"), 1)

                breaks(0)
                breaks(1)
                attend(0, s_all, lambda h, t: p1[:, t, AB_VA + h * DH:AB_VA + (h + 1) * DH], pt)
                breaks(2)
                exponents(0)
                exponents(1)
                pe.wait_ge(S("sb_masked"), 1)
                breaks(3)
                exponents(2)
                pe.wait_ge(S("at_y"), 1)
                weigh(0)
                weigh(1)
                exponents(3)
                weigh(2)
                weigh(3)
            if "ab_out" in live:
                operand(4, y)
                project("ab_out", xh, xl)

            def turn_p(i):
                pe.wait_ge(S("p_landed"), 16 * (i + 1))
                for k in range(2):
                    for t in range(NT):
                        j = turn(scr[:, 3, k * SEQ + t * P:k * SEQ + (t + 1) * P], pn[:, t, k * P:(k + 1) * P])
                j.then_inc(S("p_t"), 1)

            if "ffn_up" in live:
                operand(5, x)
                turn_p(0)
                split_loop(pe, "ffn_up", up)
            if "ffn_down" in live:
                project("ffn_down", hh, hl, lambda k0: pe.wait_ge(S("ht_ready"), KP + k0 // 4 + 1))

            def ple(i, m, r=0):
                ph = lambda k, t: ppt_hi[:, k, t * P:(t + 1) * P]
                pl = lambda k, t: ppt_lo[:, k, t * P:(t + 1) * P]
                for q in range(2):
                    products(phase[f"ple{i}"][q], 0, ph, pl, r4=r)
                operand(m, x)
                for q in range(2):
                    products(phase[f"ple{i}"][2 + q], 0, xh, xl, r4=r)

            if "ple0" in live:
                ple(0, 6)
            if "qkv" in live:
                operand(7, x)
                project("qkv", xh, xl)
                pe.wait_ge(S("rotated"), 1)
                for j in range(3):
                    if j == 2:
                        pe.wait_ge(S("qk2_ready"), 1)
                    for f in range(4 if j < 2 else 2):
                        for t in range(NT):
                            src = p2[:, t, (4 * j + f) * P:(4 * j + f + 1) * P] if j < 2 else \
                                kdup[:, t, f, :, :].rearrange("p u n -> p (u n)")
                            o = (f % 2) * SEQ + t * P
                            i = turn(scr[:, (2 * j if j < 2 else 0) + f // 2, o:o + P], src)
                    i.then_inc(S("swa_t"), 1)
                pe.wait_ge(S("qk2_ready"), 3)
                lane = lambda h: slice(DH * (h % 2), DH * (h % 2 + 1))
                for g in range(2):
                    scores(1 + g, lambda h: qk2[lane(h), 4 * g + h // 2, :], lambda h: qk2[lane(h), 8 + g, :])
                for g in range(2):
                    attend(1 + g, (s_all, s_more)[g], lambda h, t: p2[:, t, SWA_V + g * DH:SWA_V + (g + 1) * DH], pt2)
            if "c_out" in live:
                operand(8, y)
                project("c_out", xh, xl)

            def gather(part, b0):
                for k in range(KD):
                    for t in range(NT):
                        m = mm(psum[:, b0 + k // 4, (k % 4) * P:(k % 4 + 1) * P], part[:, t, k * P:(k + 1) * P],
                               sel[:, t, :], start=(t == 0), stop=(t == NT - 1))
                m.then_inc(S("gathered"), 1)

            def turn_sel(n):
                pe.wait_ge(S("xg_hi_ready"), n + 1)
                for t in range(NT):
                    turn(psum[:, 6, t * P:(t + 1) * P], sel[:, t, :].bitcast(F32))
                for t in range(NT):
                    m = mm(psum[:, 6, SEQ:SEQ + 1], sel[:, t, :].bitcast(F32), cur_pe[:, t:t + 1], start=(t == 0), stop=(t == NT - 1))
                m.then_inc(S("gathered"), 1)

            def item(i):
                c0, r = N_BEFORE_MOE, i * R_ITEM
                pe.wait_ge(S("xg_ready"), i + 1)

                def chunk(k, o, hi, lo, k0, nk, first, last):
                    pe.wait_ge(S("lo_ready"), RING + c0 + k + 1 + RING * r)
                    slot = (c0 + k) % RING
                    for kk in range(nk):
                        wh, wl = (w[:, slot, kk * NB:(kk + 1) * NB] for w in (w_hi, w_lo))
                        q = k0 + kk
                        mm(o, hi[:, q, :], wh, start=(q == first), stop=False)
                        mm(o, hi[:, q, :], wl, start=False, stop=False)
                        m = mm(o, lo[:, q, :], wh, start=False, stop=(q == last))
                    m.then_inc(S("w_used"), 1)

                def turn_h(j):
                    if j == 0:
                        pe.wait_ge(S("selt_ready"), i + 1)
                    pe.wait_ge(S("mh_ready"), MOE_PAIRS * i + j + 1)
                    if j >= 2:
                        pe.wait_ge(S("mh_split"), MOE_PAIRS * i + j - 1)
                    for k in range(4):
                        m = turn(psum[:, 6 + j % 2, k * P:(k + 1) * P], mh[:, j % 2, k * P:(k + 1) * P])
                    m.then_inc(S("mh_t"), 1)

                for j in range(MOE_PAIRS):
                    if j >= 2:
                        pe.wait_ge(S("mh_ready"), MOE_PAIRS * i + j - 1)
                    elif j == 0:
                        pe.wait_ge(S("y_added"), 2 * i + 1)
                    for h in range(2):
                        for u in range(2):
                            chunk(4 * j + 2 * h + u, psum[:, 2 * (j % 2) + h, :], xg_hi, xg_lo, 4 * u, 4, 0, KD - 1)
                        if h == 0 and j:
                            turn_h(j - 1)
                k = MOE_UP_CHUNKS
                pe.wait_ge(S("y_added"), 2 * i + 2)
                for n in range(2):
                    k0 = 0
                    for nk in MOE_DOWN:
                        pe.wait_ge(S("mh_split"), MOE_PAIRS * i + k0 // 4 + 1)
                        chunk(k, psum[:, 4 + n, :], mh_hi, mh_lo, k0, nk, 0, KE - 1)
                        if k == MOE_UP_CHUNKS:
                            turn_h(MOE_PAIRS - 1)
                        k, k0 = k + 1, k0 + nk
                pe.wait_ge(S("sel_ready"), i + 2)
                gather(xn_hi, 6)
                gather(xn_lo, 2)
                pe.wait_ge(S("ys_ready"), 2 * i + 2)
                for t in range(NT):
                    for n in range(2):
                        for q, part in enumerate((ys_hi, ys_lo)):
                            m = mm(psum[:, 4 * t + n, :], selt[:, t * P:(t + 1) * P], part[:, n * NB:(n + 1) * NB],
                                   start=(q == 0), stop=(q == 1))
                    m.then_inc(S("scattered"), 1)
                turn_sel(i + 1)

            cur_pe = route[:, 232:234]
            if "moe" in live:
                operand(9, x)
                pe.wait_ge(S("rw_landed"), 16)
                for t in range(NT):
                    for k in range(KD):
                        for q, part in enumerate((xt_hi, xt_lo)):
                            m = mm(scr[:, 0, t * N_EXP:(t + 1) * N_EXP], part[:, k, t * P:(t + 1) * P].bitcast(F32), rw[:, k, :],
                                   start=(k == 0 and q == 0), stop=(k == KD - 1 and q == 1))
                m.then_inc(S("logits"), 1)
                turn_p(1)
                pe.wait_ge(S("chosen"), 1)
                sm = lambda t: route[:, 80 + 8 * t:88 + 8 * t]
                mm(scr[:, 1, 0:8], tri_excl[:], sm(0), start=True, stop=True)
                mm(scr[:, 1, 8:16], ones[:], sm(0), start=True, stop=False)
                mm(scr[:, 1, 8:16], tri_excl[:], sm(1), start=False, stop=True)
                mm(scr[:, 1, 16:24], ones[:], sm(0), start=True, stop=False)
                mm(scr[:, 1, 16:24], ones[:], sm(1), start=False, stop=True).then_inc(S("ranks"), 1)
                pe.wait_ge(S("sel_ready"), 1)
                pe.wait_ge(S("ppt_ready"), 2)
                gather(xn_hi, 6)
                gather(xn_lo, 2)
                turn_sel(0)
                pe.wait_ge(S("counted"), 1)
                n_items = pe.value_load(route_i[0:1, 3:4], min_val=N_EXP, max_val=ITEMS)
                with pe.Fori(0, ITEMS) as i:
                    with pe.If(i < n_items):
                        item(i)
                    pe.end_ifs()
            if "ple1" in live:
                pe.wait_ge(S("y_added"), 2 * n_items + 2)
                ple(1, 10, n_items * R_ITEM)


_INS = ["x", "norm_mix_pre", "norm_mix_post", "norm_ffn_pre", "norm_ffn_post", "w_in", "conv_a", "gate_up_fwd",
        "gate_bias_fwd", "gate_up_bwd", "gate_bias_bwd", "gla_head_norm", "w_out", "w_up", "conv_ffn", "w_down",
        "p_2", "ln_mix_g_2", "ln_mix_b_2", "ln_ffn_g_2", "ln_ffn_b_2", "ab_w_in_2", "ab_b_f_2", "ab_w_out_2",
        "c_w_qkv_2", "c_sinks_2", "c_w_out_2", "ffn_w_gate_up_2", "ffn_w_down_2", "router_w_2", "router_b_2",
        "moe_w_gate_up_2", "moe_w_down_2", "ple_w_gate_2", "ple_w_proj_2"]
UPTO = "end"


def kernel(**inputs):
    import numpy as np
    import concourse.bacc as bacc
    from concourse.bass_utils import run_bass_kernel_spmd as run

    nc = bacc.Bacc("TRN2", target_bir_lowering=False, num_devices=1)
    arrays, args = {}, {}
    for name in _INS:
        arr = np.ascontiguousarray(inputs[name])
        arrays[f"in_{name}"] = arr
        args[name] = nc.dram_tensor(f"in_{name}", arr.shape, mybir.dt.from_np(arr.dtype), kind="ExternalInput").ap()
    inv = np.float32(500000.0) ** (-np.arange(ROPE_HALF, dtype=np.float32) * np.float32(2.0) / np.float32(16.0))
    ang = np.arange(SEQ, dtype=np.float32)[:, None] * inv[None, :].astype(np.float32)
    arrays["in_rope"] = np.stack([np.cos(ang), np.sin(ang)]).astype(np.float32)
    args["rope"] = nc.dram_tensor("in_rope", (2, SEQ, ROPE_HALF), F32, kind="ExternalInput").ap()
    out = nc.dram_tensor("out", (1, SEQ, D), F32, kind="ExternalOutput").ap()
    build(nc, args, out, UPTO)
    r = run(nc, [arrays], core_ids=[0])
    return r.results[0]["out"]
```
